# Optimizing a Trainium2 kernel written in Bass

```python
import math
import jax, jax.numpy as jnp
from jax import lax
import numpy as np

D_MODEL = 1024
BATCH = 1
SEQ = 1024
DEPTH = 1

EPS = 1e-6
QBLK = 128
A_HEADS = 4
A_DIM = 64
A_VDIM = 2 * A_DIM
B_HEADS = 8
B_NOPE = 64
B_ROPE = 32
B_VDIM = 64
B_Q_LORA = 384
B_KV_LORA = 256
ROPE_THETA = 10000.0
C_HEADS = 8
C_KV_HEADS = 2
C_DIM = 64
WINDOW = 128
A_OUT = A_HEADS * A_VDIM
B_OUT = B_HEADS * B_VDIM
C_OUT = C_HEADS * C_DIM
N_BRANCH = 3
IN_SPLITS = (
    2 * A_HEADS * A_DIM,
    2 * A_HEADS * A_DIM,
    A_HEADS * A_VDIM,
    B_Q_LORA,
    B_KV_LORA,
    B_ROPE,
    C_HEADS * C_DIM,
    C_KV_HEADS * C_DIM,
    C_KV_HEADS * C_DIM,
    N_BRANCH * D_MODEL,
)
IN_COLS = 6048
N_EXPERTS = 16
EC_CAPACITY = 2
D_FF_EXPERT = 1024

kernel_name = "hybrid_gated_diff_mla_swa_ec_moe"

def rms_norm(x, g):
    xf = x.astype(jnp.float32)
    y = xf * lax.rsqrt(jnp.mean(xf * xf, axis=-1, keepdims=True) + EPS)
    return (y * g.astype(jnp.float32)).astype(x.dtype)

def alibi_slopes(n):
    return 2.0 ** (-8.0 * jnp.arange(1, n + 1, dtype=jnp.float32) / n)

def rope_tables(positions):
    inv = 1.0 / (ROPE_THETA ** (jnp.arange(0, B_ROPE, 2, dtype=jnp.float32) / B_ROPE))
    ang = positions.astype(jnp.float32)[..., None] * inv
    return jnp.cos(ang), jnp.sin(ang)

def apply_rope(x, cos, sin):
    x1, x2 = jnp.split(x.astype(jnp.float32), 2, axis=-1)
    out = jnp.concatenate([x1 * cos - x2 * sin, x1 * sin + x2 * cos], axis=-1)
    return out.astype(x.dtype)

def sweep_query_blocks(fn, *qs):
    b, s = qs[0].shape[:2]
    nb = s // QBLK
    split = lambda a: jnp.moveaxis(a.reshape((b, nb, QBLK) + a.shape[2:]), 1, 0)
    out = lax.map(lambda args: fn(*args), tuple(split(a) for a in qs))
    out = jnp.moveaxis(out, 0, 1)
    return out.reshape((b, s) + out.shape[3:])

def band_blocks(a):
    b, s = a.shape[:2]
    nb = s // WINDOW
    pad = [(0, 0), (WINDOW, WINDOW)] + [(0, 0)] * (a.ndim - 2)
    ap = jnp.pad(a, pad).reshape((b, nb + 2, WINDOW) + a.shape[2:])
    return jnp.concatenate([ap[:, :-2], ap[:, 1:-1], ap[:, 2:]], axis=2)

def diff_attention(qa, ka, va, positions, qk_g, lam_params, out_g, layer_idx):
    b, s = qa.shape[:2]
    qa = rms_norm(qa.reshape(b, s, 2, A_HEADS, A_DIM), qk_g[0])
    ka = rms_norm(ka.reshape(b, s, 2, A_HEADS, A_DIM), qk_g[1])
    va = va.reshape(b, s, A_HEADS, A_VDIM)
    lam_init = 0.8 - 0.6 * math.exp(-0.3 * layer_idx)
    lp = lam_params.astype(jnp.float32)
    lam = jnp.exp(jnp.sum(lp[0] * lp[1])) - jnp.exp(jnp.sum(lp[2] * lp[3])) + lam_init
    slopes = alibi_slopes(A_HEADS)
    scale = A_DIM ** -0.5

    def block(qb, pb):
        sc = jnp.einsum('bqmhd,bkmhd->bmhqk', qb, ka).astype(jnp.float32) * scale
        dist = jnp.abs(pb[:, :, None] - positions[:, None, :]).astype(jnp.float32)
        sc = sc - (slopes[None, :, None, None] * dist[:, None])[:, None]
        p = jax.nn.softmax(sc, axis=-1)
        attn = p[:, 0] - lam * p[:, 1]
        return jnp.einsum('bhqk,bkhe->bqhe', attn.astype(va.dtype), va)

    oa = sweep_query_blocks(block, qa, positions)
    oa = rms_norm(oa, out_g) * (1.0 - lam_init)
    return oa.reshape(b, s, A_OUT)

def latent_attention(cq, ckv, kr, positions, cq_g, w_uq, ckv_g, w_ukv, qk_g):
    b, s = cq.shape[:2]
    q = (rms_norm(cq, cq_g) @ w_uq).reshape(b, s, B_HEADS, B_NOPE + B_ROPE)
    kv = (rms_norm(ckv, ckv_g) @ w_ukv).reshape(b, s, B_HEADS, B_NOPE + B_VDIM)
    cos, sin = rope_tables(positions)
    q_nope, q_rope = q[..., :B_NOPE], q[..., B_NOPE:]
    q_rope = apply_rope(q_rope, cos[:, :, None], sin[:, :, None])
    k_nope, v = kv[..., :B_NOPE], kv[..., B_NOPE:]
    k_rope = apply_rope(kr, cos, sin)[:, :, None]
    q = rms_norm(jnp.concatenate([q_nope, q_rope], axis=-1), qk_g[0])
    k = jnp.concatenate([k_nope, jnp.broadcast_to(k_rope, (b, s, B_HEADS, B_ROPE))], axis=-1)
    k = rms_norm(k, qk_g[1])
    scale = (B_NOPE + B_ROPE) ** -0.5

    def block(qb):
        sc = jnp.einsum('bqhd,bkhd->bhqk', qb, k).astype(jnp.float32) * scale
        p = jax.nn.softmax(sc, axis=-1)
        return jnp.einsum('bhqk,bkhe->bqhe', p.astype(v.dtype), v)

    ob = sweep_query_blocks(block, q)
    return ob.reshape(b, s, B_OUT)

def window_gqa(qc, kc, vc, qk_g, sink):
    b, s = qc.shape[:2]
    nb = s // WINDOW
    rep = C_HEADS // C_KV_HEADS
    q = rms_norm(qc.reshape(b, s, C_KV_HEADS, rep, C_DIM), qk_g[0])
    k = rms_norm(kc.reshape(b, s, C_KV_HEADS, C_DIM), qk_g[1])
    v = vc.reshape(b, s, C_KV_HEADS, C_DIM)
    qb = q.reshape(b, nb, WINDOW, C_KV_HEADS, rep, C_DIM)
    kb = band_blocks(k)
    vb = band_blocks(v)
    r = jnp.arange(WINDOW)[None, :, None]
    c = jnp.arange(3 * WINDOW)[None, None, :]
    blk = jnp.arange(nb)[:, None, None]
    rel = c - WINDOW - r
    kidx = (blk - 1) * WINDOW + c
    mask = (jnp.abs(rel) <= WINDOW) & (kidx >= 0) & (kidx < s)
    slopes = alibi_slopes(C_HEADS).reshape(C_KV_HEADS, rep)
    bias = -slopes[:, :, None, None] * jnp.abs(rel[0]).astype(jnp.float32)
    sc = jnp.einsum('bnqgrd,bnkgd->bgrnqk', qb, kb).astype(jnp.float32) * (C_DIM ** -0.5)
    sc = jnp.where(mask[None, None, None], sc + bias[None, :, :, None], -1e30)
    sk = sink.astype(jnp.float32).reshape(C_KV_HEADS, rep)[None, :, :, None, None, None]
    m = jnp.maximum(jnp.max(sc, axis=-1, keepdims=True), sk)
    e = jnp.exp(sc - m)
    p = e / (jnp.sum(e, axis=-1, keepdims=True) + jnp.exp(sk - m))
    oc = jnp.einsum('bgrnqk,bnkgd->bnqgrd', p.astype(vb.dtype), vb)
    return oc.reshape(b, s, C_OUT)

def hybrid_mixer(h, positions, layer_idx, w_in, diff_qk_g, diff_lambda, diff_out_g,
                 mla_cq_g, w_uq, mla_ckv_g, w_ukv, mla_qk_g, swa_qk_g, swa_sink,
                 w_branch_a, w_branch_b, w_branch_c, w_o):
    b, s, d = h.shape
    offsets = []
    acc = 0
    for width in IN_SPLITS[:-1]:
        acc += width
        offsets.append(acc)
    proj = h @ w_in
    qa, ka, va, cq, ckv, kr, qc, kc, vc, gates = jnp.split(proj, offsets, axis=-1)
    oa = diff_attention(qa, ka, va, positions, diff_qk_g, diff_lambda, diff_out_g, layer_idx)
    ob = latent_attention(cq, ckv, kr, positions, mla_cq_g, w_uq, mla_ckv_g, w_ukv, mla_qk_g)
    oc = window_gqa(qc, kc, vc, swa_qk_g, swa_sink)
    g = jax.nn.sigmoid(gates.astype(jnp.float32)).reshape(b, s, N_BRANCH, d).astype(h.dtype)
    merged = g[:, :, 0] * (oa @ w_branch_a) + g[:, :, 1] * (ob @ w_branch_b) + g[:, :, 2] * (oc @ w_branch_c)
    return merged @ w_o

def expert_choice_ffn(h, w_router, w_gate, w_up, w_down):
    b, s, d = h.shape
    cap = max(1, EC_CAPACITY * s // N_EXPERTS)
    aff = jax.nn.softmax((h @ w_router).astype(jnp.float32), axis=-1)
    top_aff, top_idx = lax.top_k(jnp.swapaxes(aff, 1, 2), cap)
    xin = jax.vmap(lambda hb, ib: hb[ib])(h, top_idx)
    hid = jax.nn.silu(jnp.einsum('becd,edf->becf', xin, w_gate)) * jnp.einsum('becd,edf->becf', xin, w_up)
    y = jnp.einsum('becf,efd->becd', hid, w_down) * top_aff[..., None].astype(h.dtype)
    flat = (top_idx + (jnp.arange(b, dtype=jnp.int32) * s)[:, None, None]).reshape(-1)
    out = jax.ops.segment_sum(y.reshape(-1, d), flat, num_segments=b * s)
    return out.reshape(b, s, d)

def setup_inputs(seed: int = 0) -> dict:
    key = jax.random.key(seed)
    ks = jax.random.split(key, 24)
    f32 = jnp.float32
    nrm = lambda k, shape, fan_in: jax.random.normal(k, shape, f32) * (fan_in ** -0.5)
    gain = lambda k, shape: 1.0 + 0.1 * jax.random.normal(k, shape, f32)
    x = jax.random.normal(ks[0], (BATCH, SEQ, D_MODEL), f32)
    offs = jax.random.randint(ks[1], (BATCH, 1), 0, 1024, dtype=jnp.int32)
    positions = offs + jnp.arange(SEQ, dtype=jnp.int32)[None, :]
    return {
        "x": x,
        "positions": positions,
        "norm_mix_g": gain(ks[2], (DEPTH, D_MODEL)),
        "w_in": nrm(ks[3], (DEPTH, D_MODEL, IN_COLS), D_MODEL),
        "diff_qk_g": gain(ks[4], (DEPTH, 2, A_DIM)),
        "diff_lambda": 0.1 * jax.random.normal(ks[5], (DEPTH, 4, A_DIM), f32),
        "diff_out_g": gain(ks[6], (DEPTH, A_VDIM)),
        "mla_cq_g": gain(ks[7], (DEPTH, B_Q_LORA)),
        "w_uq": nrm(ks[8], (DEPTH, B_Q_LORA, B_HEADS * (B_NOPE + B_ROPE)), B_Q_LORA),
        "mla_ckv_g": gain(ks[9], (DEPTH, B_KV_LORA)),
        "w_ukv": nrm(ks[10], (DEPTH, B_KV_LORA, B_HEADS * (B_NOPE + B_VDIM)), B_KV_LORA),
        "mla_qk_g": gain(ks[11], (DEPTH, 2, B_NOPE + B_ROPE)),
        "swa_qk_g": gain(ks[12], (DEPTH, 2, C_DIM)),
        "swa_sink": 0.5 * jax.random.normal(ks[13], (DEPTH, C_HEADS), f32),
        "w_branch_a": nrm(ks[14], (DEPTH, A_OUT, D_MODEL), A_OUT),
        "w_branch_b": nrm(ks[15], (DEPTH, B_OUT, D_MODEL), B_OUT),
        "w_branch_c": nrm(ks[16], (DEPTH, C_OUT, D_MODEL), C_OUT),
        "w_o": nrm(ks[17], (DEPTH, D_MODEL, D_MODEL), D_MODEL),
        "norm_ffn_g": gain(ks[18], (DEPTH, D_MODEL)),
        "w_router": nrm(ks[19], (DEPTH, D_MODEL, N_EXPERTS), D_MODEL),
        "w_exp_gate": nrm(ks[20], (DEPTH, N_EXPERTS, D_MODEL, D_FF_EXPERT), D_MODEL),
        "w_exp_up": nrm(ks[21], (DEPTH, N_EXPERTS, D_MODEL, D_FF_EXPERT), D_MODEL),
        "w_exp_down": nrm(ks[22], (DEPTH, N_EXPERTS, D_FF_EXPERT, D_MODEL), D_FF_EXPERT),
    }

def reference(x, positions, norm_mix_g, w_in, diff_qk_g, diff_lambda, diff_out_g,
              mla_cq_g, w_uq, mla_ckv_g, w_ukv, mla_qk_g, swa_qk_g, swa_sink,
              w_branch_a, w_branch_b, w_branch_c, w_o, norm_ffn_g, w_router,
              w_exp_gate, w_exp_up, w_exp_down):
    for l in range(DEPTH):
        h = rms_norm(x, norm_mix_g[l])
        x = x + hybrid_mixer(h, positions, l, w_in[l], diff_qk_g[l], diff_lambda[l], diff_out_g[l],
                             mla_cq_g[l], w_uq[l], mla_ckv_g[l], w_ukv[l], mla_qk_g[l],
                             swa_qk_g[l], swa_sink[l], w_branch_a[l], w_branch_b[l],
                             w_branch_c[l], w_o[l])
        h = rms_norm(x, norm_ffn_g[l])
        x = x + expert_choice_ffn(h, w_router[l], w_exp_gate[l], w_exp_up[l], w_exp_down[l])
    return x


_drawn_inputs = setup_inputs


def setup_inputs(seed=0):
    import zlib

    import numpy as np

    out = dict(_drawn_inputs(seed))
    spreads = {}
    factors = {'mla_cq_g': 8.0,
     'mla_ckv_g': 5.121,
     'mla_qk_g': 5.766,
     'swa_qk_g': 3.592,
     'swa_sink': 64.0,
     'diff_qk_g': 2.99,
     'diff_lambda': 5.606,
     'diff_out_g': 3.381,
     'norm_ffn_g': 3.568}
    for name, (base, spread) in spreads.items():
        noise = np.random.default_rng([zlib.crc32(name.encode()), seed]).standard_normal(out[name].shape)
        drawn = base * np.exp(spread * noise) if base else spread * noise
        out[name] = __import__('jax').numpy.asarray(drawn.astype(out[name].dtype))
    for name, factor in factors.items():
        out[name] = (out[name] * factor).astype(out[name].dtype)
    return out
```

```python
from contextlib import ExitStack

import concourse.bass as bass
from concourse import mybir

F32 = mybir.dt.float32
F32R = mybir.dt.float32r
I32 = mybir.dt.int32
U32 = mybir.dt.uint32
ALU = mybir.AluOpType
ACT = mybir.ActivationFunctionType
AX = mybir.AxisListType

P = 128
SEQ = 1024
DM = 1024
KT = DM // P
T = SEQ // P
EPS = 1e-6

A_HEADS, A_DIM, A_VDIM = 4, 64, 128
B_HEADS, B_NOPE, B_ROPE, B_VDIM = 8, 64, 32, 64
B_QK = B_NOPE + B_ROPE
B_QL, B_KVL = 384, 256
C_HEADS, C_KV, C_DIM = 8, 2, 64
WIN = 128
OUT_W = 512
ROPE_THETA = 10000.0

COL_QA = 0
COL_KA = COL_QA + 2 * A_HEADS * A_DIM
COL_VA = COL_KA + 2 * A_HEADS * A_DIM
COL_CQ = COL_VA + A_HEADS * A_VDIM
COL_CKV = COL_CQ + B_QL
COL_KR = COL_CKV + B_KVL
COL_QC = COL_KR + B_ROPE
COL_KC = COL_QC + C_HEADS * C_DIM
COL_VC = COL_KC + C_KV * C_DIM
COL_GATE = COL_VC + C_KV * C_DIM
N_MIX = COL_GATE
NCH = 8
W_MIX = N_MIX // NCH
W_GATE = 3 * DM // NCH

A_SLOPES = [2.0 ** (-8.0 * (h + 1) / A_HEADS) for h in range(A_HEADS)]
C_SLOPES = [2.0 ** (-8.0 * (h + 1) / C_HEADS) for h in range(C_HEADS)]
LAM_INIT = 0.2

N_EXP, CAP, DFF = 16, 128, 1024

TWO_PI = 6.283185307179586
TWO_PI_PARTS = (6.28125, 0.00193500518798828125, 3.0199159795074593e-07)
MAGIC = 12582912.0
PI_IN = 3.1415925


CREDIT = 4


def done(n):
    return n + CREDIT


def landed(n):
    return 16 * n + 16 * CREDIT


class Chain:

    def __init__(self, eng, sem):
        self.eng, self.sem, self.base, self.k, self.total = eng, sem, 0, 0, 0

    def step(self, ins):
        ins.then_inc(self.sem, 1)
        self.k += 1
        return ins

    def wait(self):
        self.eng.wait_ge(self.sem, self.base + self.k)

    def enter(self, turn, per):
        self.total += self.k
        self.base, self.k = turn * per + self.total, 0

    def leave(self, turns, per):
        assert self.k == per, (self.k, per)
        self.total += turns * per
        self.base, self.k = self.total, 0


def clear(nc, sems):
    with nc.Block() as block:
        @block.vector
        def _(dve):
            for s in sems:
                dve.sem_clear(s)


def bcast_rows(ap, n):
    return ap.rearrange("(a n) -> a n", a=1).to_broadcast([P, n])


def tile_of(ap, t):
    return ap.rearrange("(t p) n -> t p n", p=P)[bass.ds(t, 1)].rearrange("a p n -> (a p) n")


def project(nc, ident, x, positions, g_mix, w_in, g_a, g_cq, w_uq, g_ckv, w_ukv, g_b, g_c, inv_freq, D):
    with ExitStack() as st:
        def sb(name, shape, dt=F32):
            return st.enter_context(nc.sbuf_tensor(name, shape, dt))

        hT_hi = sb("hT_hi", [P, KT, SEQ], F32R)
        hT_lo = sb("hT_lo", [P, KT, SEQ], F32R)
        w_raw = [sb(f"w_raw{h}", [P, 4, W_GATE]) for h in range(2)]
        w_hi = [sb(f"w_hi{c}", [P, KT, W_GATE], F32R) for c in range(2)]
        w_lo = [sb(f"w_lo{c}", [P, KT, W_GATE], F32R) for c in range(2)]
        p_out = sb("p_out", [P, 4, W_GATE])
        pin = [sb(f"pin{j}", [P, N_MIX]) for j in range(2)]
        stage = sb("stage", [P, 2048])
        turned = sb("turned", [P, 2048])
        n1 = sb("n1", [P, 1024])
        sqb = sb("sqb", [P, 1024])
        wu = sb("wu", [P, 3, 768])
        wkv = sb("wkv", [P, 2, 1024])
        cT = sb("cT", [P, 5, P])
        gain_a = sb("gain_a", [P, 2, 64])
        gain_b = sb("gain_b", [P, 2, 96])
        gain_c = sb("gain_c", [P, 2, 64])
        gain_l = sb("gain_l", [P, B_QL + B_KVL])
        pos_i = sb("pos_i", [P, T], I32)
        pos_f = sb("pos_f", [P, T])
        inv = sb("inv", [P, 16])
        cos = sb("cos", [P, T, 16])
        sin = sb("sin", [P, T, 16])
        rot = sb("rot", [P, 5, 128])
        ss = sb("ss", [P, 8])
        var = sb("var", [P, 8])
        rs = sb("rs", [P, 8])
        bss = sb("bss", [P, 2])
        bvar = sb("bvar", [P, 2])
        brs = sb("brs", [P, 2])
        inv_f2 = sb("inv_f2", [P, 2, 8])
        neg_half = sb("neg_half", [P, 8])

        PG = [st.enter_context(nc.psum_tensor(f"PG{i}", [P, 512], F32)) for i in range(4)]
        PT = [st.enter_context(nc.psum_tensor(f"PT{i}", [P, 1024], F32)) for i in range(2)]

        S = {n: st.enter_context(nc.semaphore("p_" + n)) for n in
             ("const_in consts g_in x_in0 x_in1 ssq var rstd h ht_ps ht_hi ht_lo w_in0 w_in1 w_lo w_used "
              "pg p_out sent0 sent1 sent2 sent3 dve_own act_own pin_in0 pin_in1 sq uvar urs unrm uhi ulo utr uev0 uev1 ust "
              "bsq bvar brs bc bt bct bq_ps bkv_ps bq bkv vst rope angles tables").split()}
        sent = [S[f"sent{i}"] for i in range(4)]

        w_v = w_in.rearrange("(k p) n -> p k n", p=P)
        x_t = [pin[0][:, 0:1024], pin[0][:, 1024:2048]]
        h_t = [stage[:, 0:1024], stage[:, 1024:2048]]
        g_t = turned[:, 0:1024]

        UNITS = [("a", COL_QA, 8, 64, gain_a[:, 0], True), ("a", COL_KA, 8, 64, gain_a[:, 1], False),
                 ("c", COL_QC, 8, 64, gain_c[:, 0], True), ("c", COL_KC, 2, 64, gain_c[:, 1], False),
                 ("b", 0, 8, 96, gain_b[:, 0], True), ("b", 768, 8, 96, gain_b[:, 1], False)]
        NU = len(UNITS)

        def heads_of(u, j):
            _, col, G, W, _, _ = UNITS[u]
            return pin[j][:, col:col + G * W].rearrange("p (h w) -> p h w", h=G)

        def stage_of(u):
            name, _, G, W, _, q = UNITS[u]
            if name == "b" or not q:
                return stage[:, 0:G * 2 * W].rearrange("p (h s w) -> p h s w", h=G, s=2)
            return stage[:, 0:G * 4 * W].rearrange("p (h s d w) -> p h s d w", h=G, s=2, d=2)

        def part_of(u, s):
            name, _, G, W, _, q = UNITS[u]
            v = stage_of(u)
            if name == "b" or not q:
                return v[:, :, s, :], lambda ap: ap
            return v[:, :, s, :, :], lambda ap: ap.rearrange("p (h a) w -> p h a w", a=1).to_broadcast([P, G, 2, W])

        def n_blocks(u):
            name, _, G, W, _, q = UNITS[u]
            return 16 if name == "b" or q else G

        def block_w(u):
            return 96 if UNITS[u][0] == "b" else P

        with nc.Block() as block:
            @block.sync
            def _(sp):
                for n in ("w_in0", "w_in1", "x_in0", "x_in1", "pin_in0", "pin_in1", "sent0", "sent1", "sent2", "sent3", "ust", "vst"):
                    sp.sem_inc(S[n], 16 * CREDIT)
                with sp.Fori(0, T // 2) as i:
                    for j in range(2):
                        sp.wait_ge(S["h"], done(2 * i + j - 1))
                        sp.dma_start(x_t[j], tile_of(x, 2 * i + j)).then_inc(S[f"x_in{j}"], 16)

                def load_w(c, col):
                    for h in range(2):
                        sp.wait_ge(S["w_lo"], done(2 * c + h - 1))
                        sp.dma_start(w_raw[h][:], w_v[:, 4 * h:4 * h + 4, bass.ds(col, W_GATE)]).then_inc(S[f"w_in{h}"], 16)

                def send(c, m, dst):
                    sp.wait_ge(S["p_out"], done(T * c + m + 1))
                    sp.dma_start(dst, p_out[:, m % 4, 0:dst.shape[-1]]).then_inc(sent[m % 4], 16)

                def load_pin(j, t, ring=True):
                    if ring:
                        sp.wait_ge(S["unrm"], done(NU * (t - 1)))
                        sp.wait_ge(S["vst"], landed(t - 1))
                    sp.dma_start(pin[j][:], tile_of(D["mix"], t)).then_inc(S[f"pin_in{j}"], 16)

                load_w(0, 0)
                with sp.Fori(0, NCH) as c:
                    for m in range(T):
                        if m == 2:
                            load_w(c + 1, (c + 1) * W_MIX)
                        send(c, m, D["mix"][m * P:(m + 1) * P, bass.ds(c * W_MIX, W_MIX)])
                for s in sent:
                    sp.wait_ge(s, landed(2 * NCH))
                load_pin(0, 0, False)
                load_pin(1, 1, False)

                def store(t, u):
                    name, _, G, W, _, q = UNITS[u]
                    sp.wait_ge(S["uev0"], done(NU * t + u + 1))
                    sp.wait_ge(S["uev1"], done(NU * t + u + 1))
                    rows, nb = block_w(u), n_blocks(u)
                    tv = turned[0:rows, 0:nb * P]
                    if q:
                        dst = D["q" + name][bass.ds(t, 1)].rearrange("a p n -> (a p) n")
                    else:
                        dst = D["k" + name][:, :, bass.ds(t * P, P)]
                        tv = tv.rearrange("p (b w) -> p b w", b=nb)
                    sp.dma_start(dst, tv).then_inc(S["ust"], 16)

                def gates(t, j, more, rows):
                    for m in range(T):
                        if m == 2 and more:
                            load_w(t + NCH + 1, t * W_GATE + (N_MIX + W_GATE))
                        if m == 4:
                            sp.wait_ge(S["bkv"], done(2 * t + 2))
                            sp.dma_start(tile_of(D["vb"], t), pin[j][:, 1536:2048]).then_inc(S["vst"], 16)
                        if m >= 2:
                            store(t, m - 2)
                        send(t + NCH, m, D["sig"][m * P:(m + 1) * P, bass.ds(t * W_GATE, W_GATE)])
                    if rows:
                        load_pin(j, t + 2)
                with sp.Fori(0, NCH // 2 - 1) as i:
                    for j in range(2):
                        gates(2 * i + j, j, True, True)
                for j in range(2):
                    gates(NCH - 2 + j, j, j == 0, False)
                for s in sent:
                    sp.wait_ge(s, landed(4 * NCH))
                sp.wait_ge(S["ust"], landed(NU * T))
                sp.wait_ge(S["vst"], landed(T))

            @block.gpsimd
            def _(pool):
                for n in ("rstd", "urs", "brs"):
                    pool.sem_inc(S[n], CREDIT)
                pool.dma_start(g_t, bcast_rows(g_mix, DM)).then_inc(S["g_in"], 16)
                nc.gpsimd.memset(neg_half[:], -0.5).then_inc(S["consts"], 1)
                nc.gpsimd.memset(ident[:], 0.0).then_inc(S["consts"], 1)
                for h in range(A_HEADS):
                    f = A_DIM ** -0.5 / A_SLOPES[h]
                    for m in range(2):
                        i = m * A_HEADS + h
                        nc.gpsimd.memset(inv_f2[:, 0, i:i + 1], 1.0 / f ** 2).then_inc(S["consts"], 1)
                for h in range(C_HEADS):
                    f = C_DIM ** -0.5 / C_SLOPES[h]
                    nc.gpsimd.memset(inv_f2[:, 1, h:h + 1], 1.0 / f ** 2).then_inc(S["consts"], 1)
                pool.wait_ge(S["consts"], 2 + 2 * A_HEADS + C_HEADS)
                nc.gpsimd.affine_select(out=ident[:], in_=ident[:], compare_op=ALU.not_equal, fill=1.0, base=0,
                                        pattern=[[-1, P]], channel_multiplier=1).then_inc(S["consts"], 1)
                for ap, dst, n in ((g_a[0], gain_a[:, 0], 64), (g_a[1], gain_a[:, 1], 64), (g_c[0], gain_c[:, 0], 64),
                                   (g_c[1], gain_c[:, 1], 64), (g_b[0], gain_b[:, 0], 96), (g_b[1], gain_b[:, 1], 96),
                                   (g_cq, gain_l[:, 0:B_QL], B_QL), (g_ckv, gain_l[:, B_QL:], B_KVL), (inv_freq, inv[:], 16)):
                    pool.dma_start(dst, bcast_rows(ap, n)).then_inc(S["const_in"], 16)
                with nc.allow_non_contiguous_dma(reason="4 KB of positions, once"):
                    pool.dma_start(pos_i[:], positions.rearrange("(t p) -> p t", p=P)).then_inc(S["const_in"], 16)
                pool.dma_start(wu[:], w_uq.rearrange("(k p) n -> p k n", p=P)).then_inc(S["const_in"], 16)
                pool.dma_start(wkv[:], w_ukv.rearrange("(k p) n -> p k n", p=P)).then_inc(S["const_in"], 16)
                with pool.Fori(0, T) as t:
                    pool.wait_ge(S["var"], done(t + 1))
                    nc.gpsimd.tensor_tensor(rs[:, 0:1], var[:, 0:1], neg_half[:, 0:1], ALU.pow).then_inc(S["rstd"], 1)
                with pool.Fori(0, T // 2) as i:
                    for j in range(2):
                        t = 2 * i + j

                        def rstd(u):
                            G = UNITS[u][2]
                            pool.wait_ge(S["uvar"], done(NU * t + u + 1))
                            nc.gpsimd.tensor_tensor(rs[:, 0:G], var[:, 0:G], neg_half[:, 0:G], ALU.pow).then_inc(S["urs"], 1)

                        rstd(0)
                        rstd(1)
                        pool.wait_ge(S["bvar"], done(2 * t + 2))
                        nc.gpsimd.tensor_tensor(brs[:], bvar[:], neg_half[:, 0:2], ALU.pow).then_inc(S["brs"], 1)
                        for u in range(2, NU):
                            rstd(u)

            @block.scalar
            def _(act):
                for n in ("ssq", "ht_hi", "p_out", "sq", "uhi", "uev0", "bsq", "bct", "bq", "bkv"):
                    act.sem_inc(S[n], CREDIT)
                with act.Fori(0, T // 2) as i:
                    for j in range(2):
                        t = 2 * i + j
                        act.wait_ge(S[f"x_in{j}"], landed(i + 1))
                        act.wait_ge(S["var"], done(t))
                        act.wait_ge(S["ssq"], done(t))
                        nc.scalar.activation(sqb[:], x_t[j], ACT.Square, accum_out=ss[:, 0:1]).then_inc(S["ssq"], 1)
                        act.wait_ge(S["ht_ps"], done(t + 1))
                        nc.scalar.activation(hT_hi[:, :, bass.ds(t * P, P)], PT[j][:].rearrange("p (k w) -> p k w", k=KT),
                                             ACT.Copy).then_inc(S["ht_hi"], 1)
                def evac(c, m, W, fn):
                    act.wait_ge(S["pg"], done(T * c + m + 1))
                    act.wait_ge(sent[m % 4], landed(2 * c + m // 4))
                    nc.scalar.activation(p_out[:, m % 4, 0:W], PG[m % 4][:, 0:W], fn).then_inc(S["p_out"], 1)

                with act.Fori(0, NCH) as c:
                    for m in range(T):
                        evac(c, m, W_MIX, ACT.Copy)
                act.wait_ge(S["angles"], 1)
                nc.scalar.activation(sin[:].rearrange("p t f -> p (t f)"), rot[:, 0, :], ACT.Sin).then_inc(S["tables"], 1)
                nc.scalar.activation(cos[:].rearrange("p t f -> p (t f)"), rot[:, 1, :], ACT.Sin).then_inc(S["tables"], 1)
                with act.Fori(0, NCH // 2) as i:
                    for j in range(2):
                        t = 2 * i + j

                        def gate(m):
                            evac(t + NCH, m, W_GATE, ACT.Sigmoid)

                        def square(u):
                            _, _, G, W, _, _ = UNITS[u]
                            act.wait_ge(S["uvar"], done(NU * t + u))
                            if u == 0:
                                act.wait_ge(S[f"pin_in{j}"], landed(i + 1))
                            if u == 4:
                                act.wait_ge(S["rope"], done(3 * t + 2))
                            if u == 5:
                                act.wait_ge(S["rope"], done(3 * t + 3))
                                act.wait_ge(S["bkv"], done(2 * t + 2))
                            nc.scalar.activation(sqb[:, 0:G * W].rearrange("p (h w) -> p h w", h=G), heads_of(u, j),
                                                 ACT.Square).then_inc(S["sq"], 1)

                        def hi(u):
                            _, _, G, W, _, _ = UNITS[u]
                            act.wait_ge(S["unrm"], done(NU * t + u + 1))
                            act.wait_ge(S["utr"], done(NU * t + u))
                            dst, like = part_of(u, 0)
                            nc.scalar.activation(dst.bitcast(F32R), like(n1[:, 0:G * W].rearrange("p (h w) -> p h w", h=G)),
                                                 ACT.Copy).then_inc(S["uhi"], 1)

                        def ev(u):
                            rows, half = block_w(u), n_blocks(u) // 2 * P
                            act.wait_ge(S["utr"], done(NU * t + u + 1))
                            act.wait_ge(S["ust"], landed(NU * t + u))
                            nc.scalar.activation(turned[0:rows, 0:half], PT[0][0:rows, 0:half], ACT.Copy).then_inc(S["uev0"], 1)

                        def latent_squares():
                            act.wait_ge(S["bvar"], done(2 * t))
                            act.wait_ge(S["bsq"], done(2 * t))
                            r = rot[:, :, :].rearrange("p a b -> p (a b)")
                            act.wait_ge(S["rope"], done(3 * t))
                            nc.scalar.activation(r[:, 0:384], pin[j][:, COL_CQ:COL_CQ + B_QL], ACT.Square,
                                                 accum_out=bss[:, 0:1]).then_inc(S["bsq"], 1)
                            nc.scalar.activation(r[:, 384:640], pin[j][:, COL_CKV:COL_CKV + B_KVL], ACT.Square,
                                                 accum_out=bss[:, 1:2]).then_inc(S["bsq"], 1)

                        square(0)
                        gate(0)
                        square(1)
                        hi(0)
                        latent_squares()
                        hi(1)
                        ev(0)
                        gate(1)
                        square(2)
                        ev(1)
                        act.wait_ge(S["bt"], done(t + 1))
                        act.wait_ge(S["bkv_ps"], done(t))
                        nc.scalar.activation(cT[:].rearrange("p k w -> p (k w)"), PT[0][:, 0:640], ACT.Copy).then_inc(S["bct"], 1)
                        gate(2)
                        square(3)
                        hi(2)
                        act.wait_ge(S["bq_ps"], done(t + 1))
                        act.wait_ge(S["unrm"], done(NU * t + 2))
                        nc.scalar.activation(pin[j][:, 0:768].rearrange("p (a n) -> p a n", a=2),
                                             PT[1][:].rearrange("p (a n) -> p a n", a=2)[:, :, 0:384], ACT.Copy).then_inc(S["bq"], 1)
                        gate(3)
                        kv = PT[0][:].rearrange("p (h w) -> p h w", h=B_HEADS)
                        act.wait_ge(S["bkv_ps"], done(t + 1))
                        nc.scalar.activation(heads_of(5, j)[:, :, 0:64], kv[:, :, 0:64], ACT.Copy).then_inc(S["bkv"], 1)
                        nc.scalar.activation(pin[j][:, 1536:2048].rearrange("p (h w) -> p h w", h=B_HEADS), kv[:, :, 64:128],
                                             ACT.Copy).then_inc(S["bkv"], 1)
                        hi(3)
                        ev(2)
                        gate(4)
                        square(4)
                        ev(3)
                        gate(5)
                        square(5)
                        hi(4)
                        ev(4)
                        gate(6)
                        hi(5)
                        ev(5)
                        gate(7)

            @block.vector
            def _(dve):
                ch = Chain(dve, S["dve_own"])
                for n in ("var", "h", "ht_lo", "w_lo", "uvar", "unrm", "ulo", "uev1", "bvar", "bc", "rope"):
                    dve.sem_inc(S[n], CREDIT)
                dve.wait_ge(S["g_in"], 16)
                with dve.Fori(0, T // 2) as i:
                    for j in range(2):
                        t = 2 * i + j
                        dve.wait_ge(S["ssq"], done(t + 1))
                        nc.vector.tensor_scalar(var[:, 0:1], ss[:, 0:1], 1.0 / DM, EPS, ALU.mult, ALU.add).then_inc(S["var"], 1)
                        dve.wait_ge(S["rstd"], done(t + 1))
                        dve.wait_ge(S["ht_ps"], done(t - 1))
                        nc.vector.scalar_tensor_tensor(out=h_t[j], in0=x_t[j], scalar=rs[:, 0:1], in1=g_t,
                                                       op0=ALU.mult, op1=ALU.mult).then_inc(S["h"], 1)
                        dve.wait_ge(S["ht_hi"], done(t + 1))
                        cols = bass.ds(t * P, P)
                        nc.vector.tensor_tensor(hT_lo[:, :, cols], PT[j][:].rearrange("p (k w) -> p k w", k=KT),
                                                hT_hi[:, :, cols].bitcast(F32), ALU.subtract).then_inc(S["ht_lo"], 1)

                def split(c, par):
                    for h in range(2):
                        ks = slice(4 * h, 4 * h + 4)
                        dve.wait_ge(S[f"w_in{h}"], landed(c + 1))
                        dve.wait_ge(S["w_used"], done(c - 1))
                        ch.step(nc.vector.tensor_copy(w_hi[par][:, ks, :], w_raw[h][:]))
                        ch.wait()
                        nc.vector.tensor_tensor(w_lo[par][:, ks, :], w_raw[h][:], w_hi[par][:, ks, :].bitcast(F32),
                                                ALU.subtract).then_inc(S["w_lo"], 1)

                with dve.Fori(0, NCH // 2) as i:
                    ch.enter(i, 4)
                    for j in range(2):
                        split(2 * i + j, j)
                    ch.leave(NCH // 2, 4)

                dve.wait_ge(S["const_in"], 16 * 12)
                ch.step(nc.vector.tensor_copy(pos_f[:], pos_i[:]))
                ch.wait()
                ang, turns, part = (rot[:, a, :].rearrange("p (t f) -> p t f", f=16) for a in (0, 2, 3))
                ch.step(nc.vector.tensor_tensor(ang, pos_f[:].rearrange("p (t a) -> p t a", a=1).to_broadcast([P, T, 16]),
                                                inv[:].rearrange("p (a f) -> p a f", a=1).to_broadcast([P, T, 16]), ALU.mult))
                ch.wait()
                ch.step(nc.vector.tensor_scalar(turns, ang, 1.0 / TWO_PI, MAGIC, ALU.mult, ALU.add))
                ch.wait()
                ch.step(nc.vector.tensor_scalar(turns, turns, MAGIC, None, ALU.subtract))
                for c in TWO_PI_PARTS:
                    ch.wait()
                    ch.step(nc.vector.tensor_scalar(part, turns, c, None, ALU.mult))
                    ch.wait()
                    ch.step(nc.vector.tensor_tensor(ang, ang, part, ALU.subtract))
                ch.wait()
                ch.step(nc.vector.tensor_scalar(ang, ang, PI_IN, -PI_IN, ALU.min, ALU.max))
                ch.wait()
                quarter = rot[:, 1, :].rearrange("p (t f) -> p t f", f=16)
                ch.step(nc.vector.scalar_tensor_tensor(out=quarter, in0=ang, scalar=-1.0, in1=ang, op0=ALU.mult, op1=ALU.max))
                ch.wait()
                nc.vector.tensor_scalar(quarter, quarter, -1.0, TWO_PI / 4, ALU.mult, ALU.add).then_inc(S["angles"], 1)

                PREP = 26
                with dve.Fori(0, T // 2) as i:
                    ch.enter(i, 2 * PREP)
                    for j in range(2):
                        t = 2 * i + j

                        def stat(u):
                            name, _, G, W, _, q = UNITS[u]
                            dve.wait_ge(S["sq"], done(NU * t + u + 1))
                            dve.wait_ge(S["uvar"], done(NU * t + u))
                            ch.step(nc.vector.tensor_reduce(ss[:, 0:G], sqb[:, 0:G * W].rearrange("p (h w) -> p h w", h=G),
                                                            AX.X, ALU.add))
                            ch.wait()
                            f2 = B_QK if name == "b" and q else 1.0
                            op = nc.vector.tensor_scalar(var[:, 0:G], ss[:, 0:G], f2 / W, f2 * EPS, ALU.mult, ALU.add)
                            if name != "b" and q:
                                ch.step(op)
                                ch.wait()
                                op = nc.vector.tensor_tensor(var[:, 0:G], var[:, 0:G], inv_f2[:, 0 if name == "a" else 1, :], ALU.mult)
                            op.then_inc(S["uvar"], 1)

                        def scale(u):
                            _, _, G, W, gain, _ = UNITS[u]
                            v = n1[:, 0:G * W].rearrange("p (h w) -> p h w", h=G)
                            dve.wait_ge(S["urs"], done(NU * t + u + 1))
                            dve.wait_ge(S["ulo"], done(NU * t + u))
                            ch.step(nc.vector.tensor_tensor(v, heads_of(u, j), rs[:, 0:G].rearrange("p (h a) -> p h a", a=1)
                                                            .to_broadcast([P, G, W]), ALU.mult))
                            ch.wait()
                            nc.vector.tensor_tensor(v, v, gain.rearrange("p (a w) -> p a w", a=1).to_broadcast([P, G, W]),
                                                    ALU.mult).then_inc(S["unrm"], 1)

                        def lo(u):
                            _, _, G, W, _, _ = UNITS[u]
                            dve.wait_ge(S["uhi"], done(NU * t + u + 1))
                            dve.wait_ge(S["unrm"], done(NU * t + u + 1))
                            hi_part, _ = part_of(u, 0)
                            dst, like = part_of(u, 1)
                            nc.vector.tensor_tensor(dst, like(n1[:, 0:G * W].rearrange("p (h w) -> p h w", h=G)), hi_part,
                                                    ALU.subtract).then_inc(S["ulo"], 1)

                        def ev(u):
                            rows, half = block_w(u), n_blocks(u) // 2 * P
                            dve.wait_ge(S["utr"], done(NU * t + u + 1))
                            dve.wait_ge(S["ust"], landed(NU * t + u))
                            nc.vector.tensor_copy(turned[0:rows, half:2 * half], PT[1][0:rows, 0:half]).then_inc(S["uev1"], 1)

                        def rotate(x, heads):
                            dve.wait_ge(S["rope"], done(3 * t + (2 if heads == 1 else 0)))
                            sh = [P, heads, 16]
                            c, s = (a[:, bass.ds(t, 1), :].to_broadcast(sh) for a in (cos, sin))
                            prods = [rot[:, a, 0:heads * 16].rearrange("p (h f) -> p h f", f=16) for a in range(4)]
                            for dst, half, w in zip(prods, (0, 1, 0, 1), (c, s, s, c)):
                                ch.step(nc.vector.tensor_tensor(dst, x[:, :, 16 * half:16 * half + 16], w, ALU.mult))
                            ch.wait()
                            return prods

                        split(t + NCH, j)
                        if j == 0:
                            dve.wait_ge(S["tables"], 2)
                        stat(0)
                        scale(0)
                        stat(1)
                        lo(0)
                        scale(1)
                        for a, n in enumerate((B_QL, B_KVL)):
                            dve.wait_ge(S["bsq"], done(2 * t + a + 1))
                            nc.vector.tensor_scalar(bvar[:, a:a + 1], bss[:, a:a + 1], 1.0 / n, EPS, ALU.mult, ALU.add)\
                              .then_inc(S["bvar"], 1)
                        ev(0)
                        lo(1)
                        dve.wait_ge(S["brs"], done(t + 1))
                        for a, (col, n) in enumerate(((COL_CQ, B_QL), (COL_CKV, B_KVL))):
                            v = pin[j][:, col:col + n]
                            nc.vector.scalar_tensor_tensor(out=v, in0=v, scalar=brs[:, a:a + 1], in1=gain_l[:, a * B_QL:a * B_QL + n],
                                                           op0=ALU.mult, op1=ALU.mult).then_inc(S["bc"], 1)
                        stat(2)
                        ev(1)
                        scale(2)
                        stat(3)
                        lo(2)
                        dve.wait_ge(S["bq"], done(t + 1))
                        xq = heads_of(4, j)[:, :, 64:96]
                        a, b, c, d = rotate(xq, 8)
                        nc.vector.tensor_tensor(xq[:, :, 0:16], a, b, ALU.subtract).then_inc(S["rope"], 1)
                        nc.vector.tensor_tensor(xq[:, :, 16:32], c, d, ALU.add).then_inc(S["rope"], 1)
                        scale(3)
                        ev(2)
                        lo(3)
                        kr = pin[j][:, COL_KR:COL_KR + 32].rearrange("p (a f) -> p a f", a=1)
                        a, b, c, d = rotate(kr, 1)
                        k32 = rot[:, 4, 0:32]
                        ch.step(nc.vector.tensor_tensor(k32[:, 0:16], a[:, 0, :], b[:, 0, :], ALU.subtract))
                        ch.step(nc.vector.tensor_tensor(k32[:, 16:32], c[:, 0, :], d[:, 0, :], ALU.add))
                        ch.wait()
                        nc.vector.tensor_copy(heads_of(5, j)[:, :, 64:96], k32.rearrange("p (a f) -> p a f", a=1)
                                              .to_broadcast([P, 8, 32])).then_inc(S["rope"], 1)
                        stat(4)
                        ev(3)
                        scale(4)
                        stat(5)
                        lo(4)
                        scale(5)
                        ev(4)
                        lo(5)
                        ev(5)
                    ch.leave(T // 2, 2 * PREP)

            @block.tensor
            def _(pe):
                for n in ("ht_ps", "w_used", "pg", "utr", "bt", "bq_ps", "bkv_ps"):
                    pe.sem_inc(S[n], CREDIT)
                pe.wait_ge(S["consts"], 3 + 2 * A_HEADS + C_HEADS)
                with pe.Fori(0, T // 2) as i:
                    for j in range(2):
                        t = 2 * i + j
                        pe.wait_ge(S["h"], done(t + 1))
                        pe.wait_ge(S["ht_lo"], done(t - 1))
                        for k in range(KT):
                            mm = nc.tensor.transpose(PT[j][:, k * P:(k + 1) * P], h_t[j][:, k * P:(k + 1) * P], ident[:])
                        mm.then_inc(S["ht_ps"], 1)

                def row_tile(c, par, m, W):
                    pe.wait_ge(S["p_out"], done(T * c + m - 3))
                    ms = slice(m * P, (m + 1) * P)
                    out = PG[m % 4][:, 0:W]
                    for k in range(KT):
                        nc.tensor.matmul(out, hT_hi[:, k, ms], w_hi[par][:, k, 0:W], start=(k == 0), stop=False)
                        nc.tensor.matmul(out, hT_hi[:, k, ms], w_lo[par][:, k, 0:W], start=False, stop=False)
                        mm = nc.tensor.matmul(out, hT_lo[:, k, ms], w_hi[par][:, k, 0:W], start=False, stop=(k == KT - 1))
                    mm.then_inc(S["pg"], 1)

                def chunk_done():
                    pe.drain().then_inc(S["w_used"], 1)

                pe.wait_ge(S["ht_lo"], done(T))
                with pe.Fori(0, NCH // 2) as i:
                    for j in range(2):
                        c = 2 * i + j
                        pe.wait_ge(S["w_lo"], done(2 * c + 2))
                        for m in range(T):
                            row_tile(c, j, m, W_MIX)
                        chunk_done()
                with pe.Fori(0, T // 2) as i:
                    for j in range(2):
                        t = 2 * i + j

                        def gate(m):
                            row_tile(t + NCH, j, m, W_GATE)

                        def turn(u):
                            rows, nb = block_w(u), n_blocks(u)
                            pe.wait_ge(S["ulo"], done(NU * t + u + 1))
                            pe.wait_ge(S["uhi"], done(NU * t + u + 1))
                            pe.wait_ge(S["uev0"], done(NU * t + u))
                            pe.wait_ge(S["uev1"], done(NU * t + u))
                            if u == 2:
                                pe.wait_ge(S["bq"], done(t + 1))
                                pe.wait_ge(S["bkv"], done(2 * t + 2))
                            for b in range(nb):
                                dst = PT[b // (nb // 2)][0:rows, b % (nb // 2) * P:(b % (nb // 2) + 1) * P]
                                mm = nc.tensor.transpose(dst, stage[:, b * rows:(b + 1) * rows], ident[:])
                            mm.then_inc(S["utr"], 1)

                        pe.wait_ge(S["w_lo"], done(2 * (t + NCH) + 2))
                        gate(0)
                        turn(0)
                        gate(1)
                        turn(1)
                        pe.wait_ge(S["bc"], done(2 * t + 2))
                        pe.wait_ge(S["uev0"], done(NU * t + 2))
                        for k in range(5):
                            mm = nc.tensor.transpose(PT[0][:, k * P:(k + 1) * P], pin[j][:, COL_CQ + k * P:COL_CQ + (k + 1) * P], ident[:])
                        mm.then_inc(S["bt"], 1)
                        gate(2)
                        pe.wait_ge(S["bct"], done(t + 1))
                        pe.wait_ge(S["uev1"], done(NU * t + 2))
                        for a in range(2):
                            for k in range(3):
                                mm = nc.tensor.matmul(PT[1][:, a * 512:a * 512 + 384], cT[:, k, :], wu[:, k, a * 384:(a + 1) * 384],
                                                      start=(k == 0), stop=(k == 2))
                        mm.then_inc(S["bq_ps"], 1)
                        for a in range(2):
                            for k in range(2):
                                mm = nc.tensor.matmul(PT[0][:, a * 512:(a + 1) * 512], cT[:, 3 + k, :], wkv[:, k, a * 512:(a + 1) * 512],
                                                      start=(k == 0), stop=(k == 1))
                        mm.then_inc(S["bkv_ps"], 1)
                        gate(3)
                        turn(2)
                        gate(4)
                        turn(3)
                        gate(5)
                        turn(4)
                        gate(6)
                        turn(5)
                        gate(7)
                        chunk_done()
        clear(nc, S.values())


NEG_BIG = -3.0e38


class Own:

    def __init__(self, eng, sem, base, per):
        self.eng, self.sem, self.base, self.per = eng, sem, base, per

    def at(self, n):
        self.now, self.k = n * self.per + self.base, 0

    def step(self, ins):
        ins.then_inc(self.sem, 1)
        self.k += 1

    def wait(self):
        assert self.k <= self.per
        self.eng.wait_ge(self.sem, self.now + self.k)

    def end(self, units):
        return self.base + units * self.per


def sweep(eng, parts, units, tiles, peel_last=False):
    def turn(t, before, now=True):
        for u in range(units):
            for lag, fn in parts:
                if u >= lag and now:
                    fn(t, u - lag)
                elif u < lag and before is not None:
                    fn(before, u - lag + units)
    turn(0, None)
    with eng.Fori(1, tiles - 1 if peel_last else tiles) as t:
        turn(t, t - 1)
    if peel_last:
        turn(tiles - 1, tiles - 2)
    turn(None, tiles - 1, now=False)


def attention(nc, ident, positions, lam_params, g_out, sink, D):
    with ExitStack() as st:
        def sb(name, shape, dt=F32):
            return st.enter_context(nc.sbuf_tensor(name, shape, dt))

        ka = sb("ka", [P, 2 * A_HEADS, SEQ], F32R)
        va = sb("va", [P, T, OUT_W])
        kb = sb("kb", [B_QK, 2 * B_HEADS, SEQ], F32R)
        vb = sb("vb", [P, T, OUT_W])
        kc = sb("kc", [P, C_KV, SEQ + 2 * WIN], F32R)
        vc = sb("vc", [P, T + 2, C_KV * C_DIM])
        q = sb("q", [P, 16 * P], F32R)
        scores = [sb(f"scores{i}", [P, SEQ]) for i in range(2)]
        e = [sb(f"e{i}", [P, SEQ]) for i in range(4)]
        pT = [sb(f"pT{i}", [P, SEQ]) for i in range(2)]
        dist = sb("dist", [P, SEQ])
        out = sb("out", [P, OUT_W])
        o4 = sb("o4", [P, OUT_W])
        pk_i = e[3][:].bitcast(I32)
        pos_i = sb("apos_i", [P, T], I32)
        neg_pos = sb("neg_pos", [P, T])
        lp = sb("lp", [P, 4, 64])
        lam2 = sb("lam2", [P, 2])
        lam = sb("lam", [P, 1])
        go = sb("go", [P, A_VDIM])
        small = sb("small", [P, 64])
        window = [sb(f"window{i}", [P, 3 * WIN]) for i in range(3)]
        sk = sb("sk", [P, C_HEADS])
        sk_s = sb("sk_s", [P, C_HEADS])
        slope = sb("slope", [P, C_HEADS])
        neg_half = sb("aneg_half", [P, 4])
        pos_k = sb("pos_k", [P, SEQ])

        PS = [st.enter_context(nc.psum_tensor(f"PS{i}", [P, 1024], F32)) for i in range(2)]
        PT = st.enter_context(nc.psum_tensor("PTr", [P, 1024], F32))
        PO = [st.enter_context(nc.psum_tensor(f"PO{i}", [P, 512], F32)) for i in range(2)]

        def sems(prefix, names):
            return {n: st.enter_context(nc.semaphore(prefix + n)) for n in names.split()}
        L = sems("a_", "k_a v_a k_b v_b k_c v_c pads small_in consts lam ready gate dve act")
        A = sems("aa_", "q_in0 q_in1 q_in2 q_in3 s dist sub0 bias exp0 exp1 comb tr pt pv sq o var rs out sent")
        B = sems("ab_", "q_in0 q_in1 q_in2 q_in3 s bias exp tr pt pv o sent0 sent1")
        C = sems("ac_", "q_in0 q_in1 q_in2 q_in3 s sub bias exp den tr pt pv o sent0 sent1 esk")
        U_A, U_B, U_C = A_HEADS, B_HEADS, C_HEADS

        qa = q[:, :].rearrange("p (h m s w) -> p h m s w", h=4, m=2, s=2)
        qb = q[:, :].rearrange("p (h s w) -> p h s w", h=8, s=2)
        mx, nb, sm, rc, cc = (small[:, 8 * i:8 * i + 8] for i in range(5))
        ssq, var, rs = (small[:, 40 + 4 * i:44 + 4 * i] for i in range(3))

        c_scores = [[scores[0], scores[1], dist, pos_k][i // 2][:, 512 * (i % 2):512 * (i % 2) + 3 * WIN] for i in range(8)]

        with nc.Block() as block:
            @block.sync
            def _(sp):
                for Q in (A, B, C):
                    for i in range(4):
                        sp.sem_inc(Q[f"q_in{i}"], 16 * CREDIT)
                sp.sem_inc(A["sent"], 16 * CREDIT)
                for Q in (B, C):
                    for i in range(2):
                        sp.sem_inc(Q[f"sent{i}"], 16 * CREDIT)

                def load(sem, dst, src):
                    sp.dma_start(dst, src).then_inc(sem, 16)

                mix = D["mix"].rearrange("(t p) n -> p t n", p=P)

                def q_a(t, h):
                    sp.wait_ge(A["s"], done(U_A * (t - 1) + h + 1))
                    load(A[f"q_in{h}"], qa[:, h].bitcast(F32),
                         D["qa"][bass.ds(t, 1)].rearrange("a p (m h s w) -> (a p) h m s w", m=2, h=4, s=2)[:, h])

                def q_bc(X, src, rows, t, i, after=None):
                    if after is None:
                        sp.wait_ge(X["s"], done(U_B * (t - 1) + 2 * i + 2))
                    else:
                        sp.wait_ge(*after)
                    load(X[f"q_in{i}"], qb[0:rows, 2 * i:2 * i + 2].bitcast(F32),
                         src[bass.ds(t, 1)].rearrange("a p (h s w) -> (a p) h s w", h=8, s=2)[:, 2 * i:2 * i + 2])

                for h in range(U_A):
                    q_a(0, h)
                load(L["k_a"], ka[:].bitcast(F32), D["ka"])
                load(L["v_a"], va[:], mix[:, :, COL_VA:COL_VA + OUT_W])
                def send_a(t):
                    sp.wait_ge(A["out"], done(4 * t + 4))
                    sp.dma_start(tile_of(D["o"][:, 0:OUT_W], t), out[:]).then_inc(A["sent"], 16)
                for h in range(U_A):
                    q_a(1, h)
                    if h == 1:
                        load(L["k_b"], kb[:].bitcast(F32), D["kb"])
                        load(L["v_b"], vb[:], D["vb"].rearrange("(t p) n -> p t n", p=P))
                        load(L["k_c"], kc[:, :, WIN:WIN + SEQ].bitcast(F32), D["kc"])
                        load(L["v_c"], vc[:, 1:T + 1, :], mix[:, :, COL_VC:COL_VC + C_KV * C_DIM])
                with sp.Fori(2, T) as t:
                    q_a(t, 0)
                    q_a(t, 1)
                    q_a(t, 2)
                    send_a(t - 2)
                    q_a(t, 3)
                for i in range(4):
                    q_bc(B, D["qb"], B_QK, 0, i, (A["s"], done(U_A * (T - 1) + i + 1)))
                send_a(T - 2)
                send_a(T - 1)

                def send(X, col, t, half):
                    sp.wait_ge(X["o"], done(2 * t + half + 1) if X is C else done(U_B * t + 4 * half + 4))
                    sp.dma_start(tile_of(D["o"][:, col + 256 * half:col + 256 * half + 256], t),
                                 out[:, 256 * half:256 * half + 256]).then_inc(X[f"sent{half}"], 16)

                with sp.Fori(1, T) as t:
                    for i in range(4):
                        q_bc(B, D["qb"], B_QK, t, i)
                        if i >= 2:
                            send(B, OUT_W, t - 1, i - 2)
                for i in range(4):
                    q_bc(C, D["qc"], P, 0, i, (B["s"], done(U_B * (T - 1) + 2 * i + 2)))
                send(B, OUT_W, T - 1, 0)
                send(B, OUT_W, T - 1, 1)
                with sp.Fori(1, T) as t:
                    for i in range(4):
                        q_bc(C, D["qc"], P, t, i)
                        if i >= 2:
                            send(C, 2 * OUT_W, t - 1, i - 2)
                send(C, 2 * OUT_W, T - 1, 0)
                send(C, 2 * OUT_W, T - 1, 1)
                sp.wait_ge(A["sent"], landed(T))
                for X in (B, C):
                    for i in range(2):
                        sp.wait_ge(X[f"sent{i}"], landed(T))

            @block.gpsimd
            def _(pool):
                pool.sem_inc(A["rs"], CREDIT)
                pool.dma_start(pk_i, bcast_rows(positions, SEQ)).then_inc(L["small_in"], 16)
                with nc.allow_non_contiguous_dma(reason="4 KB of positions, once"):
                    pool.dma_start(pos_i[:], positions.rearrange("(t p) -> p t", p=P)).then_inc(L["small_in"], 16)
                pool.dma_start(lp[:].rearrange("p a b -> p (a b)"), bcast_rows(lam_params.rearrange("a b -> (a b)"), 256)).then_inc(L["small_in"], 16)
                pool.dma_start(go[:], bcast_rows(g_out, A_VDIM)).then_inc(L["small_in"], 16)
                pool.dma_start(sk[:], bcast_rows(sink, C_HEADS)).then_inc(L["small_in"], 16)
                nc.gpsimd.memset(neg_half[:], -0.5).then_inc(L["consts"], 1)
                nc.gpsimd.memset(kc[:, :, 0:WIN].bitcast(F32), 0.0).then_inc(L["consts"], 1)
                nc.gpsimd.memset(kc[:, :, WIN + SEQ:].bitcast(F32), 0.0).then_inc(L["consts"], 1)
                nc.gpsimd.memset(vc[:, 0, :], 0.0).then_inc(L["consts"], 1)
                nc.gpsimd.memset(vc[:, T + 1, :], 0.0).then_inc(L["consts"], 1)
                for h in range(C_HEADS):
                    nc.gpsimd.memset(slope[:, h:h + 1], C_SLOPES[h]).then_inc(L["consts"], 1)
                n = 5 + C_HEADS
                nc.gpsimd.iota(window[0][:], [[1, 3 * WIN]], base=-WIN, channel_multiplier=-1,
                               allow_small_or_imprecise_dtypes=True).then_inc(L["consts"], 1)
                pool.wait_ge(L["dve"], 1)
                nc.gpsimd.affine_select(out=window[1][:], in_=window[1][:], compare_op=ALU.is_ge, fill=1e30, base=0,
                                        pattern=[[1, 3 * WIN]], channel_multiplier=-1).then_inc(L["consts"], 1)
                pool.wait_ge(L["consts"], n + 2)
                nc.gpsimd.affine_select(out=window[1][:], in_=window[1][:], compare_op=ALU.is_ge, fill=1e30, base=2 * WIN,
                                        pattern=[[-1, 3 * WIN]], channel_multiplier=1).then_inc(L["consts"], 1)
                pool.wait_ge(L["consts"], n + 3)
                nc.gpsimd.affine_select(out=window[0][:], in_=window[1][:], compare_op=ALU.is_ge, fill=1e30, base=-WIN,
                                        pattern=[[1, 3 * WIN]], channel_multiplier=0).then_inc(L["consts"], 1)
                nc.gpsimd.affine_select(out=window[2][:], in_=window[1][:], compare_op=ALU.is_ge, fill=1e30, base=2 * WIN - 1,
                                        pattern=[[-1, 3 * WIN]], channel_multiplier=0).then_inc(L["consts"], 1)
                with pool.Fori(0, T) as t:
                    pool.wait_ge(A["var"], done(t + 1))
                    nc.gpsimd.tensor_tensor(rs, var, neg_half[:], ALU.pow).then_inc(A["rs"], 1)

            @block.tensor
            def _(pe):
                for X in (A, B, C):
                    for n in ("s", "tr", "pv"):
                        pe.sem_inc(X[n], CREDIT)
                pe.wait_ge(L["k_a"], 16)
                pe.wait_ge(L["v_a"], 16)

                def s_a(t, h):
                    n = U_A * t + h
                    pe.wait_ge(A[f"q_in{h}"], landed(t + 1))
                    for m in range(2):
                        pe.wait_ge(A["sub0"], done(2 * n - 1 + m))
                        for half in range(2):
                            cols = slice(512 * half, 512 * half + 512)
                            for s in range(2):
                                mm = nc.tensor.matmul(PS[m][:, cols], qa[:, h, m, s, :], ka[:, m * A_HEADS + h, cols],
                                                      start=(s == 0), stop=(s == 1))
                    mm.then_inc(A["s"], 1)

                def turn(src, blocks, last):
                    for b in range(blocks):
                        mm = nc.tensor.transpose(PT[:, b * P:(b + 1) * P], src[:, b * P:(b + 1) * P], ident[:])
                    mm.then_inc(last, 1)

                def t_a(t, h):
                    n = U_A * t + h
                    pe.wait_ge(A["comb"], done(n + 1))
                    pe.wait_ge(A["pt"], done(n))
                    turn(e[2 * (h % 2)], T, A["tr"])

                def pv_a(t, h):
                    n = U_A * t + h
                    pe.wait_ge(A["pt"], done(n + 1))
                    pe.wait_ge(A["o"], done(n - 1))
                    for b in range(T):
                        mm = nc.tensor.matmul(PO[h % 2][:, 0:P], pT[h % 2][:, b * P:(b + 1) * P], va[:, b, h * P:(h + 1) * P],
                                              start=(b == 0), stop=(b == T - 1))
                    mm.then_inc(A["pv"], 1)

                sweep(pe, [(0, s_a), (3, pv_a), (2, t_a)], U_A, T)

                def s_b(t, h):
                    n = U_B * t + h
                    pe.wait_ge(B[f"q_in{h // 2}"], landed(t + 1))
                    pe.wait_ge(B["exp"], done(n - 1))
                    for half in range(2):
                        cols = slice(512 * half, 512 * half + 512)
                        for i, (a, b) in enumerate(((0, 0), (0, 1), (1, 0))):
                            mm = nc.tensor.matmul(PS[h % 2][:, cols], qb[0:B_QK, h, a, :], kb[:, 2 * h + b, cols],
                                                  start=(i == 0), stop=(i == 2))
                    mm.then_inc(B["s"], 1)

                def t_b(t, h):
                    n = U_B * t + h
                    pe.wait_ge(B["exp"], done(n + 1))
                    pe.wait_ge(B["pt"], done(n))
                    turn(e[h % 4], T, B["tr"])

                def pv_b(t, h):
                    n = U_B * t + h
                    pe.wait_ge(B["pt"], done(n + 1))
                    pe.wait_ge(B["o"], done(n - 1))
                    for b in range(T):
                        mm = nc.tensor.matmul(PO[h % 2][:, 0:B_VDIM], pT[h % 2][:, b * P:(b + 1) * P],
                                              vb[:, b, h * B_VDIM:(h + 1) * B_VDIM], start=(b == 0), stop=(b == T - 1))
                    mm.then_inc(B["pv"], 1)

                pe.wait_ge(A["sub0"], done(2 * U_A * T))
                pe.wait_ge(A["pt"], done(U_A * T))
                pe.wait_ge(A["o"], done(U_A * T))
                pe.wait_ge(A["sq"], done(U_A * T))
                pe.wait_ge(L["k_b"], 16)
                pe.wait_ge(L["v_b"], 16)
                sweep(pe, [(0, s_b), (3, pv_b), (2, t_b)], U_B, T)

                def s_c(t, h):
                    n = U_C * t + h
                    bank = PS[h % 4 // 2][:, 512 * (h % 2):512 * (h % 2) + 3 * WIN]
                    pe.wait_ge(C[f"q_in{h // 2}"], landed(t + 1))
                    pe.wait_ge(C["sub"], done(n - 3))
                    for s in range(2):
                        mm = nc.tensor.matmul(bank, qb[:, h, s, :], kc[:, h // (C_HEADS // C_KV), bass.ds(t * P, 3 * WIN)],
                                              start=(s == 0), stop=(s == 1))
                    mm.then_inc(C["s"], 1)

                def t_c(t, h):
                    n = U_C * t + h
                    pe.wait_ge(C["exp"], done(n + 1))
                    pe.wait_ge(C["pt"], done(n - 1))
                    for b in range(3):
                        mm = nc.tensor.transpose(PT[:, 512 * (h % 2) + b * P:512 * (h % 2) + (b + 1) * P],
                                                 e[h % 4][:, b * P:(b + 1) * P], ident[:])
                    mm.then_inc(C["tr"], 1)

                def pv_c(t, h):
                    n = U_C * t + h
                    g = h // 4
                    kv = h // (C_HEADS // C_KV)
                    pe.wait_ge(C["pt"], done(n + 1))
                    if h % 4 == 0:
                        pe.wait_ge(C["o"], done(2 * t + g - 1))
                    for b in range(3):
                        mm = nc.tensor.matmul(PO[g][:, (h % 4) * C_DIM:(h % 4 + 1) * C_DIM], pT[h % 2][:, b * P:(b + 1) * P],
                                              vc[:, bass.ds(t + b, 1), kv * C_DIM:(kv + 1) * C_DIM].rearrange("p a w -> p (a w)"),
                                              start=(b == 0), stop=(b == 2), skip_group_check=True)
                    mm.then_inc(C["pv"], 1)

                pe.wait_ge(B["exp"], done(U_B * T))
                pe.wait_ge(B["pt"], done(U_B * T))
                pe.wait_ge(B["o"], done(U_B * T))
                pe.wait_ge(L["k_c"], 16)
                pe.wait_ge(L["v_c"], 16)
                pe.wait_ge(L["consts"], 5 + C_HEADS + 5)
                sweep(pe, [(0, s_c), (7, pv_c), (6, t_c)], U_C, T)

            @block.scalar
            def _(act):
                for X, names in ((A, ("dist", "exp0", "exp1", "pt", "sq")), (B, ("exp", "pt")), (C, ("exp", "pt", "esk"))):
                    for n in names:
                        act.sem_inc(X[n], CREDIT)
                act.wait_ge(L["lam"], 1)
                nc.scalar.activation(lam2[:], small[:, 0:2], ACT.Exp).then_inc(L["act"], 1)
                act.wait_ge(L["ready"], 1)

                def dist_a(t, h):
                    if h:
                        return
                    act.wait_ge(A["sub0"], done(2 * U_A * t))
                    nc.scalar.activation(dist[:], pos_k[:], ACT.Abs, bias=neg_pos[:, bass.ds(t, 1)]).then_inc(A["dist"], 1)

                def exp_a(t, h):
                    n = U_A * t + h
                    act.wait_ge(A["bias"], done(n + 1))
                    act.wait_ge(A["comb"], done(n - 1))
                    act.wait_ge(A["tr"], done(n - 1))
                    for m in range(2):
                        k = 2 * h + m
                        nc.scalar.activation(e[2 * (h % 2) + m][:], scores[m][:], ACT.Exp, bias=nb[:, k:k + 1],
                                             scale=A_SLOPES[h], accum_out=sm[:, k:k + 1]).then_inc(A[f"exp{m}"], 1)

                def pt(X, U, half=None):
                    def fn(t, h):
                        n = U * t + h
                        act.wait_ge(X["tr"], done(n + 1))
                        act.wait_ge(X["pv"], done(n - 1))
                        nc.scalar.activation(pT[h % 2][:], PT[:], ACT.Copy).then_inc(X["pt"], 1)
                    return fn

                def sq_a(t, h):
                    n = U_A * t + h
                    act.wait_ge(A["pv"], done(n + 1))
                    act.wait_ge(A["o"], done(n + 1))
                    act.wait_ge(A["var"], done(t))
                    act.wait_ge(A["sq"], done(n))
                    nc.scalar.activation(dist_junk, o4[:, h * P:(h + 1) * P], ACT.Square, accum_out=ssq[:, h:h + 1]).then_inc(A["sq"], 1)

                dist_junk = lp[:].rearrange("p a b -> p (a b)")[:, 0:P]
                sweep(act, [(0, dist_a), (2, pt(A, U_A)), (0, exp_a), (3, sq_a)], U_A, T)

                def exp_b(t, h):
                    n = U_B * t + h
                    act.wait_ge(B["bias"], done(n + 1))
                    act.wait_ge(B["tr"], done(n - 3))
                    act.wait_ge(B["o"], done(n - 3))
                    nc.scalar.activation(e[h % 4][:], PS[h % 2][:], ACT.Exp, bias=nb[:, h % 4:h % 4 + 1],
                                         accum_out=sm[:, h % 4:h % 4 + 1]).then_inc(B["exp"], 1)
                act.wait_ge(A["tr"], done(U_A * T))
                act.wait_ge(A["pv"], done(U_A * T))
                sweep(act, [(2, pt(B, U_B)), (0, exp_b)], U_B, T)

                def exp_c(t, h):
                    n = U_C * t + h
                    g = h // 4
                    if h % 4 == 0:
                        act.wait_ge(C["bias"], done(2 * t + g + 1))
                        act.wait_ge(C["o"], done(2 * t + g - 1))
                    act.wait_ge(C["tr"], done(n - 3))
                    nc.scalar.activation(e[h % 4][:, 0:3 * WIN], c_scores[h], ACT.Exp, bias=nb[:, h:h + 1], scale=C_SLOPES[h],
                                         accum_out=sm[:, h:h + 1]).then_inc(C["exp"], 1)
                    if h % 4 == 3:
                        nc.scalar.activation(cc[:, 4 * g:4 * g + 4], mx[:, 4 * g:4 * g + 4], ACT.Exp).then_inc(C["esk"], 1)

                def pt_c(t, h):
                    n = U_C * t + h
                    act.wait_ge(C["tr"], done(n + 1))
                    act.wait_ge(C["pv"], done(n - 1))
                    nc.scalar.activation(pT[h % 2][:, 0:3 * WIN], PT[:, 512 * (h % 2):512 * (h % 2) + 3 * WIN], ACT.Copy).then_inc(C["pt"], 1)
                act.wait_ge(B["tr"], done(U_B * T))
                act.wait_ge(B["pv"], done(U_B * T))
                sweep(act, [(6, pt_c), (4, exp_c)], U_C, T)

            @block.vector
            def _(dve):
                ch = Chain(dve, L["dve"])
                for X, names in ((A, ("sub0", "bias", "comb", "o", "var", "out")), (B, ("bias", "o")), (C, ("sub", "bias", "den", "o"))):
                    for n in names:
                        dve.sem_inc(X[n], CREDIT)
                dve.wait_ge(L["consts"], 6 + C_HEADS)
                ch.step(nc.vector.scalar_tensor_tensor(out=window[1][:], in0=window[0][:], scalar=-1.0, in1=window[0][:],
                                                       op0=ALU.mult, op1=ALU.max))
                dve.wait_ge(L["small_in"], 16 * 5)
                ch.step(nc.vector.tensor_copy(pos_k[:], pk_i))
                ch.step(nc.vector.tensor_copy(neg_pos[:], pos_i[:]))
                ch.step(nc.vector.tensor_tensor(lp[:, 0, :], lp[:, 0, :], lp[:, 1, :], ALU.mult))
                ch.step(nc.vector.tensor_tensor(lp[:, 2, :], lp[:, 2, :], lp[:, 3, :], ALU.mult))
                ch.step(nc.vector.tensor_scalar(go[:], go[:], 1.0 - LAM_INIT, None, ALU.mult))
                ch.step(nc.vector.tensor_copy(sk_s[:], sk[:]))
                ch.wait()
                ch.step(nc.vector.tensor_scalar(neg_pos[:], neg_pos[:], -1.0, None, ALU.mult))
                for h in range(C_HEADS):
                    ch.step(nc.vector.tensor_scalar(sk_s[:, h:h + 1], sk[:, h:h + 1], 1.0 / C_SLOPES[h], None, ALU.mult))
                for a in range(2):
                    op = nc.vector.tensor_reduce(small[:, a:a + 1], lp[:, 2 * a, :], AX.X, ALU.add)
                    ch.step(op)
                ch.wait()
                nc.vector.tensor_copy(lp[:, 1, 0:1], small[:, 0:1]).then_inc(L["lam"], 1)
                dve.wait_ge(L["act"], 1)
                dve.wait_ge(L["lam"], 1)
                ch.step(nc.vector.tensor_tensor(lam[:], lam2[:, 1:2], lam2[:, 0:1], ALU.subtract))
                ch.wait()
                ch.step(nc.vector.tensor_scalar(lam[:], lam[:], LAM_INIT, None, ALU.subtract))
                ch.wait()
                nc.vector.tensor_copy(lp[:, 1, 1:2], lam[:]).then_inc(L["ready"], 1)

                def sub_a(t, h):
                    n = U_A * t + h
                    k = 2 * h
                    for m in range(2):
                        if m == 0:
                            dve.wait_ge(A["s"], done(n + 1))
                            dve.wait_ge(A["dist"], done(t + 1))
                            dve.wait_ge(A["bias"], done(n))
                        dve.wait_ge(A[f"exp{m}"], done(n))
                        dve.sem_inc(L["gate"], 1)
                        nc.vector.tensor_tensor_reduce(scores[m][:], PS[m][:], dist[:], 1.0, NEG_BIG, ALU.subtract, ALU.max,
                                                       mx[:, k + m:k + m + 1]).then_inc(A["sub0"], 1)
                    dve.wait_ge(A["sub0"], done(2 * n + 2))
                    nc.vector.tensor_scalar(nb[:, k:k + 2], mx[:, k:k + 2], -A_SLOPES[h], None, ALU.mult).then_inc(A["bias"], 1)

                def comb_a(t, h):
                    n = U_A * t + h
                    k = 2 * h
                    dve.wait_ge(A["exp0"], done(n + 1))
                    dve.wait_ge(A["exp1"], done(n + 1))
                    dve.wait_ge(A["o"], done(n - 3))
                    dve.wait_ge(A["comb"], done(n))
                    ops.step(nc.vector.reciprocal(rc[:, k:k + 2], sm[:, k:k + 2]))
                    ops.wait()
                    ops.step(nc.vector.scalar_tensor_tensor(out=cc[:, k:k + 1], in0=sm[:, k:k + 1], scalar=rc[:, k + 1:k + 2], in1=lam[:],
                                                            op0=ALU.mult, op1=ALU.mult))
                    ops.wait()
                    e0, e1 = e[2 * (h % 2)], e[2 * (h % 2) + 1]
                    nc.vector.scalar_tensor_tensor(out=e0[:], in0=e1[:], scalar=cc[:, k:k + 1], in1=e0[:],
                                                   op0=ALU.mult, op1=ALU.add).then_inc(A["comb"], 1)

                def o_a(t, h):
                    n = U_A * t + h
                    k = 2 * h
                    dve.wait_ge(A["pv"], done(n + 1))
                    dve.wait_ge(A["out"], done(4 * t))
                    nc.vector.tensor_scalar(o4[:, h * P:(h + 1) * P], PO[h % 2][:, 0:P], rc[:, k:k + 1], None, ALU.mult)\
                      .then_inc(A["o"], 1)

                def norm_a(t, h):
                    if h < U_A - 1:
                        return
                    dve.wait_ge(A["sq"], done(U_A * t + U_A))
                    dve.wait_ge(A["out"], done(4 * t))
                    nc.vector.tensor_scalar(var, ssq, 1.0 / A_VDIM, EPS, ALU.mult, ALU.add).then_inc(A["var"], 1)

                def out_a(t, h):
                    if h < U_A - 1:
                        return
                    dve.wait_ge(A["rs"], done(t + 1))
                    dve.wait_ge(A["sent"], landed(t))
                    for i in range(A_HEADS):
                        v = slice(i * P, (i + 1) * P)
                        nc.vector.scalar_tensor_tensor(out=out[:, v], in0=o4[:, v], scalar=rs[:, i:i + 1], in1=go[:],
                                                       op0=ALU.mult, op1=ALU.mult).then_inc(A["out"], 1)

                own = Own(dve, L["dve"], ch.k, 2)
                ops = own

                def comb(t, h):
                    own.at(U_A * t + h)
                    comb_a(t, h)
                sweep(dve, [(0, sub_a), (1, comb), (4, out_a), (3, o_a), (3, norm_a)], U_A, T)
                base = own.end(U_A * T)

                def max_b(t, h):
                    n = U_B * t + h
                    dve.wait_ge(B["s"], done(n + 1))
                    dve.wait_ge(B["exp"], done(n - 3))
                    own.at(n)
                    own.step(nc.vector.tensor_reduce(mx[:, h % 4:h % 4 + 1], PS[h % 2][:], AX.X, ALU.max))
                    own.wait()
                    nc.vector.tensor_scalar(nb[:, h % 4:h % 4 + 1], mx[:, h % 4:h % 4 + 1], -1.0, None, ALU.mult).then_inc(B["bias"], 1)

                def o_b(t, h):
                    n = U_B * t + h
                    k = h % 4
                    dve.wait_ge(B["pv"], done(n + 1))
                    dve.wait_ge(B["o"], done(n))
                    nc.vector.reciprocal(rc[:, k:k + 1], sm[:, k:k + 1]).then_inc(L["pads"], 1)
                    dve.wait_ge(L["pads"], n + 1)
                    if h % 4 == 0:
                        dve.wait_ge(B[f"sent{h // 4}"], landed(t))
                    nc.vector.tensor_scalar(out[:, h * B_VDIM:(h + 1) * B_VDIM], PO[h % 2][:, 0:B_VDIM], rc[:, k:k + 1], None, ALU.mult)\
                      .then_inc(B["o"], 1)
                own = Own(dve, L["dve"], base, 1)
                dve.wait_ge(A["sent"], landed(T))
                dve.wait_ge(A["bias"], done(U_A * T))
                sweep(dve, [(0, max_b), (3, o_b)], U_B, T)
                base = own.end(U_B * T)

                def sub_c(t, h):
                    n = U_C * t + h
                    g = h // 4
                    win = window[0 if isinstance(t, int) and t == 0 else 2 if isinstance(t, int) else 1]
                    dve.wait_ge(C["s"], done(n + 1))
                    if not isinstance(t, int) or t:
                        dve.wait_ge(C["exp"], done(n - 7))
                    if h % 4 == 0:
                        dve.wait_ge(C["esk"], done(2 * t + g - 1))
                    dve.sem_inc(L["gate"], 1)
                    nc.vector.tensor_tensor_reduce(c_scores[h], PS[h % 4 // 2][:, 512 * (h % 2):512 * (h % 2) + 3 * WIN], win[:], 1.0,
                                                   NEG_BIG, ALU.subtract, ALU.max, mx[:, h:h + 1]).then_inc(C["sub"], 1)
                    if h % 4 == 3:
                        v = slice(4 * g, 4 * g + 4)
                        own.at(2 * t + g)
                        dve.wait_ge(C["sub"], done(n + 1))
                        own.step(nc.vector.tensor_tensor(mx[:, v], mx[:, v], sk_s[:, v], ALU.max))
                        own.wait()
                        own.step(nc.vector.scalar_tensor_tensor(out=nb[:, v], in0=mx[:, v], scalar=-1.0, in1=slope[:, v],
                                                                op0=ALU.mult, op1=ALU.mult))
                        own.wait()
                        nc.vector.tensor_tensor(mx[:, v], nb[:, v], sk[:, v], ALU.add).then_inc(C["bias"], 1)

                def o_c(t, h):
                    if h % 4 < 3:
                        return
                    n = U_C * t + h
                    g = h // 4
                    v = slice(4 * g, 4 * g + 4)
                    dve.wait_ge(C["pv"], done(n + 1))
                    dve.wait_ge(C["esk"], done(2 * t + g + 1))
                    dve.wait_ge(C["o"], done(2 * t + g))
                    nc.vector.tensor_tensor(rc[:, v], sm[:, v], cc[:, v], ALU.add).then_inc(C["den"], 1)
                    dve.wait_ge(C["den"], done(4 * t + 2 * g + 1))
                    nc.vector.reciprocal(rc[:, v], rc[:, v]).then_inc(C["den"], 1)
                    dve.wait_ge(C["den"], done(4 * t + 2 * g + 2))
                    dve.wait_ge(C[f"sent{g}"], landed(t))
                    nc.vector.tensor_tensor(out[:, 256 * g:256 * g + 256].rearrange("p (h w) -> p h w", h=4),
                                            PO[g][:, 0:256].rearrange("p (h w) -> p h w", h=4),
                                            rc[:, v].rearrange("p (h a) -> p h a", a=1).to_broadcast([P, 4, C_DIM]), ALU.mult)\
                      .then_inc(C["o"], 1)
                own = Own(dve, L["dve"], base, 2)
                for i in range(2):
                    dve.wait_ge(B[f"sent{i}"], landed(T))
                dve.wait_ge(B["exp"], done(U_B * T))
                dve.wait_ge(B["o"], done(U_B * T))
                dve.wait_ge(L["consts"], 5 + C_HEADS + 5)
                sweep(dve, [(0, sub_c), (8, o_c)], U_C, T, peel_last=True)
        clear(nc, [s for group in (L, A, B, C) for s in group.values()])


def merge(nc, ident, x, w_branch, w_o, g_ffn, w_router, x2_out, aff, D):
    OK = OUT_W // P
    NB = len(w_branch)
    with ExitStack() as st:
        def sb(name, shape, dt=F32):
            return st.enter_context(nc.sbuf_tensor(name, shape, dt))

        NW = NB * OK + KT
        w_hi = sb("mw_hi", [P, NW, DM], F32R)
        w_lo = sb("mw_lo", [P, NW, DM], F32R)
        o_in = sb("o_in", [P, NB * OUT_W])
        sig = [sb(f"msig{i}", [P, 512]) for i in range(3)]
        oT_hi = [sb(f"oT_hi{b}", [P, OK * P], F32R) for b in range(NB)]
        oT_lo = [sb(f"oT_lo{b}", [P, OK * P], F32R) for b in range(NB)]
        merged = sb("merged", [P, DM])
        mT_hi = sb("mT_hi", [P, DM], F32R)
        mT_lo = sb("mT_lo", [P, DM], F32R)
        x2 = sb("x2", [P, DM])
        hT = sb("hT", [P, DM])
        wr = sb("wr", [P, KT, N_EXP])
        gT = sb("gT", [P, KT])
        few = sb("few", [P, 8])
        ex = sb("ex", [P, N_EXP])
        neg_half = sb("mneg_half", [P, 1])
        ssq, var, rs, top, neg, den, rden = (few[:, i:i + 1] for i in range(7))

        BR = [st.enter_context(nc.psum_tensor(f"BR{i}", [P, 512], F32)) for i in range(2)]
        WO = [st.enter_context(nc.psum_tensor(f"WO{i}", [P, 512], F32)) for i in range(2)]
        OT = st.enter_context(nc.psum_tensor("OT", [P, 512], F32))
        MT = [st.enter_context(nc.psum_tensor(f"MT{i}", [P, 512], F32)) for i in range(2)]
        RT = st.enter_context(nc.psum_tensor("RT", [P, 512], F32))

        S = {n: st.enter_context(nc.semaphore("m_" + n)) for n in
             "small consts w_in0 w_in1 w_in2 w_hi w_lo o_in sig0 sig1 sig2 x_in o_tr oT_hi oT_lo br mul mrg m_tr mT_hi mT_lo wo x2 "
             "out_sent sq var rs h2 h2_sent h_tr hT rt bias exp den aff".split()}
        stages = [merged, x2, hT]
        halves = [slice(512 * h, 512 * h + 512) for h in range(2)]

        def w_rows(i):
            if i < NB * OK:
                return w_branch[i // OK][(i % OK) * P:(i % OK + 1) * P, :]
            i -= NB * OK
            return w_o[i * P:(i + 1) * P, :]

        with nc.Block() as block:
            def over_tiles(eng, turn):
                turn(0, None)
                with eng.Fori(1, T) as t:
                    turn(t, t - 1)
                turn(None, T - 1)

            @block.sync
            def _(sp):
                for n in ("o_in", "sig0", "sig1", "sig2", "x_in", "out_sent", "h2_sent"):
                    sp.sem_inc(S[n], 16 * CREDIT)
                sp.dma_start(wr[:], w_router.rearrange("(k p) n -> p k n", p=P)).then_inc(S["small"], 16)
                with nc.allow_non_contiguous_dma(reason="4 KB of gains, once"):
                    sp.dma_start(gT[:], g_ffn.rearrange("(k p) -> p k", p=P)).then_inc(S["small"], 16)

                def load_sig(t, i):
                    sp.wait_ge(S["mrg"], done(6 * t + i - 2))
                    sp.dma_start(sig[i % 3][:], tile_of(D["sig"][:, 512 * i:512 * i + 512], t)).then_inc(S[f"sig{i % 3}"], 16)

                def load_o(t):
                    sp.wait_ge(S["o_tr"], done(NB * t))
                    sp.dma_start(o_in[:], tile_of(D["o"], t)).then_inc(S["o_in"], 16)

                load_o(0)
                for i in range(NW):
                    if i >= 3:
                        sp.wait_ge(S["w_lo"], i - 2)
                    sp.dma_start(stages[i % 3][:], w_rows(i)).then_inc(S[f"w_in{i % 3}"], 16)
                for i in range(3):
                    load_sig(0, i)
                sp.wait_ge(S["w_lo"], NW)

                def turn(t, b, more=True):
                    if t is not None:
                        load_sig(t, 3)
                        load_sig(t, 4)
                        load_sig(t, 5)
                    if more:
                        load_o(t + 1)
                    if b is not None:
                        sp.wait_ge(S["x2"], done(2 * b + 2))
                        sp.dma_start(tile_of(x2_out, b), x2[:]).then_inc(S["out_sent"], 16)
                    if more:
                        load_sig(t + 1, 0)
                        load_sig(t + 1, 1)
                    if b is not None:
                        sp.wait_ge(S["h2"], done(b + 1))
                        sp.dma_start(tile_of(D["h2"], b), x2[:]).then_inc(S["h2_sent"], 16)
                    if t is not None:
                        sp.wait_ge(S["h2_sent"], landed(t))
                        sp.wait_ge(S["h_tr"], done(2 * t))
                        sp.dma_start(x2[:], tile_of(x, t)).then_inc(S["x_in"], 16)
                    if more:
                        load_sig(t + 1, 2)
                turn(0, None)
                with sp.Fori(1, T - 1) as t:
                    turn(t, t - 1)
                turn(T - 1, T - 2, more=False)
                turn(None, T - 1, more=False)
                sp.wait_ge(S["out_sent"], landed(T))
                sp.wait_ge(S["h2_sent"], landed(T))

            @block.gpsimd
            def _(pool):
                pool.sem_inc(S["rs"], CREDIT)
                nc.gpsimd.memset(neg_half[:], -0.5).then_inc(S["consts"], 1)
                pool.wait_ge(S["consts"], 1)
                with pool.Fori(0, T) as t:
                    pool.wait_ge(S["var"], done(t + 1))
                    nc.gpsimd.tensor_tensor(rs, var, neg_half[:], ALU.pow).then_inc(S["rs"], 1)

            @block.tensor
            def _(pe):
                for n in ("o_tr", "br", "m_tr", "wo", "h_tr", "rt"):
                    pe.sem_inc(S[n], CREDIT)

                def flip(bank, src, at):
                    for k in range(4):
                        mm = nc.tensor.transpose(bank[:, k * P:(k + 1) * P], src[:, at + k * P:at + (k + 1) * P], ident[:])
                    return mm

                def turn_o(t, b):
                    if b == 0:
                        pe.wait_ge(S["o_in"], landed(t + 1))
                    pe.wait_ge(S["oT_lo"], done(NB * t + b))
                    flip(OT, o_in, b * OUT_W).then_inc(S["o_tr"], 1)

                def branch(t, b, h):
                    if isinstance(t, int):
                        pe.wait_ge(S["w_lo"], OK * (b + 1))
                    pe.wait_ge(S["oT_lo"], done(NB * t + b + 1))
                    pe.wait_ge(S["mrg"], done(6 * t + 2 * b + h - 1))
                    n = 0
                    for k in range(OK):
                        at = slice(k * P, (k + 1) * P)
                        for l, r in ((oT_hi, w_hi), (oT_hi, w_lo), (oT_lo, w_hi)):
                            mm = nc.tensor.matmul(BR[h][:], l[b][:, at], r[:, b * OK + k, halves[h]],
                                                  start=(n == 0), stop=(n == 3 * OK - 1))
                            n += 1
                    mm.then_inc(S["br"], 1)

                def turn_m(t):
                    pe.wait_ge(S["mrg"], done(6 * t + 6))
                    pe.wait_ge(S["hT"], done(2 * t))
                    for g in range(2):
                        flip(MT[g], merged, 512 * g).then_inc(S["m_tr"], 1)

                def w_out(t):
                    pe.wait_ge(S["w_lo"], NW)
                    pe.wait_ge(S["mT_lo"], done(2 * t + 2))
                    for h in range(2):
                        pe.wait_ge(S["x2"], done(2 * t + h - 1))
                        n = 0
                        for k in range(KT):
                            at = slice(k * P, (k + 1) * P)
                            for l, r in ((mT_hi, w_hi), (mT_hi, w_lo), (mT_lo, w_hi)):
                                mm = nc.tensor.matmul(WO[h][:], l[:, at], r[:, NB * OK + k, halves[h]],
                                                      start=(n == 0), stop=(n == 3 * KT - 1))
                                n += 1
                        mm.then_inc(S["wo"], 1)

                def turn_h(t):
                    pe.wait_ge(S["h2"], done(t + 1))
                    pe.wait_ge(S["mT_lo"], done(2 * t + 2))
                    for g in range(2):
                        flip(MT[g], x2, 512 * g).then_inc(S["h_tr"], 1)

                def router(t):
                    pe.wait_ge(S["hT"], done(2 * t + 2))
                    pe.wait_ge(S["exp"], done(t))
                    for k in range(KT):
                        mm = nc.tensor.matmul(RT[:, 0:N_EXP], hT[:, k * P:(k + 1) * P], wr[:, k, :], start=(k == 0), stop=(k == KT - 1))
                    mm.then_inc(S["rt"], 1)

                def turn(t, before):
                    now, last = t is not None, before is not None
                    if now:
                        turn_o(t, 0)
                        turn_o(t, 1)
                        branch(t, 0, 0)
                    if last:
                        turn_m(before)
                    if now:
                        branch(t, 0, 1)
                        turn_o(t, 2)
                        branch(t, 1, 0)
                        branch(t, 1, 1)
                    if last:
                        w_out(before)
                    if now:
                        branch(t, 2, 0)
                    if last:
                        turn_h(before)
                    if now:
                        branch(t, 2, 1)
                    if last:
                        router(before)
                pe.wait_ge(S["small"], 32)
                over_tiles(pe, turn)

            @block.scalar
            def _(act):
                for n in ("oT_hi", "mT_hi", "sq", "exp"):
                    act.sem_inc(S[n], CREDIT)
                for i in range(NW):
                    act.wait_ge(S[f"w_in{i % 3}"], 16 * (i // 3 + 1))
                    nc.scalar.activation(w_hi[:, i, :], stages[i % 3][:], ACT.Copy).then_inc(S["w_hi"], 1)
                act.wait_ge(S["w_lo"], NW)

                def hi_o(t, b):
                    act.wait_ge(S["o_tr"], done(NB * t + b + 1))
                    act.wait_ge(S["br"], done(6 * t + 2 * b - 4) if not isinstance(t, int) or t else 1)
                    nc.scalar.activation(oT_hi[b][:], OT[:], ACT.Copy).then_inc(S["oT_hi"], 1)

                def hi_m(t):
                    for g in range(2):
                        act.wait_ge(S["m_tr"], done(2 * t + g + 1))
                        act.wait_ge(S["wo"], done(2 * t))
                        nc.scalar.activation(mT_hi[:, halves[g]], MT[g][:], ACT.Copy).then_inc(S["mT_hi"], 1)

                def turn(t, before):
                    now, last = t is not None, before is not None
                    if now:
                        hi_o(t, 0)
                        hi_o(t, 1)
                    if last:
                        hi_m(before)
                    if now:
                        hi_o(t, 2)
                    if last:
                        act.wait_ge(S["x2"], done(2 * before + 2))
                        act.wait_ge(S["rt"], done(before))
                        act.wait_ge(S["var"], done(before))
                        nc.scalar.activation(hT[:], x2[:], ACT.Square, accum_out=ssq).then_inc(S["sq"], 1)
                        act.wait_ge(S["bias"], done(before + 1))
                        act.wait_ge(S["aff"], done(before))
                        nc.scalar.activation(ex[:], RT[:, 0:N_EXP], ACT.Exp, bias=neg, accum_out=den).then_inc(S["exp"], 1)
                over_tiles(act, turn)

            @block.vector
            def _(dve):
                for n in ("oT_lo", "mul", "mrg", "mT_lo", "x2", "var", "h2", "hT", "bias", "den", "aff"):
                    dve.sem_inc(S[n], CREDIT)
                for i in range(NW):
                    dve.wait_ge(S["w_hi"], i + 1)
                    nc.vector.tensor_tensor(w_lo[:, i, :], stages[i % 3][:], w_hi[:, i, :].bitcast(F32), ALU.subtract).then_inc(S["w_lo"], 1)
                dve.wait_ge(S["w_lo"], NW)
                dve.wait_ge(S["small"], 32)

                def lo_o(t, b):
                    dve.wait_ge(S["oT_hi"], done(NB * t + b + 1))
                    nc.vector.tensor_tensor(oT_lo[b][:], OT[:], oT_hi[b][:].bitcast(F32), ALU.subtract).then_inc(S["oT_lo"], 1)

                def merge_half(t, b, h):
                    i = 2 * b + h
                    m = merged[:, halves[h]]
                    s = sig[i % 3]
                    dve.wait_ge(S["br"], done(6 * t + i + 1))
                    dve.wait_ge(S[f"sig{i % 3}"], landed(2 * t + i // 3 + 1))
                    if b == 0:
                        dve.wait_ge(S["m_tr"], done(2 * t))
                        nc.vector.tensor_tensor(m, BR[h][:], s[:], ALU.mult).then_inc(S["mrg"], 1)
                    else:
                        nc.vector.tensor_tensor(s[:], BR[h][:], s[:], ALU.mult).then_inc(S["mul"], 1)
                        dve.wait_ge(S["mul"], done(4 * t + i - 1))
                        dve.wait_ge(S["mrg"], done(6 * t + i - 1))
                        nc.vector.tensor_tensor(m, m, s[:], ALU.add).then_inc(S["mrg"], 1)

                def turn(t, before):
                    now, last = t is not None, before is not None
                    if now:
                        lo_o(t, 0)
                        lo_o(t, 1)
                        merge_half(t, 0, 0)
                    if last:
                        for g in range(2):
                            dve.wait_ge(S["mT_hi"], done(2 * before + g + 1))
                            nc.vector.tensor_tensor(mT_lo[:, halves[g]], MT[g][:], mT_hi[:, halves[g]].bitcast(F32), ALU.subtract)\
                              .then_inc(S["mT_lo"], 1)
                    if now:
                        merge_half(t, 0, 1)
                        lo_o(t, 2)
                        merge_half(t, 1, 0)
                        merge_half(t, 1, 1)
                    if last:
                        dve.wait_ge(S["x_in"], landed(before + 1))
                        for h in range(2):
                            dve.wait_ge(S["wo"], done(2 * before + h + 1))
                            nc.vector.tensor_tensor(x2[:, halves[h]], WO[h][:], x2[:, halves[h]], ALU.add).then_inc(S["x2"], 1)
                        dve.wait_ge(S["sq"], done(before + 1))
                        dve.wait_ge(S["rs"], done(before))
                        nc.vector.tensor_scalar(var, ssq, 1.0 / DM, EPS, ALU.mult, ALU.add).then_inc(S["var"], 1)
                    if now:
                        merge_half(t, 2, 0)
                    if last:
                        dve.wait_ge(S["rs"], done(before + 1))
                        dve.wait_ge(S["out_sent"], landed(before + 1))
                        dve.wait_ge(S["x2"], done(2 * before + 2))
                        nc.vector.tensor_scalar(x2[:], x2[:], rs, None, ALU.mult).then_inc(S["h2"], 1)
                    if now:
                        merge_half(t, 2, 1)
                    if last:
                        for g in range(2):
                            dve.wait_ge(S["h_tr"], done(2 * before + g + 1))
                            nc.vector.tensor_tensor(hT[:, halves[g]].rearrange("p (k w) -> p k w", k=4),
                                                    MT[g][:].rearrange("p (k w) -> p k w", k=4),
                                                    gT[:, 4 * g:4 * g + 4].rearrange("p (k a) -> p k a", a=1).to_broadcast([P, 4, P]),
                                                    ALU.mult).then_inc(S["hT"], 1)
                        dve.wait_ge(S["rt"], done(before + 1))
                        dve.wait_ge(S["bias"], done(before))
                        nc.vector.tensor_reduce(top, RT[:, 0:N_EXP], AX.X, ALU.max).then_inc(S["den"], 1)
                        dve.wait_ge(S["den"], done(2 * before + 1))
                        dve.wait_ge(S["exp"], done(before))
                        nc.vector.tensor_scalar(neg, top, -1.0, None, ALU.mult).then_inc(S["bias"], 1)
                        dve.wait_ge(S["exp"], done(before + 1))
                        dve.wait_ge(S["aff"], done(before))
                        nc.vector.reciprocal(rden, den).then_inc(S["den"], 1)
                        dve.wait_ge(S["den"], done(2 * before + 2))
                        nc.vector.tensor_scalar(aff[:, bass.ds(before, 1), :].rearrange("p a n -> p (a n)"), ex[:], rden, None, ALU.mult)\
                          .then_inc(S["aff"], 1)
                over_tiles(dve, turn)


def experts(nc, ident, g_ffn, w_gate, w_up, w_down, out, aff, D):
    with ExitStack() as st:
        def sb(name, shape, dt=F32):
            return st.enter_context(nc.sbuf_tensor(name, shape, dt))

        SLOTS = 3 * KT
        RAW, SPLIT = 16, 8
        LEAD = 6
        TH = KT + 5
        raw = [sb(f"raw{i}", [P, DM]) for i in range(RAW)]
        e_hi = [sb(f"e_hi{i}", [P, DM], F32R) for i in range(SPLIT)]
        e_lo = [sb(f"e_lo{i}", [P, DM], F32R) for i in range(SPLIT)]
        xg = [sb(f"xg{i}", [P, DM]) for i in range(2)]
        xT_hi = [sb(f"xT_hi{i}", [P, DM], F32R) for i in range(2)]
        xT_lo = [sb(f"xT_lo{i}", [P, DM], F32R) for i in range(2)]
        hid = sb("hid", [P, DFF])
        dT_hi = sb("dT_hi", [P, DFF], F32R)
        dT_lo = sb("dT_lo", [P, DFF], F32R)
        y = [sb(f"y{i}", [P, DM]) for i in range(2)]
        gain = sb("egain", [P, DM])
        pool_of = [sb(f"affT{i}", [N_EXP, SEQ]) for i in range(2)]
        vals = sb("vals", [N_EXP, CAP])
        idx = sb("idx", [N_EXP, CAP], U32)
        idx_f = sb("idx_f", [N_EXP, CAP])
        idx_t = sb("idx_t", [P, N_EXP])
        val_t = sb("val_t", [P, N_EXP])
        take = [sb(f"take{i}", [P, 1], U32) for i in range(2)]
        give = [sb(f"give{i}", [P, 1], U32) for i in range(2)]
        weight = [sb(f"weight{i}", [P, 1]) for i in range(2)]

        G, U, Y, XT = ([st.enter_context(nc.psum_tensor(f"{n}ps{i}", [P, 512], F32)) for i in range(2)] for n in "GUYX")
        S = {n: st.enter_context(nc.semaphore("e_" + n)) for n in
             ("w_hi w_lo used silu hid x_tr xT_hi xT_lo d_tr dT_hi dT_lo y added sent take give gained gate "
              "gain aff_tr top idx_tr idx xg0 xg1").split() + [f"raw{i}" for i in range(RAW)]}
        halves = [slice(512 * h, 512 * h + 512) for h in range(2)]

        def number(e, s):
            return KT + SLOTS * e + s

        def uses(i, j, s):
            return (SLOTS * 2 // RAW) * i + (KT + SLOTS * j + s) // RAW

        def over_experts(eng, turn, first=0):
            for e in range(2 * first):
                turn(e, e // 2, e % 2)
            with eng.Fori(first, N_EXP // 2 - 1) as i:
                for j in range(2):
                    turn(2 * i + j, i, j)
            for j in range(2):
                turn(N_EXP - 2 + j, N_EXP // 2 - 1, j)

        def last(e):
            return isinstance(e, int) and e == N_EXP - 1

        def length(e):
            return 2 * KT if last(e) else SLOTS

        def after_gate(e):
            return KT if isinstance(e, int) and e == 0 else number(e, 0) - KT

        def after_up(e):
            return number(e, KT)

        def after_down(e):
            return number(e, length(e))

        with nc.Block() as block:
            @block.sync
            def _(sp):
                for i in range(RAW):
                    sp.sem_inc(S[f"raw{i}"], 16 * CREDIT)

                def load(w, e, k, n, pos):
                    if not isinstance(n, int) or n >= RAW:
                        sp.wait_ge(S["w_lo"], done(n - RAW + 1))
                    sp.dma_start(raw[pos % RAW][:], w[bass.ds(e, 1), k * P:(k + 1) * P, :].rearrange("a p n -> (a p) n"))\
                      .then_inc(S[f"raw{pos % RAW}"], 16)

                for k in range(KT):
                    load(w_gate, 0, k, k, k)

                def turn(e, i, j):
                    for s in range(length(e)):
                        w = w_up if s < KT else w_down if s >= length(e) - KT else w_gate
                        load(w, e + 1 if w is w_gate else e, s % KT, number(e, s), KT + SLOTS * j + s)
                over_experts(sp, turn, first=1)

            @block.gpsimd
            def _(pool):
                for n in ("gained", "sent"):
                    pool.sem_inc(S[n], CREDIT)
                pool.dma_start(gain[:], bcast_rows(g_ffn, DM)).then_inc(S["gain"], 16)
                pool.wait_ge(S["gain"], 16)

                def gather(e, i, j):
                    pool.wait_ge(S["take"], done(e + 1))
                    pool.wait_ge(S["x_tr"], done(2 * e - 2))
                    pool.sem_inc(S["gate"], 1)
                    nc.gpsimd.indirect_dma_start(xg[j][:], None, D["h2"], bass.IndirectOffsetOnAxis(ap=take[j][:, 0:1], axis=0))\
                      .then_inc(S[f"xg{j}"], 16)
                    pool.wait_ge(S[f"xg{j}"], 16 * (i + 1))
                    nc.gpsimd.tensor_tensor(xg[j][:], xg[j][:], gain[:], ALU.mult).then_inc(S["gained"], 1)

                def scatter(e, i, j):
                    pool.wait_ge(S["give"], done(e + 1))
                    pool.wait_ge(S["y"], done(2 * e + 2))
                    pool.sem_inc(S["gate"], 1)
                    nc.gpsimd.indirect_dma_start(out, bass.IndirectOffsetOnAxis(ap=give[j][:, 0:1], axis=0), y[j][:], None,
                                                 compute_op=ALU.add).then_inc(S["added"], 16)
                    pool.wait_ge(S["added"], 16 * (e + 1))
                    pool.sem_inc(S["sent"], 1)
                gather(0, 0, 0)
                gather(1, 0, 1)
                with pool.Fori(0, N_EXP // 2 - 1) as i:
                    for j in range(2):
                        gather(2 * i + j + 2, i + 1, j)
                        scatter(2 * i + j, i, j)
                for j in range(2):
                    scatter(N_EXP - 2 + j, N_EXP // 2 - 1, j)
                pool.wait_ge(S["added"], 16 * N_EXP)

            @block.tensor
            def _(pe):
                for n in ("used", "x_tr", "d_tr"):
                    pe.sem_inc(S[n], CREDIT)
                for t in range(T):
                    mm = nc.tensor.transpose(XT[t // 4][0:N_EXP, (t % 4) * P:(t % 4 + 1) * P], aff[:, t, :], ident[:])
                mm.then_inc(S["aff_tr"], 1)
                pe.wait_ge(S["top"], 1 + 3 * CAP // 8 + 1)
                nc.tensor.transpose(XT[0][:, 0:N_EXP], idx_f[:], ident[0:N_EXP, 0:N_EXP])
                nc.tensor.transpose(XT[1][:, 0:N_EXP], vals[:], ident[0:N_EXP, 0:N_EXP]).then_inc(S["idx_tr"], 1)
                pe.wait_ge(S["idx"], 2)

                def turn_x(e, j):
                    pe.wait_ge(S["gained"], done(e + 1))
                    pe.wait_ge(S["dT_lo"], done(2 * e - 2))
                    for g in range(2):
                        for k in range(4):
                            at = slice((4 * g + k) * P, (4 * g + k + 1) * P)
                            mm = nc.tensor.transpose(XT[g][:, k * P:(k + 1) * P], xg[j][:, at], ident[:])
                        mm.then_inc(S["x_tr"], 1)

                def chunk(bank, hi, lo, k, n):
                    pe.wait_ge(S["w_lo"], done(n + 1))
                    at = slice(k * P, (k + 1) * P)
                    for i, (l, r) in enumerate(((hi, e_hi), (hi, e_lo), (lo, e_hi))):
                        for h in range(2):
                            mm = nc.tensor.matmul(bank[h][:], l[:, at], r[k][:, halves[h]],
                                                  start=(k == 0 and i == 0), stop=(k == KT - 1 and i == 2))
                    mm.then_inc(S["used"], 1)

                def gate(e, j, k, n):
                    if k == 0:
                        pe.wait_ge(S["xT_lo"], done(2 * e + 2))
                        pe.wait_ge(S["silu"], done(2 * e))
                    chunk(G, xT_hi[j], xT_lo[j], k, n)

                turn_x(0, 0)
                for k in range(KT):
                    gate(0, 0, k, k)

                def turn(e, i, j):
                    if not last(e):
                        turn_x(e + 1, 1 - j)
                    pe.wait_ge(S["hid"], done(2 * e))
                    for k in range(KT):
                        chunk(U, xT_hi[j], xT_lo[j], k, number(e, k))
                    for s in range(KT, TH):
                        if not last(e):
                            gate(e + 1, 1 - j, s - KT, number(e, s))
                    pe.wait_ge(S["hid"], done(2 * e + 2))
                    for g in range(2):
                        pe.wait_ge(S["xT_lo"], done(2 * e + 3 + g) if not last(e) else done(2 * e + 2))
                        for k in range(4):
                            at = slice((4 * g + k) * P, (4 * g + k + 1) * P)
                            mm = nc.tensor.transpose(XT[g][:, k * P:(k + 1) * P], hid[:, at], ident[:])
                        mm.then_inc(S["d_tr"], 1)
                    for s in range(TH, 2 * KT):
                        if not last(e):
                            gate(e + 1, 1 - j, s - KT, number(e, s))
                    pe.wait_ge(S["dT_lo"], done(2 * e + 2))
                    pe.wait_ge(S["y"], done(2 * e))
                    for k in range(KT):
                        chunk(Y, dT_hi, dT_lo, k, number(e, length(e) - KT + k))
                over_experts(pe, turn)

            def around(split, ops):
                def turn(e, i, j):
                    n = length(e)
                    for s in range(n):
                        if s + LEAD < n or not last(e):
                            split(i, j, s + LEAD, number(e, s + LEAD))
                        ops(e, i, j, s if not last(e) or s < KT else s + KT)
                        if last(e) and s == KT - 1:
                            ops(e, i, j, TH - 1)
                return turn

            @block.scalar
            def _(act):
                for n in ("w_hi", "silu", "xT_hi", "dT_hi", "y"):
                    act.sem_inc(S[n], CREDIT)

                def split(i, j, s, n):
                    act.wait_ge(S[f"raw{(KT + SLOTS * j + s) % RAW}"], landed(uses(i, j, s) + 1))
                    if not isinstance(n, int) or n >= SPLIT:
                        act.wait_ge(S["used"], done(n - SPLIT + 1))
                    nc.scalar.activation(e_hi[s % SPLIT][:], raw[(KT + SLOTS * j + s) % RAW][:], ACT.Copy).then_inc(S["w_hi"], 1)

                def x_hi(e, j):
                    for g in range(2):
                        act.wait_ge(S["x_tr"], done(2 * e + g + 1))
                        nc.scalar.activation(xT_hi[j][:, halves[g]], XT[g][:], ACT.Copy).then_inc(S["xT_hi"], 1)

                def silu(e):
                    for h in range(2):
                        act.wait_ge(S["used"], done(after_gate(e)))
                        act.wait_ge(S["d_tr"], done(2 * e))
                        nc.scalar.activation(hid[:, halves[h]], G[h][:], ACT.Silu).then_inc(S["silu"], 1)

                def ops(e, i, j, s):
                    if s == 0 and not last(e):
                        x_hi(e + 1, 1 - j)
                    if s == TH - 1:
                        for g in range(2):
                            act.wait_ge(S["d_tr"], done(2 * e + g + 1))
                            act.wait_ge(S["used"], done(number(e, 0)))
                            nc.scalar.activation(dT_hi[:, halves[g]], XT[g][:], ACT.Copy).then_inc(S["dT_hi"], 1)
                    if s == 2 * KT and not last(e):
                        silu(e + 1)
                    if s == SLOTS - 1:
                        for h in range(2):
                            act.wait_ge(S["used"], done(after_down(e)))
                            act.wait_ge(S["sent"], done(e - 1))
                            act.wait_ge(S["give"], done(e + 1))
                            nc.scalar.activation(y[j][:, halves[h]], Y[h][:], ACT.Copy, scale=weight[j][:]).then_inc(S["y"], 1)

                for s in range(-KT, LEAD - KT):
                    split(0, 0, s, KT + s)
                x_hi(0, 0)
                for s in range(LEAD - KT, LEAD):
                    split(0, 0, s, KT + s)
                silu(0)
                over_experts(act, around(split, ops))

            @block.vector
            def _(dve):
                for n in ("w_lo", "hid", "xT_lo", "dT_lo", "take", "give"):
                    dve.sem_inc(S[n], CREDIT)

                def split(i, j, s, n):
                    dve.wait_ge(S["w_hi"], done(n + 1))
                    at = (KT + SLOTS * j + s) % RAW
                    nc.vector.tensor_tensor(e_lo[s % SPLIT][:], raw[at][:], e_hi[s % SPLIT][:].bitcast(F32), ALU.subtract)\
                      .then_inc(S["w_lo"], 1)

                dve.wait_ge(S["aff_tr"], 1)
                for h in range(2):
                    op = nc.vector.tensor_copy(pool_of[0][:, halves[h]], XT[h][0:N_EXP, :])
                op.then_inc(S["top"], 1)
                n = 1
                for r in range(CAP // 8):
                    at = slice(8 * r, 8 * r + 8)
                    left, rest = pool_of[r % 2], pool_of[1 - r % 2]
                    dve.wait_ge(S["top"], n)
                    nc.vector.max(vals[:, at], left[:]).then_inc(S["top"], 1)
                    dve.wait_ge(S["top"], n + 1)
                    nc.vector.max_index(idx[:, at], vals[:, at], left[:]).then_inc(S["top"], 1)
                    nc.vector.match_replace(rest[:], vals[:, at], left[:], -1.0).then_inc(S["top"], 1)
                    if r < LEAD:
                        split(0, 0, r - KT, r)
                    n += 3
                dve.wait_ge(S["top"], n)
                nc.vector.tensor_copy(idx_f[:], idx[:]).then_inc(S["top"], 1)
                dve.wait_ge(S["idx_tr"], 1)
                nc.vector.tensor_copy(idx_t[:], XT[0][:, 0:N_EXP]).then_inc(S["idx"], 1)
                nc.vector.tensor_copy(val_t[:], XT[1][:, 0:N_EXP]).then_inc(S["idx"], 1)
                dve.wait_ge(S["idx"], 2)
                nc.vector.tensor_copy(take[0][:], idx_t[:, 0:1]).then_inc(S["take"], 1)
                nc.vector.tensor_copy(take[1][:], idx_t[:, 1:2]).then_inc(S["take"], 1)

                def x_lo(e, j):
                    for g in range(2):
                        dve.wait_ge(S["xT_hi"], done(2 * e + g + 1))
                        nc.vector.tensor_tensor(xT_lo[j][:, halves[g]], XT[g][:], xT_hi[j][:, halves[g]].bitcast(F32), ALU.subtract)\
                          .then_inc(S["xT_lo"], 1)

                def ops(e, i, j, s):
                    if s == 0 and not last(e):
                        x_lo(e + 1, 1 - j)
                    if s == 3 and not (isinstance(e, int) and e >= N_EXP - 2):
                        dve.wait_ge(S[f"xg{j}"], 16 * (i + 1))
                        nc.vector.tensor_scalar(take[j][:], idx_t[:, bass.ds(e + 2, 1)], 1.0, None, ALU.mult).then_inc(S["take"], 1)
                    if s == 5:
                        dve.wait_ge(S["sent"], done(e - 1))
                        dve.wait_ge(S["y"], done(2 * e - 2))
                        nc.vector.tensor_scalar(weight[j][:], val_t[:, bass.ds(e, 1)], 1.0, None, ALU.mult)
                        nc.vector.tensor_scalar(give[j][:], idx_t[:, bass.ds(e, 1)], 1.0, None, ALU.mult).then_inc(S["give"], 1)
                    if s == KT - 1:
                        for h in range(2):
                            dve.wait_ge(S["used"], done(after_up(e)))
                            dve.wait_ge(S["silu"], done(2 * e + 2))
                            nc.vector.tensor_tensor(hid[:, halves[h]], U[h][:], hid[:, halves[h]], ALU.mult).then_inc(S["hid"], 1)
                    if s == TH - 1:
                        for g in range(2):
                            dve.wait_ge(S["dT_hi"], done(2 * e + g + 1))
                            nc.vector.tensor_tensor(dT_lo[:, halves[g]], XT[g][:], dT_hi[:, halves[g]].bitcast(F32), ALU.subtract)\
                              .then_inc(S["dT_lo"], 1)

                x_lo(0, 0)
                for s in range(LEAD - KT, LEAD):
                    split(0, 0, s, KT + s)
                over_experts(dve, around(split, ops))


def build(nc, A, out, D):
    with nc.sbuf_tensor("ident", [P, P], F32) as ident, nc.sbuf_tensor("aff", [P, T, N_EXP], F32) as aff:
        project(nc, ident, A["x"], A["positions"], A["norm_mix_g"], A["w_in"], A["diff_qk_g"], A["mla_cq_g"], A["w_uq"],
                A["mla_ckv_g"], A["w_ukv"], A["mla_qk_g"], A["swa_qk_g"], A["inv_freq"], D)
        attention(nc, ident, A["positions"], A["diff_lambda"], A["diff_out_g"], A["swa_sink"], D)
        merge(nc, ident, A["x"], [A["w_branch_a"], A["w_branch_b"], A["w_branch_c"]], A["w_o"], A["norm_ffn_g"], A["w_router"],
              out, aff, D)
        experts(nc, ident, A["norm_ffn_g"], A["w_exp_gate"], A["w_exp_up"], A["w_exp_down"], out, aff, D)


def kernel(**inputs):
    import numpy as np
    import concourse.bacc as bacc
    from concourse.bass_utils import run_bass_kernel_spmd

    nc = bacc.Bacc("TRN2", target_bir_lowering=False, num_devices=1)
    given = {name: np.ascontiguousarray(a)[0] for name, a in inputs.items()}
    given["inv_freq"] = (1.0 / (ROPE_THETA ** (np.arange(0, B_ROPE, 2, dtype=np.float32) / np.float32(B_ROPE)))).astype(np.float32)
    A = {name: nc.dram_tensor("in_" + name, a.shape, mybir.dt.from_np(a.dtype), kind="ExternalInput").ap() for name, a in given.items()}
    shapes = dict(mix=(SEQ, N_MIX), sig=(SEQ, 3 * DM), qa=(T, P, 2048), ka=(P, 2 * A_HEADS, SEQ), qc=(T, P, 2048),
                  kc=(P, C_KV, SEQ), qb=(T, B_QK, 2048), kb=(B_QK, 2 * B_HEADS, SEQ), vb=(SEQ, OUT_W), o=(SEQ, 3 * OUT_W),
                  h2=(SEQ, DM))
    D = {name: nc.dram_tensor("s_" + name, shape, F32, kind="Internal").ap() for name, shape in shapes.items()}
    out = nc.dram_tensor("layer_out", (SEQ, DM), F32, kind="ExternalOutput").ap()
    build(nc, A, out, D)
    result = run_bass_kernel_spmd(nc, [{"in_" + name: a for name, a in given.items()}], core_ids=[0])
    return result.results[0]["layer_out"].reshape(1, SEQ, DM)
```

```python
from contextlib import ExitStack

import concourse.bass as bass
from concourse import mybir

F32 = mybir.dt.float32
F32R = mybir.dt.float32r
I32 = mybir.dt.int32
U32 = mybir.dt.uint32
ALU = mybir.AluOpType
ACT = mybir.ActivationFunctionType
AX = mybir.AxisListType

P = 128
SEQ = 1024
DM = 1024
KT = DM // P
T = SEQ // P
EPS = 1e-6

A_HEADS, A_DIM, A_VDIM = 4, 64, 128
B_HEADS, B_NOPE, B_ROPE, B_VDIM = 8, 64, 32, 64
B_QK = B_NOPE + B_ROPE
B_QL, B_KVL = 384, 256
C_HEADS, C_KV, C_DIM = 8, 2, 64
WIN = 128
OUT_W = 512
ROPE_THETA = 10000.0

COL_QA = 0
COL_KA = COL_QA + 2 * A_HEADS * A_DIM
COL_VA = COL_KA + 2 * A_HEADS * A_DIM
COL_CQ = COL_VA + A_HEADS * A_VDIM
COL_CKV = COL_CQ + B_QL
COL_KR = COL_CKV + B_KVL
COL_QC = COL_KR + B_ROPE
COL_KC = COL_QC + C_HEADS * C_DIM
COL_VC = COL_KC + C_KV * C_DIM
COL_GATE = COL_VC + C_KV * C_DIM
N_MIX = COL_GATE
NCH = 8
W_MIX = N_MIX // NCH
W_GATE = 3 * DM // NCH

A_SLOPES = [2.0 ** (-8.0 * (h + 1) / A_HEADS) for h in range(A_HEADS)]
C_SLOPES = [2.0 ** (-8.0 * (h + 1) / C_HEADS) for h in range(C_HEADS)]
LAM_INIT = 0.2

N_EXP, CAP, DFF = 16, 128, 1024

TWO_PI = 6.283185307179586
TWO_PI_PARTS = (6.28125, 0.00193500518798828125, 3.0199159795074593e-07)
MAGIC = 12582912.0
PI_IN = 3.1415925


CREDIT = 4


def done(n):
    return n + CREDIT


def landed(n):
    return 16 * n + 16 * CREDIT


class Chain:

    def __init__(self, eng, sem):
        self.eng, self.sem, self.base, self.k, self.total = eng, sem, 0, 0, 0

    def step(self, ins):
        ins.then_inc(self.sem, 1)
        self.k += 1
        return ins

    def wait(self):
        self.eng.wait_ge(self.sem, self.base + self.k)

    def enter(self, turn, per):
        self.total += self.k
        self.base, self.k = turn * per + self.total, 0

    def leave(self, turns, per):
        assert self.k == per, (self.k, per)
        self.total += turns * per
        self.base, self.k = self.total, 0


def clear(nc, sems):
    with nc.Block() as block:
        @block.vector
        def _(dve):
            for s in sems:
                dve.sem_clear(s)


def bcast_rows(ap, n):
    return ap.rearrange("(a n) -> a n", a=1).to_broadcast([P, n])


def tile_of(ap, t):
    return ap.rearrange("(t p) n -> t p n", p=P)[bass.ds(t, 1)].rearrange("a p n -> (a p) n")


def project(nc, ident, x, positions, g_mix, w_in, g_a, g_cq, w_uq, g_ckv, w_ukv, g_b, g_c, inv_freq, D):
    with ExitStack() as st:
        def sb(name, shape, dt=F32):
            return st.enter_context(nc.sbuf_tensor(name, shape, dt))

        hT_hi = sb("hT_hi", [P, KT, SEQ], F32R)
        hT_lo = sb("hT_lo", [P, KT, SEQ], F32R)
        w_raw = [sb(f"w_raw{h}", [P, 4, W_GATE]) for h in range(2)]
        w_hi = [sb(f"w_hi{c}", [P, KT, W_GATE], F32R) for c in range(2)]
        w_lo = [sb(f"w_lo{c}", [P, KT, W_GATE], F32R) for c in range(2)]
        p_out = sb("p_out", [P, 4, W_GATE])
        pin = [sb(f"pin{j}", [P, N_MIX]) for j in range(2)]
        stage = sb("stage", [P, 2048])
        turned = sb("turned", [P, 2048])
        n1 = sb("n1", [P, 1024])
        sqb = sb("sqb", [P, 1024])
        wu = sb("wu", [P, 3, 768])
        wkv = sb("wkv", [P, 2, 1024])
        cT = sb("cT", [P, 5, P])
        gain_a = sb("gain_a", [P, 2, 64])
        gain_b = sb("gain_b", [P, 2, 96])
        gain_c = sb("gain_c", [P, 2, 64])
        gain_l = sb("gain_l", [P, B_QL + B_KVL])
        pos_i = sb("pos_i", [P, T], I32)
        pos_f = sb("pos_f", [P, T])
        inv = sb("inv", [P, 16])
        cos = sb("cos", [P, T, 16])
        sin = sb("sin", [P, T, 16])
        rot = sb("rot", [P, 5, 128])
        ss = sb("ss", [P, 8])
        var = sb("var", [P, 8])
        rs = sb("rs", [P, 8])
        bss = sb("bss", [P, 2])
        bvar = sb("bvar", [P, 2])
        brs = sb("brs", [P, 2])
        inv_f2 = sb("inv_f2", [P, 2, 8])
        neg_half = sb("neg_half", [P, 8])

        PG = [st.enter_context(nc.psum_tensor(f"PG{i}", [P, 512], F32)) for i in range(4)]
        PT = [st.enter_context(nc.psum_tensor(f"PT{i}", [P, 1024], F32)) for i in range(2)]

        S = {n: st.enter_context(nc.semaphore("p_" + n)) for n in
             ("const_in consts g_in x_in0 x_in1 ssq var rstd h ht_ps ht_hi ht_lo w_in0 w_in1 w_lo w_used "
              "pg p_out sent0 sent1 sent2 sent3 dve_own act_own pin_in0 pin_in1 sq uvar urs unrm uhi ulo utr uev0 uev1 ust "
              "bsq bvar brs bc bt bct bq_ps bkv_ps bq bkv vst rope angles tables").split()}
        sent = [S[f"sent{i}"] for i in range(4)]

        w_v = w_in.rearrange("(k p) n -> p k n", p=P)
        x_t = [pin[0][:, 0:1024], pin[0][:, 1024:2048]]
        h_t = [stage[:, 0:1024], stage[:, 1024:2048]]
        g_t = turned[:, 0:1024]

        UNITS = [("a", COL_QA, 8, 64, gain_a[:, 0], True), ("a", COL_KA, 8, 64, gain_a[:, 1], False),
                 ("c", COL_QC, 8, 64, gain_c[:, 0], True), ("c", COL_KC, 2, 64, gain_c[:, 1], False),
                 ("b", 0, 8, 96, gain_b[:, 0], True), ("b", 768, 8, 96, gain_b[:, 1], False)]
        NU = len(UNITS)

        def heads_of(u, j):
            _, col, G, W, _, _ = UNITS[u]
            return pin[j][:, col:col + G * W].rearrange("p (h w) -> p h w", h=G)

        def stage_of(u):
            name, _, G, W, _, q = UNITS[u]
            if name == "b" or not q:
                return stage[:, 0:G * 2 * W].rearrange("p (h s w) -> p h s w", h=G, s=2)
            return stage[:, 0:G * 4 * W].rearrange("p (h s d w) -> p h s d w", h=G, s=2, d=2)

        def part_of(u, s):
            name, _, G, W, _, q = UNITS[u]
            v = stage_of(u)
            if name == "b" or not q:
                return v[:, :, s, :], lambda ap: ap
            return v[:, :, s, :, :], lambda ap: ap.rearrange("p (h a) w -> p h a w", a=1).to_broadcast([P, G, 2, W])

        def n_blocks(u):
            name, _, G, W, _, q = UNITS[u]
            return 16 if name == "b" or q else G

        def block_w(u):
            return 96 if UNITS[u][0] == "b" else P

        with nc.Block() as block:
            @block.sync
            def _(sp):
                for n in ("w_in0", "w_in1", "x_in0", "x_in1", "pin_in0", "pin_in1", "sent0", "sent1", "sent2", "sent3"):
                    sp.sem_inc(S[n], 16 * CREDIT)

                def load_x(i, j):
                    sp.wait_ge(S["h"], done(2 * i + j - 1))
                    sp.dma_start(x_t[j], tile_of(x, 2 * i + j)).then_inc(S[f"x_in{j}"], 16)

                def load_w(c, col):
                    for h in range(2):
                        sp.wait_ge(S["w_lo"], done(2 * c + h - 1))
                        sp.dma_start(w_raw[h][:], w_v[:, 4 * h:4 * h + 4, bass.ds(col, W_GATE)]).then_inc(S[f"w_in{h}"], 16)

                def send(c, m, dst):
                    sp.wait_ge(S["p_out"], done(T * c + m + 1))
                    sp.dma_start(dst, p_out[:, m % 4, 0:dst.shape[-1]]).then_inc(sent[m % 4], 16)

                def load_pin(j, t, ring=True):
                    if ring:
                        sp.wait_ge(S["unrm"], done(NU * (t - 1)))
                        sp.wait_ge(S["vst"], landed(t - 1))
                    sp.dma_start(pin[j][:], tile_of(D["mix"], t)).then_inc(S[f"pin_in{j}"], 16)

                load_x(0, 0)
                load_x(0, 1)
                load_w(0, 0)
                with sp.Fori(1, T // 2) as i:
                    for j in range(2):
                        load_x(i, j)
                with sp.Fori(0, NCH - 1) as c:
                    for m in range(T):
                        if m == 2:
                            load_w(c + 1, (c + 1) * W_MIX)
                        send(c, m, D["mix"][m * P:(m + 1) * P, bass.ds(c * W_MIX, W_MIX)])
                for m in range(T):
                    if m == 2:
                        load_w(NCH, NCH * W_MIX)
                    send(NCH - 1, m, D["mix"][m * P:(m + 1) * P, (NCH - 1) * W_MIX:])
                    if m in (4, 5):
                        sp.wait_ge(sent[m - 4], landed(2 * NCH - 1))
                        load_pin(m - 4, m - 4, False)
                for s in sent:
                    sp.wait_ge(s, landed(2 * NCH))

                def gates(t, j, more, rows):
                    for m in range(T):
                        if m == 2 and more:
                            load_w(t + NCH + 1, t * W_GATE + (N_MIX + W_GATE))
                        send(t + NCH, m, D["sig"][m * P:(m + 1) * P, bass.ds(t * W_GATE, W_GATE)])
                    if rows:
                        load_pin(j, t + 2)
                with sp.Fori(0, NCH // 2 - 1) as i:
                    for j in range(2):
                        gates(2 * i + j, j, True, True)
                for j in range(2):
                    gates(NCH - 2 + j, j, j == 0, False)
                for s in sent:
                    sp.wait_ge(s, landed(4 * NCH))
                sp.wait_ge(S["ust"], landed(NU * T))
                sp.wait_ge(S["vst"], landed(T))

            @block.gpsimd
            def _(pool):
                for n in ("rstd", "urs", "brs"):
                    pool.sem_inc(S[n], CREDIT)
                pool.dma_start(g_t, bcast_rows(g_mix, DM)).then_inc(S["g_in"], 16)
                nc.gpsimd.memset(neg_half[:], -0.5).then_inc(S["consts"], 1)
                nc.gpsimd.memset(ident[:], 0.0).then_inc(S["consts"], 1)
                for h in range(A_HEADS):
                    f = A_DIM ** -0.5 / A_SLOPES[h]
                    for m in range(2):
                        i = m * A_HEADS + h
                        nc.gpsimd.memset(inv_f2[:, 0, i:i + 1], 1.0 / f ** 2).then_inc(S["consts"], 1)
                for h in range(C_HEADS):
                    f = C_DIM ** -0.5 / C_SLOPES[h]
                    nc.gpsimd.memset(inv_f2[:, 1, h:h + 1], 1.0 / f ** 2).then_inc(S["consts"], 1)
                pool.wait_ge(S["consts"], 2 + 2 * A_HEADS + C_HEADS)
                nc.gpsimd.affine_select(out=ident[:], in_=ident[:], compare_op=ALU.not_equal, fill=1.0, base=0,
                                        pattern=[[-1, P]], channel_multiplier=1).then_inc(S["consts"], 1)
                with pool.Fori(0, T) as t:
                    pool.wait_ge(S["var"], done(t + 1))
                    nc.gpsimd.tensor_tensor(rs[:, 0:1], var[:, 0:1], neg_half[:, 0:1], ALU.pow).then_inc(S["rstd"], 1)
                for ap, dst, n in ((g_a[0], gain_a[:, 0], 64), (g_a[1], gain_a[:, 1], 64), (g_c[0], gain_c[:, 0], 64),
                                   (g_c[1], gain_c[:, 1], 64), (g_b[0], gain_b[:, 0], 96), (g_b[1], gain_b[:, 1], 96),
                                   (g_cq, gain_l[:, 0:B_QL], B_QL), (g_ckv, gain_l[:, B_QL:], B_KVL), (inv_freq, inv[:], 16)):
                    pool.dma_start(dst, bcast_rows(ap, n)).then_inc(S["const_in"], 16)
                with nc.allow_non_contiguous_dma(reason="4 KB of positions, once"):
                    pool.dma_start(pos_i[:], positions.rearrange("(t p) -> p t", p=P)).then_inc(S["const_in"], 16)
                pool.dma_start(wu[:], w_uq.rearrange("(k p) n -> p k n", p=P)).then_inc(S["const_in"], 16)
                pool.dma_start(wkv[:], w_ukv.rearrange("(k p) n -> p k n", p=P)).then_inc(S["const_in"], 16)
                with pool.Fori(0, T // 2) as i:
                    for j in range(2):
                        t = 2 * i + j

                        def rstd(u):
                            G = UNITS[u][2]
                            pool.wait_ge(S["uvar"], done(NU * t + u + 1))
                            nc.gpsimd.tensor_tensor(rs[:, 0:G], var[:, 0:G], neg_half[:, 0:G], ALU.pow).then_inc(S["urs"], 1)

                        pool.wait_ge(S["bvar"], done(2 * t + 2))
                        nc.gpsimd.tensor_tensor(brs[:], bvar[:], neg_half[:, 0:2], ALU.pow).then_inc(S["brs"], 1)
                        for u in range(NU):
                            rstd(u)

            @block.scalar
            def _(act):
                for n in ("ust", "vst"):
                    act.sem_inc(S[n], 16 * CREDIT)
                for n in ("ssq", "ht_hi", "p_out", "sq", "uhi", "uev0", "bsq", "bct", "bq", "bkv"):
                    act.sem_inc(S[n], CREDIT)
                def x_square(t, i, j):
                    act.wait_ge(S[f"x_in{j}"], landed(i + 1))
                    act.wait_ge(S["var"], done(t - 1))
                    act.wait_ge(S["ssq"], done(t))
                    nc.scalar.activation(sqb[:], x_t[j], ACT.Square, accum_out=ss[:, j:j + 1]).then_inc(S["ssq"], 1)

                def h_hi(t, j):
                    act.wait_ge(S["ht_ps"], done(t + 1))
                    nc.scalar.activation(hT_hi[:, :, bass.ds(t * P, P)], PT[j][:].rearrange("p (k w) -> p k w", k=KT),
                                         ACT.Copy).then_inc(S["ht_hi"], 1)

                x_square(0, 0, 0)
                with act.Fori(0, T // 2 - 1) as i:
                    x_square(2 * i + 1, i, 1)
                    h_hi(2 * i, 0)
                    x_square(2 * i + 2, i + 1, 0)
                    h_hi(2 * i + 1, 1)
                x_square(T - 1, T // 2 - 1, 1)
                h_hi(T - 2, 0)
                h_hi(T - 1, 1)
                def evac(c, m, W, fn):
                    act.wait_ge(S["pg"], done(T * c + m + 1))
                    act.wait_ge(sent[m % 4], landed(2 * c + m // 4))
                    nc.scalar.activation(p_out[:, m % 4, 0:W], PG[m % 4][:, 0:W], fn).then_inc(S["p_out"], 1)

                with act.Fori(0, NCH) as c:
                    for m in range(T):
                        evac(c, m, W_MIX, ACT.Copy)
                act.wait_ge(S["angles"], 1)
                nc.scalar.activation(sin[:].rearrange("p t f -> p (t f)"), rot[:, 0, :], ACT.Sin).then_inc(S["tables"], 1)
                nc.scalar.activation(cos[:].rearrange("p t f -> p (t f)"), rot[:, 1, :], ACT.Sin).then_inc(S["tables"], 1)
                def store(t, u):
                    name, _, G, W, _, q = UNITS[u]
                    act.wait_ge(S["uev0"], done(NU * t + u + 1))
                    act.wait_ge(S["uev1"], done(NU * t + u + 1))
                    rows, nb = block_w(u), n_blocks(u)
                    tv = turned[0:rows, 0:nb * P]
                    if q:
                        dst = D["q" + name][bass.ds(t, 1)].rearrange("a p n -> (a p) n")
                    else:
                        dst = D["k" + name][:, :, bass.ds(t * P, P)]
                        tv = tv.rearrange("p (b w) -> p b w", b=nb)
                    act.dma_start(dst, tv).then_inc(S["ust"], 16)

                act.wait_ge(S["tables"], 2)
                with act.Fori(0, NCH // 2) as i:
                    for j in range(2):
                        t = 2 * i + j

                        def gate(m):
                            evac(t + NCH, m, W_GATE, ACT.Sigmoid)

                        def square(u):
                            _, _, G, W, _, _ = UNITS[u]
                            act.wait_ge(S["uvar"], done(NU * t + u))
                            if u == 4:
                                act.wait_ge(S["rope"], done(3 * t + 2))
                            if u == 5:
                                act.wait_ge(S["rope"], done(3 * t + 3))
                                act.wait_ge(S["bkv"], done(2 * t + 2))
                            nc.scalar.activation(sqb[:, 0:G * W].rearrange("p (h w) -> p h w", h=G), heads_of(u, j),
                                                 ACT.Square).then_inc(S["sq"], 1)

                        def hi(u):
                            _, _, G, W, _, _ = UNITS[u]
                            act.wait_ge(S["unrm"], done(NU * t + u + 1))
                            act.wait_ge(S["utr"], done(NU * t + u))
                            dst, like = part_of(u, 0)
                            nc.scalar.activation(dst.bitcast(F32R), like(n1[:, 0:G * W].rearrange("p (h w) -> p h w", h=G)),
                                                 ACT.Copy).then_inc(S["uhi"], 1)

                        def ev(u):
                            rows, half = block_w(u), n_blocks(u) // 2 * P
                            act.wait_ge(S["utr"], done(NU * t + u + 1))
                            act.wait_ge(S["ust"], landed(NU * t + u))
                            nc.scalar.activation(turned[0:rows, 0:half], PT[0][0:rows, 0:half], ACT.Copy).then_inc(S["uev0"], 1)

                        def latent_squares():
                            act.wait_ge(S[f"pin_in{j}"], landed(i + 1))
                            act.wait_ge(S["bvar"], done(2 * t))
                            act.wait_ge(S["bsq"], done(2 * t))
                            r = rot[:, :, :].rearrange("p a b -> p (a b)")
                            act.wait_ge(S["rope"], done(3 * t))
                            nc.scalar.activation(r[:, 0:384], pin[j][:, COL_CQ:COL_CQ + B_QL], ACT.Square,
                                                 accum_out=bss[:, 0:1]).then_inc(S["bsq"], 1)
                            nc.scalar.activation(r[:, 384:640], pin[j][:, COL_CKV:COL_CKV + B_KVL], ACT.Square,
                                                 accum_out=bss[:, 1:2]).then_inc(S["bsq"], 1)

                        latent_squares()
                        square(0)
                        gate(0)
                        square(1)
                        hi(0)
                        act.wait_ge(S["bt"], done(t + 1))
                        act.wait_ge(S["bkv_ps"], done(t))
                        nc.scalar.activation(cT[:].rearrange("p k w -> p (k w)"), PT[0][:, 0:640], ACT.Copy).then_inc(S["bct"], 1)
                        gate(1)
                        act.wait_ge(S["bq_ps"], done(t + 1))
                        act.wait_ge(S["unrm"], done(NU * t + 2))
                        nc.scalar.activation(pin[j][:, 0:768].rearrange("p (a n) -> p a n", a=2),
                                             PT[1][:].rearrange("p (a n) -> p a n", a=2)[:, :, 0:384], ACT.Copy).then_inc(S["bq"], 1)
                        kv = PT[0][:].rearrange("p (h w) -> p h w", h=B_HEADS)
                        act.wait_ge(S["bkv_ps"], done(t + 1))
                        nc.scalar.activation(heads_of(5, j)[:, :, 0:64], kv[:, :, 0:64], ACT.Copy).then_inc(S["bkv"], 1)
                        nc.scalar.activation(pin[j][:, 1536:2048].rearrange("p (h w) -> p h w", h=B_HEADS), kv[:, :, 64:128],
                                             ACT.Copy).then_inc(S["bkv"], 1)
                        act.wait_ge(S["bkv"], done(2 * t + 2))
                        act.dma_start(tile_of(D["vb"], t), pin[j][:, 1536:2048]).then_inc(S["vst"], 16)
                        square(2)
                        ev(0)
                        store(t, 0)
                        hi(1)
                        gate(2)
                        hi(2)
                        ev(1)
                        store(t, 1)
                        square(3)
                        gate(3)
                        ev(2)
                        square(4)
                        store(t, 2)
                        hi(3)
                        gate(4)
                        ev(3)
                        store(t, 3)
                        hi(4)
                        square(5)
                        gate(5)
                        ev(4)
                        store(t, 4)
                        hi(5)
                        gate(6)
                        ev(5)
                        store(t, 5)
                        gate(7)

            @block.vector
            def _(dve):
                ch = Chain(dve, S["dve_own"])
                for n in ("var", "h", "ht_lo", "w_lo", "uvar", "unrm", "ulo", "uev1", "bvar", "bc", "rope"):
                    dve.sem_inc(S[n], CREDIT)
                dve.wait_ge(S["g_in"], 16)
                def normalise(t, j):
                    dve.wait_ge(S["ssq"], done(t + 1))
                    nc.vector.tensor_scalar(var[:, 0:1], ss[:, j:j + 1], 1.0 / DM, EPS, ALU.mult, ALU.add).then_inc(S["var"], 1)
                    dve.wait_ge(S["rstd"], done(t + 1))
                    dve.wait_ge(S["ht_ps"], done(t - 1))
                    nc.vector.scalar_tensor_tensor(out=h_t[j], in0=x_t[j], scalar=rs[:, 0:1], in1=g_t,
                                                   op0=ALU.mult, op1=ALU.mult).then_inc(S["h"], 1)

                def h_lo(t, j):
                    dve.wait_ge(S["ht_hi"], done(t + 1))
                    cols = bass.ds(t * P, P)
                    nc.vector.tensor_tensor(hT_lo[:, :, cols], PT[j][:].rearrange("p (k w) -> p k w", k=KT),
                                            hT_hi[:, :, cols].bitcast(F32), ALU.subtract).then_inc(S["ht_lo"], 1)

                normalise(0, 0)
                with dve.Fori(0, T // 2 - 1) as i:
                    normalise(2 * i + 1, 1)
                    h_lo(2 * i, 0)
                    normalise(2 * i + 2, 0)
                    h_lo(2 * i + 1, 1)

                def split(c, par, hs=(0, 1)):
                    for h in hs:
                        ks = slice(4 * h, 4 * h + 4)
                        dve.wait_ge(S[f"w_in{h}"], landed(c + 1))
                        dve.wait_ge(S["w_used"], done(c - 1))
                        ch.step(nc.vector.tensor_copy(w_hi[par][:, ks, :], w_raw[h][:]))
                        ch.wait()
                        nc.vector.tensor_tensor(w_lo[par][:, ks, :], w_raw[h][:], w_hi[par][:, ks, :].bitcast(F32),
                                                ALU.subtract).then_inc(S["w_lo"], 1)

                normalise(T - 1, 1)
                split(0, 0, (0,))
                h_lo(T - 2, 0)
                split(0, 0, (1,))
                h_lo(T - 1, 1)
                split(1, 1)
                with dve.Fori(1, NCH // 2) as i:
                    ch.enter(i - 1, 4)
                    for j in range(2):
                        split(2 * i + j, j)
                    ch.leave(NCH // 2 - 1, 4)

                dve.wait_ge(S["const_in"], 16 * 12)
                ch.step(nc.vector.tensor_copy(pos_f[:], pos_i[:]))
                ch.wait()
                ang, turns, part = (rot[:, a, :].rearrange("p (t f) -> p t f", f=16) for a in (0, 2, 3))
                ch.step(nc.vector.tensor_tensor(ang, pos_f[:].rearrange("p (t a) -> p t a", a=1).to_broadcast([P, T, 16]),
                                                inv[:].rearrange("p (a f) -> p a f", a=1).to_broadcast([P, T, 16]), ALU.mult))
                ch.wait()
                ch.step(nc.vector.tensor_scalar(turns, ang, 1.0 / TWO_PI, MAGIC, ALU.mult, ALU.add))
                ch.wait()
                ch.step(nc.vector.tensor_scalar(turns, turns, MAGIC, None, ALU.subtract))
                for c in TWO_PI_PARTS:
                    ch.wait()
                    ch.step(nc.vector.tensor_scalar(part, turns, c, None, ALU.mult))
                    ch.wait()
                    ch.step(nc.vector.tensor_tensor(ang, ang, part, ALU.subtract))
                ch.wait()
                ch.step(nc.vector.tensor_scalar(ang, ang, PI_IN, -PI_IN, ALU.min, ALU.max))
                ch.wait()
                quarter = rot[:, 1, :].rearrange("p (t f) -> p t f", f=16)
                ch.step(nc.vector.scalar_tensor_tensor(out=quarter, in0=ang, scalar=-1.0, in1=ang, op0=ALU.mult, op1=ALU.max))
                ch.wait()
                nc.vector.tensor_scalar(quarter, quarter, -1.0, TWO_PI / 4, ALU.mult, ALU.add).then_inc(S["angles"], 1)

                def prepare(t, i, j, more=True):

                    def stat(u):
                        name, _, G, W, _, q = UNITS[u]
                        dve.wait_ge(S["sq"], done(NU * t + u + 1))
                        dve.wait_ge(S["uvar"], done(NU * t + u))
                        ch.step(nc.vector.tensor_reduce(ss[:, 0:G], sqb[:, 0:G * W].rearrange("p (h w) -> p h w", h=G),
                                                        AX.X, ALU.add))
                        ch.wait()
                        f2 = B_QK if name == "b" and q else 1.0
                        op = nc.vector.tensor_scalar(var[:, 0:G], ss[:, 0:G], f2 / W, f2 * EPS, ALU.mult, ALU.add)
                        if name != "b" and q:
                            ch.step(op)
                            ch.wait()
                            op = nc.vector.tensor_tensor(var[:, 0:G], var[:, 0:G], inv_f2[:, 0 if name == "a" else 1, :], ALU.mult)
                        op.then_inc(S["uvar"], 1)

                    def scale(u):
                        _, _, G, W, gain, _ = UNITS[u]
                        v = n1[:, 0:G * W].rearrange("p (h w) -> p h w", h=G)
                        dve.wait_ge(S["urs"], done(NU * t + u + 1))
                        dve.wait_ge(S["ulo"], done(NU * t + u))
                        ch.step(nc.vector.tensor_tensor(v, heads_of(u, j), rs[:, 0:G].rearrange("p (h a) -> p h a", a=1)
                                                        .to_broadcast([P, G, W]), ALU.mult))
                        ch.wait()
                        nc.vector.tensor_tensor(v, v, gain.rearrange("p (a w) -> p a w", a=1).to_broadcast([P, G, W]),
                                                ALU.mult).then_inc(S["unrm"], 1)

                    def lo(u):
                        _, _, G, W, _, _ = UNITS[u]
                        dve.wait_ge(S["uhi"], done(NU * t + u + 1))
                        dve.wait_ge(S["unrm"], done(NU * t + u + 1))
                        hi_part, _ = part_of(u, 0)
                        dst, like = part_of(u, 1)
                        nc.vector.tensor_tensor(dst, like(n1[:, 0:G * W].rearrange("p (h w) -> p h w", h=G)), hi_part,
                                                ALU.subtract).then_inc(S["ulo"], 1)

                    def ev(u):
                        rows, half = block_w(u), n_blocks(u) // 2 * P
                        dve.wait_ge(S["utr"], done(NU * t + u + 1))
                        dve.wait_ge(S["ust"], landed(NU * t + u))
                        nc.vector.tensor_copy(turned[0:rows, half:2 * half], PT[1][0:rows, 0:half]).then_inc(S["uev1"], 1)

                    def rotate(x, heads):
                        dve.wait_ge(S["rope"], done(3 * t + (2 if heads == 1 else 0)))
                        sh = [P, heads, 16]
                        c, s = (a[:, bass.ds(t, 1), :].to_broadcast(sh) for a in (cos, sin))
                        prods = [rot[:, a, 0:heads * 16].rearrange("p (h f) -> p h f", f=16) for a in range(4)]
                        for dst, half, w in zip(prods, (0, 1, 0, 1), (c, s, s, c)):
                            ch.step(nc.vector.tensor_tensor(dst, x[:, :, 16 * half:16 * half + 16], w, ALU.mult))
                        ch.wait()
                        return prods

                    if j == 0:
                        dve.wait_ge(S["tables"], 2)
                    for a, n in enumerate((B_QL, B_KVL)):
                        dve.wait_ge(S["bsq"], done(2 * t + a + 1))
                        nc.vector.tensor_scalar(bvar[:, a:a + 1], bss[:, a:a + 1], 1.0 / n, EPS, ALU.mult, ALU.add)\
                          .then_inc(S["bvar"], 1)
                    dve.wait_ge(S["brs"], done(t + 1))
                    for a, (col, n) in enumerate(((COL_CQ, B_QL), (COL_CKV, B_KVL))):
                        v = pin[j][:, col:col + n]
                        nc.vector.scalar_tensor_tensor(out=v, in0=v, scalar=brs[:, a:a + 1], in1=gain_l[:, a * B_QL:a * B_QL + n],
                                                       op0=ALU.mult, op1=ALU.mult).then_inc(S["bc"], 1)
                    stat(0)
                    scale(0)
                    stat(1)
                    lo(0)
                    scale(1)
                    ev(0)
                    stat(2)
                    lo(1)
                    scale(2)
                    lo(2)
                    ev(1)
                    stat(3)
                    dve.wait_ge(S["bq"], done(t + 1))
                    xq = heads_of(4, j)[:, :, 64:96]
                    a, b, c, d = rotate(xq, 8)
                    nc.vector.tensor_tensor(xq[:, :, 0:16], a, b, ALU.subtract).then_inc(S["rope"], 1)
                    nc.vector.tensor_tensor(xq[:, :, 16:32], c, d, ALU.add).then_inc(S["rope"], 1)
                    scale(3)
                    ev(2)
                    stat(4)
                    lo(3)
                    kr = pin[j][:, COL_KR:COL_KR + 32].rearrange("p (a f) -> p a f", a=1)
                    a, b, c, d = rotate(kr, 1)
                    k32 = rot[:, 4, 0:32]
                    ch.step(nc.vector.tensor_tensor(k32[:, 0:16], a[:, 0, :], b[:, 0, :], ALU.subtract))
                    ch.step(nc.vector.tensor_tensor(k32[:, 16:32], c[:, 0, :], d[:, 0, :], ALU.add))
                    ch.wait()
                    nc.vector.tensor_copy(heads_of(5, j)[:, :, 64:96], k32.rearrange("p (a f) -> p a f", a=1)
                                          .to_broadcast([P, 8, 32])).then_inc(S["rope"], 1)
                    scale(4)
                    ev(3)
                    lo(4)
                    stat(5)
                    scale(5)
                    ev(4)
                    lo(5)
                    if more:
                        split(t + NCH + 1, 1 - j)
                    ev(5)

                split(NCH, 0)
                PREP = 26
                with dve.Fori(0, T // 2 - 1) as i:
                    ch.enter(i, 2 * PREP)
                    for j in range(2):
                        prepare(2 * i + j, i, j)
                    ch.leave(T // 2 - 1, 2 * PREP)
                prepare(T - 2, T // 2 - 1, 0)
                prepare(T - 1, T // 2 - 1, 1, more=False)

            @block.tensor
            def _(pe):
                for n in ("ht_ps", "w_used", "pg", "utr", "bt", "bq_ps", "bkv_ps"):
                    pe.sem_inc(S[n], CREDIT)
                pe.wait_ge(S["consts"], 3 + 2 * A_HEADS + C_HEADS)
                with pe.Fori(0, T // 2) as i:
                    for j in range(2):
                        t = 2 * i + j
                        pe.wait_ge(S["h"], done(t + 1))
                        pe.wait_ge(S["ht_lo"], done(t - 1))
                        for k in range(KT):
                            mm = nc.tensor.transpose(PT[j][:, k * P:(k + 1) * P], h_t[j][:, k * P:(k + 1) * P], ident[:])
                        mm.then_inc(S["ht_ps"], 1)

                def row_tile(c, par, m, W):
                    pe.wait_ge(S["p_out"], done(T * c + m - 3))
                    ms = slice(m * P, (m + 1) * P)
                    out = PG[m % 4][:, 0:W]
                    for k in range(KT):
                        nc.tensor.matmul(out, hT_hi[:, k, ms], w_hi[par][:, k, 0:W], start=(k == 0), stop=False)
                        nc.tensor.matmul(out, hT_hi[:, k, ms], w_lo[par][:, k, 0:W], start=False, stop=False)
                        mm = nc.tensor.matmul(out, hT_lo[:, k, ms], w_hi[par][:, k, 0:W], start=False, stop=(k == KT - 1))
                    mm.then_inc(S["pg"], 1)

                def chunk_done():
                    pe.drain().then_inc(S["w_used"], 1)

                pe.wait_ge(S["ht_lo"], done(T))
                with pe.Fori(0, NCH // 2) as i:
                    for j in range(2):
                        c = 2 * i + j
                        pe.wait_ge(S["w_lo"], done(2 * c + 2))
                        for m in range(T):
                            row_tile(c, j, m, W_MIX)
                        chunk_done()
                with pe.Fori(0, T // 2) as i:
                    for j in range(2):
                        t = 2 * i + j

                        def gate(m):
                            row_tile(t + NCH, j, m, W_GATE)

                        def turn(u):
                            rows, nb = block_w(u), n_blocks(u)
                            pe.wait_ge(S["ulo"], done(NU * t + u + 1))
                            pe.wait_ge(S["uhi"], done(NU * t + u + 1))
                            pe.wait_ge(S["uev0"], done(NU * t + u))
                            pe.wait_ge(S["uev1"], done(NU * t + u))
                            if u == 0:
                                pe.wait_ge(S["bq"], done(t + 1))
                                pe.wait_ge(S["bkv"], done(2 * t + 2))
                            for b in range(nb):
                                dst = PT[b // (nb // 2)][0:rows, b % (nb // 2) * P:(b % (nb // 2) + 1) * P]
                                mm = nc.tensor.transpose(dst, stage[:, b * rows:(b + 1) * rows], ident[:])
                            mm.then_inc(S["utr"], 1)

                        pe.wait_ge(S["w_lo"], done(2 * (t + NCH) + 2))
                        gate(0)
                        pe.wait_ge(S["bc"], done(2 * t + 2))
                        pe.wait_ge(S["uev0"], done(NU * t))
                        for k in range(5):
                            mm = nc.tensor.transpose(PT[0][:, k * P:(k + 1) * P], pin[j][:, COL_CQ + k * P:COL_CQ + (k + 1) * P], ident[:])
                        mm.then_inc(S["bt"], 1)
                        gate(1)
                        pe.wait_ge(S["bct"], done(t + 1))
                        pe.wait_ge(S["uev1"], done(NU * t))
                        for a in range(2):
                            for k in range(3):
                                mm = nc.tensor.matmul(PT[1][:, a * 512:a * 512 + 384], cT[:, k, :], wu[:, k, a * 384:(a + 1) * 384],
                                                      start=(k == 0), stop=(k == 2))
                        mm.then_inc(S["bq_ps"], 1)
                        for a in range(2):
                            for k in range(2):
                                mm = nc.tensor.matmul(PT[0][:, a * 512:(a + 1) * 512], cT[:, 3 + k, :], wkv[:, k, a * 512:(a + 1) * 512],
                                                      start=(k == 0), stop=(k == 1))
                        mm.then_inc(S["bkv_ps"], 1)
                        turn(0)
                        gate(2)
                        turn(1)
                        gate(3)
                        turn(2)
                        gate(4)
                        turn(3)
                        gate(5)
                        turn(4)
                        gate(6)
                        turn(5)
                        gate(7)
                        chunk_done()
        clear(nc, S.values())


NEG_BIG = -3.0e38


class Own:

    def __init__(self, eng, sem, base, per):
        self.eng, self.sem, self.base, self.per = eng, sem, base, per

    def at(self, n):
        self.now, self.k = n * self.per + self.base, 0

    def step(self, ins):
        ins.then_inc(self.sem, 1)
        self.k += 1

    def wait(self):
        assert self.k <= self.per
        self.eng.wait_ge(self.sem, self.now + self.k)

    def end(self, units):
        return self.base + units * self.per


def sweep(eng, parts, units, tiles, peel_last=False):
    def turn(t, before, now=True):
        for u in range(units):
            for lag, fn in parts:
                if u >= lag and now:
                    fn(t, u - lag)
                elif u < lag and before is not None:
                    fn(before, u - lag + units)
    turn(0, None)
    with eng.Fori(1, tiles - 1 if peel_last else tiles) as t:
        turn(t, t - 1)
    if peel_last:
        turn(tiles - 1, tiles - 2)
    turn(None, tiles - 1, now=False)


def attention(nc, ident, positions, lam_params, g_out, sink, D):
    with ExitStack() as st:
        def sb(name, shape, dt=F32):
            return st.enter_context(nc.sbuf_tensor(name, shape, dt))

        ka = sb("ka", [P, 2 * A_HEADS, SEQ], F32R)
        va = sb("va", [P, T, OUT_W], F32R)
        kb = sb("kb", [B_QK, 2 * B_HEADS, SEQ], F32R)
        vb = sb("vb", [P, T, OUT_W])
        kc = sb("kc", [P, C_KV, SEQ + 2 * WIN], F32R)
        vc = sb("vc", [P, T + 2, C_KV * C_DIM])
        q = sb("q", [P, 16 * P], F32R)
        scores = [sb(f"scores{i}", [P, SEQ]) for i in range(2)]
        e = [sb(f"e{i}", [P, SEQ]) for i in range(4)]
        pT = [sb(f"pT{i}", [P, SEQ]) for i in range(2)]
        dist = sb("dist", [P, SEQ])
        out = sb("out", [P, OUT_W])
        o4 = sb("o4", [P, OUT_W])
        pk_i = e[3][:].bitcast(I32)
        pos_i = sb("apos_i", [P, T], I32)
        neg_pos = sb("neg_pos", [P, T])
        lp = sb("lp", [P, 4, 64])
        lam2 = sb("lam2", [P, 2])
        lam = sb("lam", [P, 1])
        go = sb("go", [P, A_VDIM])
        small = sb("small", [P, 64])
        window = [sb(f"window{i}", [P, 3 * WIN]) for i in range(3)]
        sk = sb("sk", [P, C_HEADS])
        sk_s = sb("sk_s", [P, C_HEADS])
        slope = sb("slope", [P, C_HEADS])
        neg_half = sb("aneg_half", [P, 4])
        pos_k = sb("pos_k", [P, SEQ])
        fold = sb("fold", [P, B_VDIM])

        PS = [st.enter_context(nc.psum_tensor(f"PS{i}", [P, 1024], F32)) for i in range(2)]
        PT = st.enter_context(nc.psum_tensor("PTr", [P, 1024], F32))
        PO = [st.enter_context(nc.psum_tensor(f"PO{i}", [P, 512], F32)) for i in range(2)]

        def sems(prefix, names):
            return {n: st.enter_context(nc.semaphore(prefix + n)) for n in names.split()}
        L = sems("a_", "k_a0 k_a1 k_a2 k_a3 v_a k_b v_b k_c v_c pads half small_in consts pos lam ready gate dve act")
        A = sems("aa_", "q_in0 q_in1 q_in2 q_in3 s dist sub0 bias exp0 exp1 comb tr pt pv sq o var rs out sent")
        B = sems("ab_", "q_in0 q_in1 q_in2 q_in3 v_hi v_lo s bias exp tr pt lo pv sum back o sent0 sent1")
        C = sems("ac_", "q_in0 q_in1 q_in2 q_in3 s sub bias exp den tr pt pv o sent0 sent1 esk")
        U_A, U_B, U_C = A_HEADS, B_HEADS, C_HEADS

        qa = q[:, :].rearrange("p (h m s w) -> p h m s w", h=4, m=2, s=2)
        qb = q[:, :].rearrange("p (h s w) -> p h s w", h=8, s=2)
        vb_s = ka[:].rearrange("p t (h s w) -> p t h s w", h=B_HEADS, s=2)
        pT_s = [va[:, 4 * i:4 * i + 4, :].rearrange("p a w -> p (a w)").rearrange("p (b s w) -> p b s w", b=T, s=2) for i in range(2)]
        mx, nb, sm, rc, cc = (small[:, 8 * i:8 * i + 8] for i in range(5))
        ssq, var, rs = (small[:, 40 + 4 * i:44 + 4 * i] for i in range(3))

        c_scores = [[scores[0], scores[1], dist, pos_k][i // 2][:, 512 * (i % 2):512 * (i % 2) + 3 * WIN] for i in range(8)]

        o_sum = [o4[:, i * P:(i + 1) * P] for i in range(2)]

        with nc.Block() as block:
            @block.sync
            def _(sp):
                for Q in (A, B, C):
                    for i in range(4):
                        sp.sem_inc(Q[f"q_in{i}"], 16 * CREDIT)
                sp.sem_inc(A["sent"], 16 * CREDIT)
                for Q in (B, C):
                    for i in range(2):
                        sp.sem_inc(Q[f"sent{i}"], 16 * CREDIT)

                def load(sem, dst, src):
                    sp.dma_start(dst, src).then_inc(sem, 16)

                mix = D["mix"].rearrange("(t p) n -> p t n", p=P)

                def q_a(t, h):
                    sp.wait_ge(A["s"], done(U_A * (t - 1) + h + 1))
                    load(A[f"q_in{h}"], qa[:, h].bitcast(F32),
                         D["qa"][bass.ds(t, 1)].rearrange("a p (m h s w) -> (a p) h m s w", m=2, h=4, s=2)[:, h])

                def q_bc(X, src, rows, t, i, after=None):
                    if after is None:
                        sp.wait_ge(X["s"], done(U_B * (t - 1) + 2 * i + 2))
                    else:
                        sp.wait_ge(*after)
                    load(X[f"q_in{i}"], qb[0:rows, 2 * i:2 * i + 2].bitcast(F32),
                         src[bass.ds(t, 1)].rearrange("a p (h s w) -> (a p) h s w", h=8, s=2)[:, 2 * i:2 * i + 2])

                for h in range(U_A):
                    q_a(0, h)
                for h in range(U_A):
                    for m in range(2):
                        load(L[f"k_a{h}"], ka[:, m * A_HEADS + h, :].bitcast(F32), D["ka"][:, m * A_HEADS + h, :])
                    if h == 0:
                        sp.wait_ge(L["small_in"], 16 * 5)
                load(L["v_a"], va[:].bitcast(F32), mix[:, :, COL_VA:COL_VA + OUT_W])
                def send_a(t):
                    sp.wait_ge(A["out"], done(4 * t + 4))
                    sp.dma_start(tile_of(D["o"][:, 0:OUT_W], t), out[:]).then_inc(A["sent"], 16)
                for h in range(U_A):
                    q_a(1, h)
                vb_in = D["vb"].rearrange("(t p) n -> p t n", p=P)
                load(L["k_b"], kb[:, 2 * (T - 2):, :].bitcast(F32), D["kb"][:, 2 * (T - 2):, :])
                load(L["v_b"], vb[:, T - 2:, :], vb_in[:, T - 2:, :])
                load(L["k_c"], kc[:, :, WIN:WIN + SEQ].bitcast(F32), D["kc"])
                load(L["v_c"], vc[:, 1:T + 1, :], mix[:, :, COL_VC:COL_VC + C_KV * C_DIM])
                with sp.Fori(2, T) as t:
                    pair = bass.ds((t - 2) * 2, 2)
                    load(L["k_b"], kb[:, pair, :].bitcast(F32), D["kb"][:, pair, :])
                    load(L["v_b"], vb[:, bass.ds(t - 2, 1), :], vb_in[:, bass.ds(t - 2, 1), :])
                    q_a(t, 0)
                    q_a(t, 1)
                    q_a(t, 2)
                    send_a(t - 2)
                    q_a(t, 3)
                for i in range(4):
                    q_bc(B, D["qb"], B_QK, 0, i, (A["s"], done(U_A * (T - 1) + i + 1)))
                send_a(T - 2)
                send_a(T - 1)

                def send(X, col, t, half):
                    sp.wait_ge(X["o"], done(2 * t + half + 1) if X is C else done(U_B * t + 4 * half + 4))
                    sp.dma_start(tile_of(D["o"][:, col + 256 * half:col + 256 * half + 256], t),
                                 out[:, 256 * half:256 * half + 256]).then_inc(X[f"sent{half}"], 16)

                def b_turn(t, more=True):
                    def q_next(i):
                        if more:
                            q_bc(B, D["qb"], B_QK, t + 1, i)
                        else:
                            q_bc(C, D["qc"], P, 0, i, (B["s"], done(U_B * (T - 1) + 2 * i + 2)))
                    q_next(0)
                    if not isinstance(t, int) or t:
                        send(B, OUT_W, t - 1, 1)
                    q_next(1)
                    q_next(2)
                    send(B, OUT_W, t, 0)
                    q_next(3)
                b_turn(0)
                with sp.Fori(1, T - 1) as t:
                    b_turn(t)
                b_turn(T - 1, more=False)
                send(B, OUT_W, T - 1, 1)

                for i in range(4):
                    q_bc(C, D["qc"], P, 1, i)
                with sp.Fori(1, T - 1) as t:
                    q_bc(C, D["qc"], P, t + 1, 0)
                    q_bc(C, D["qc"], P, t + 1, 1)
                    send(C, 2 * OUT_W, t - 1, 0)
                    q_bc(C, D["qc"], P, t + 1, 2)
                    q_bc(C, D["qc"], P, t + 1, 3)
                    send(C, 2 * OUT_W, t - 1, 1)
                for t in (T - 2, T - 1):
                    for half in range(2):
                        send(C, 2 * OUT_W, t, half)
                sp.wait_ge(A["sent"], landed(T))
                for X in (B, C):
                    for i in range(2):
                        sp.wait_ge(X[f"sent{i}"], landed(T))

            @block.gpsimd
            def _(pool):
                pool.sem_inc(A["rs"], CREDIT)
                pool.dma_start(pk_i, bcast_rows(positions, SEQ)).then_inc(L["small_in"], 16)
                with nc.allow_non_contiguous_dma(reason="4 KB of positions, once"):
                    pool.dma_start(pos_i[:], positions.rearrange("(t p) -> p t", p=P)).then_inc(L["small_in"], 16)
                pool.dma_start(lp[:].rearrange("p a b -> p (a b)"), bcast_rows(lam_params.rearrange("a b -> (a b)"), 256)).then_inc(L["small_in"], 16)
                pool.dma_start(go[:], bcast_rows(g_out, A_VDIM)).then_inc(L["small_in"], 16)
                pool.dma_start(sk[:], bcast_rows(sink, C_HEADS)).then_inc(L["small_in"], 16)
                nc.gpsimd.memset(neg_half[:], -0.5).then_inc(L["consts"], 1)
                nc.gpsimd.memset(kc[:, :, 0:WIN].bitcast(F32), 0.0).then_inc(L["consts"], 1)
                nc.gpsimd.memset(kc[:, :, WIN + SEQ:].bitcast(F32), 0.0).then_inc(L["consts"], 1)
                nc.gpsimd.memset(vc[:, 0, :], 0.0).then_inc(L["consts"], 1)
                nc.gpsimd.memset(vc[:, T + 1, :], 0.0).then_inc(L["consts"], 1)
                for h in range(C_HEADS):
                    nc.gpsimd.memset(slope[:, h:h + 1], C_SLOPES[h]).then_inc(L["consts"], 1)
                n = 5 + C_HEADS
                nc.gpsimd.iota(window[0][:], [[1, 3 * WIN]], base=-WIN, channel_multiplier=-1,
                               allow_small_or_imprecise_dtypes=True).then_inc(L["consts"], 1)
                pool.wait_ge(L["dve"], 1)
                nc.gpsimd.affine_select(out=window[1][:], in_=window[1][:], compare_op=ALU.is_ge, fill=1e30, base=0,
                                        pattern=[[1, 3 * WIN]], channel_multiplier=-1).then_inc(L["consts"], 1)
                pool.wait_ge(L["consts"], n + 2)
                nc.gpsimd.affine_select(out=window[1][:], in_=window[1][:], compare_op=ALU.is_ge, fill=1e30, base=2 * WIN,
                                        pattern=[[-1, 3 * WIN]], channel_multiplier=1).then_inc(L["consts"], 1)
                pool.wait_ge(L["consts"], n + 3)
                nc.gpsimd.affine_select(out=window[0][:], in_=window[1][:], compare_op=ALU.is_ge, fill=1e30, base=-WIN,
                                        pattern=[[1, 3 * WIN]], channel_multiplier=0).then_inc(L["consts"], 1)
                nc.gpsimd.affine_select(out=window[2][:], in_=window[1][:], compare_op=ALU.is_ge, fill=1e30, base=2 * WIN - 1,
                                        pattern=[[-1, 3 * WIN]], channel_multiplier=0).then_inc(L["consts"], 1)
                with pool.Fori(0, T) as t:
                    pool.wait_ge(A["var"], done(t + 1))
                    nc.gpsimd.tensor_tensor(rs, var, neg_half[:], ALU.pow).then_inc(A["rs"], 1)

            @block.tensor
            def _(pe):
                for X in (A, B, C):
                    for n in ("s", "tr", "pv"):
                        pe.sem_inc(X[n], CREDIT)
                pe.sem_inc(B["back"], CREDIT)

                def s_a(t, h):
                    n = U_A * t + h
                    pe.wait_ge(A[f"q_in{h}"], landed(t + 1))
                    if isinstance(t, int):
                        pe.wait_ge(L[f"k_a{h}"], 32)
                    for m in range(2):
                        pe.wait_ge(A["sub0"], done(2 * n - 1 + m))
                        for half in range(2):
                            cols = slice(512 * half, 512 * half + 512)
                            for s in range(2):
                                mm = nc.tensor.matmul(PS[m][:, cols], qa[:, h, m, s, :], ka[:, m * A_HEADS + h, cols],
                                                      start=(s == 0), stop=(s == 1))
                    mm.then_inc(A["s"], 1)

                def turn(src, blocks, last):
                    for b in range(blocks):
                        mm = nc.tensor.transpose(PT[:, b * P:(b + 1) * P], src[:, b * P:(b + 1) * P], ident[:])
                    mm.then_inc(last, 1)

                def t_a(t, h):
                    n = U_A * t + h
                    pe.wait_ge(A["comb"], done(n + 1))
                    pe.wait_ge(A["pt"], done(n))
                    turn(e[2 * (h % 2)], T, A["tr"])

                def pv_a(t, h):
                    n = U_A * t + h
                    pe.wait_ge(A["pt"], done(n + 1))
                    if isinstance(t, int):
                        pe.wait_ge(L["v_a"], 16)
                    pe.wait_ge(A["o"], done(n - 1))
                    for b in range(T):
                        mm = nc.tensor.matmul(PO[h % 2][:, 0:P], pT[h % 2][:, b * P:(b + 1) * P], va[:, b, h * P:(h + 1) * P].bitcast(F32),
                                              start=(b == 0), stop=(b == T - 1))
                    mm.then_inc(A["pv"], 1)

                sweep(pe, [(0, s_a), (3, pv_a), (2, t_a)], U_A, T)

                def s_b(t, h):
                    n = U_B * t + h
                    pe.wait_ge(B[f"q_in{h // 2}"], landed(t + 1))
                    pe.wait_ge(B["exp"], done(n - 1))
                    for half in range(2):
                        cols = slice(512 * half, 512 * half + 512)
                        for i, (a, b) in enumerate(((0, 0), (0, 1), (1, 0))):
                            mm = nc.tensor.matmul(PS[h % 2][:, cols], qb[0:B_QK, h, a, :], kb[:, 2 * h + b, cols],
                                                  start=(i == 0), stop=(i == 2))
                    mm.then_inc(B["s"], 1)

                def t_b(t, h):
                    n = U_B * t + h
                    pe.wait_ge(B["exp"], done(n + 1))
                    pe.wait_ge(B["lo"], done(n))
                    turn(e[h % 4], T, B["tr"])

                def pv_b(t, h):
                    n = U_B * t + h
                    if isinstance(t, int):
                        pe.wait_ge(B["v_lo"], 1)
                    pe.wait_ge(B["lo"], done(n + 1))
                    pe.wait_ge(B["sum"], done(n - 1))
                    for b in range(T):
                        mm = nc.tensor.matmul(PO[h % 2][:, 0:2 * P], ka[:, b, h * P:(h + 1) * P],
                                              pT_s[h % 2][:, b, :, :].rearrange("p s w -> p (s w)"),
                                              start=(b == 0), stop=(b == T - 1), skip_group_check=True)
                    mm.then_inc(B["pv"], 1)

                def back_b(t, h):
                    n = U_B * t + h
                    pe.wait_ge(B["sum"], done(n + 1))
                    pe.wait_ge(B["o"], done(n - 1))
                    nc.tensor.matmul(PO[h % 2][:, 2 * P:2 * P + B_VDIM], o_sum[h % 2], fold[:], start=True, stop=True,
                                     skip_group_check=True).then_inc(B["back"], 1)

                pe.wait_ge(A["sub0"], done(2 * U_A * T))
                pe.wait_ge(A["pt"], done(U_A * T))
                pe.wait_ge(A["o"], done(U_A * T))
                pe.wait_ge(A["sq"], done(U_A * T))
                pe.wait_ge(L["k_b"], 16 * (T - 1))
                sweep(pe, [(0, s_b), (5, back_b), (4, pv_b), (2, t_b)], U_B, T)

                def s_c(t, h):
                    n = U_C * t + h
                    bank = PS[h % 4 // 2][:, 512 * (h % 2):512 * (h % 2) + 3 * WIN]
                    pe.wait_ge(C[f"q_in{h // 2}"], landed(t + 1))
                    pe.wait_ge(C["sub"], done(n - 3))
                    for s in range(2):
                        mm = nc.tensor.matmul(bank, qb[:, h, s, :], kc[:, h // (C_HEADS // C_KV), bass.ds(t * P, 3 * WIN)],
                                              start=(s == 0), stop=(s == 1))
                    mm.then_inc(C["s"], 1)

                def t_c(t, h):
                    n = U_C * t + h
                    pe.wait_ge(C["exp"], done(n + 1))
                    pe.wait_ge(C["pt"], done(n - 1))
                    for b in range(3):
                        mm = nc.tensor.transpose(PT[:, 512 * (h % 2) + b * P:512 * (h % 2) + (b + 1) * P],
                                                 e[h % 4][:, b * P:(b + 1) * P], ident[:])
                    mm.then_inc(C["tr"], 1)

                def pv_c(t, h):
                    n = U_C * t + h
                    g = h // 4
                    kv = h // (C_HEADS // C_KV)
                    pe.wait_ge(C["pt"], done(n + 1))
                    if h % 4 == 0:
                        pe.wait_ge(C["o"], done(2 * t + g - 1))
                    for b in range(3):
                        mm = nc.tensor.matmul(PO[g][:, (h % 4) * C_DIM:(h % 4 + 1) * C_DIM], pT[h % 2][:, b * P:(b + 1) * P],
                                              vc[:, bass.ds(t + b, 1), kv * C_DIM:(kv + 1) * C_DIM].rearrange("p a w -> p (a w)"),
                                              start=(b == 0), stop=(b == 2), skip_group_check=True)
                    mm.then_inc(C["pv"], 1)

                pe.wait_ge(B["exp"], done(U_B * T))
                pe.wait_ge(B["lo"], done(U_B * T))
                pe.wait_ge(B["o"], done(U_B * T))
                pe.wait_ge(L["k_c"], 16)
                pe.wait_ge(L["v_c"], 16)
                pe.wait_ge(L["consts"], 5 + C_HEADS + 5)
                sweep(pe, [(0, s_c), (8, pv_c), (6, t_c)], U_C, T)

            @block.scalar
            def _(act):
                for X, names in ((A, ("dist", "exp0", "exp1", "pt", "sq")), (B, ("exp", "pt")), (C, ("exp", "pt", "esk"))):
                    for n in names:
                        act.sem_inc(X[n], CREDIT)
                act.wait_ge(L["pos"], 1)
                nc.scalar.activation(dist[:], pos_k[:], ACT.Abs, bias=neg_pos[:, 0:1]).then_inc(A["dist"], 1)
                act.wait_ge(L["lam"], 1)
                nc.scalar.activation(lam2[:], small[:, 0:2], ACT.Exp).then_inc(L["act"], 1)
                act.wait_ge(L["ready"], 1)

                def dist_a(t, h):
                    if h < U_A - 1 or isinstance(t, int) and t == T - 1:
                        return
                    act.wait_ge(A["sub0"], done(2 * U_A * (t + 1)))
                    nc.scalar.activation(dist[:], pos_k[:], ACT.Abs, bias=neg_pos[:, bass.ds(t + 1, 1)]).then_inc(A["dist"], 1)

                def exp_a(t, h):
                    n = U_A * t + h
                    act.wait_ge(A["bias"], done(n + 1))
                    act.wait_ge(A["comb"], done(n - 1))
                    act.wait_ge(A["tr"], done(n - 1))
                    for m in range(2):
                        k = 2 * h + m
                        nc.scalar.activation(e[2 * (h % 2) + m][:], scores[m][:], ACT.Exp, bias=nb[:, k:k + 1],
                                             scale=A_SLOPES[h], accum_out=sm[:, k:k + 1]).then_inc(A[f"exp{m}"], 1)

                def pt(X, U, half=None):
                    def fn(t, h):
                        n = U * t + h
                        act.wait_ge(X["tr"], done(n + 1))
                        act.wait_ge(X["pv"], done(n - 1))
                        nc.scalar.activation(pT[h % 2][:], PT[:], ACT.Copy).then_inc(X["pt"], 1)
                    return fn

                def sq_a(t, h):
                    n = U_A * t + h
                    act.wait_ge(A["pv"], done(n + 1))
                    act.wait_ge(A["o"], done(n + 1))
                    act.wait_ge(A["var"], done(t))
                    act.wait_ge(A["sq"], done(n))
                    nc.scalar.activation(dist_junk, o4[:, h * P:(h + 1) * P], ACT.Square, accum_out=ssq[:, h:h + 1]).then_inc(A["sq"], 1)

                dist_junk = lp[:].rearrange("p a b -> p (a b)")[:, 0:P]
                sweep(act, [(2, pt(A, U_A)), (0, exp_a), (0, dist_a), (3, sq_a)], U_A, T, peel_last=True)

                def exp_b(t, h):
                    n = U_B * t + h
                    act.wait_ge(B["bias"], done(n + 1))
                    act.wait_ge(B["tr"], done(n - 3))
                    act.wait_ge(B["o"], done(n - 7) if not isinstance(t, int) or t else 1)
                    nc.scalar.activation(e[h % 4][:], PS[h % 2][:], ACT.Exp, bias=nb[:, h:h + 1],
                                         accum_out=sm[:, h:h + 1]).then_inc(B["exp"], 1)
                act.wait_ge(A["tr"], done(U_A * T))
                act.wait_ge(A["pv"], done(U_A * T))

                def hi_b(t, h):
                    n = U_B * t + h
                    act.wait_ge(B["tr"], done(n + 1))
                    act.wait_ge(B["pv"], done(n - 1))
                    nc.scalar.activation(pT_s[h % 2][:, :, 0, :], PT[:].rearrange("p (b w) -> p b w", b=T), ACT.Copy).then_inc(B["pt"], 1)

                act.wait_ge(A["s"], done(U_A * T))
                act.wait_ge(L["v_b"], 16 * (T - 1))
                nc.scalar.activation(vb_s[:, :, :, 0, :], vb[:].rearrange("p t (h w) -> p t h w", h=B_HEADS), ACT.Copy)\
                  .then_inc(B["v_hi"], 1)
                sweep(act, [(2, hi_b), (0, exp_b)], U_B, T)

                def exp_c(t, h):
                    n = U_C * t + h
                    g = h // 4
                    if h % 4 == 0:
                        act.wait_ge(C["bias"], done(2 * t + g + 1))
                        act.wait_ge(C["o"], done(2 * t + g - 1))
                    act.wait_ge(C["tr"], done(n - 3))
                    nc.scalar.activation(e[h % 4][:, 0:3 * WIN], c_scores[h], ACT.Exp, bias=nb[:, h:h + 1], scale=C_SLOPES[h],
                                         accum_out=sm[:, h:h + 1]).then_inc(C["exp"], 1)
                    if h % 4 == 3:
                        nc.scalar.activation(cc[:, 4 * g:4 * g + 4], mx[:, 4 * g:4 * g + 4], ACT.Exp).then_inc(C["esk"], 1)

                def pt_c(t, h):
                    n = U_C * t + h
                    act.wait_ge(C["tr"], done(n + 1))
                    act.wait_ge(C["pv"], done(n - 1))
                    nc.scalar.activation(pT[h % 2][:, 0:3 * WIN], PT[:, 512 * (h % 2):512 * (h % 2) + 3 * WIN], ACT.Copy).then_inc(C["pt"], 1)
                act.wait_ge(B["tr"], done(U_B * T))
                act.wait_ge(B["pv"], done(U_B * T))
                sweep(act, [(6, pt_c), (4, exp_c)], U_C, T)

            @block.vector
            def _(dve):
                ch = Chain(dve, L["dve"])
                for X, names in ((A, ("sub0", "bias", "comb", "o", "var", "out")), (B, ("bias", "lo", "sum", "o")), (C, ("sub", "bias", "den", "o"))):
                    for n in names:
                        dve.sem_inc(X[n], CREDIT)
                dve.wait_ge(L["consts"], 6 + C_HEADS)
                ch.step(nc.vector.scalar_tensor_tensor(out=window[1][:], in0=window[0][:], scalar=-1.0, in1=window[0][:],
                                                       op0=ALU.mult, op1=ALU.max))
                dve.wait_ge(L["small_in"], 16 * 5)
                ch.step(nc.vector.tensor_copy(pos_k[:], pk_i))
                ch.step(nc.vector.tensor_copy(neg_pos[:], pos_i[:]))
                ch.step(nc.vector.tensor_tensor(lp[:, 0, :], lp[:, 0, :], lp[:, 1, :], ALU.mult))
                ch.step(nc.vector.tensor_tensor(lp[:, 2, :], lp[:, 2, :], lp[:, 3, :], ALU.mult))
                ch.wait()
                nc.vector.tensor_scalar(neg_pos[:], neg_pos[:], -1.0, None, ALU.mult).then_inc(L["pos"], 1)
                for a in range(2):
                    ch.step(nc.vector.tensor_reduce(small[:, a:a + 1], lp[:, 2 * a, :], AX.X, ALU.add))
                ch.wait()
                nc.vector.tensor_copy(lp[:, 1, 0:1], small[:, 0:1]).then_inc(L["lam"], 1)
                ch.step(nc.vector.tensor_scalar(go[:], go[:], 1.0 - LAM_INIT, None, ALU.mult))
                ch.step(nc.vector.tensor_copy(sk_s[:], sk[:]))
                ch.wait()
                for h in range(C_HEADS):
                    ch.step(nc.vector.tensor_scalar(sk_s[:, h:h + 1], sk[:, h:h + 1], 1.0 / C_SLOPES[h], None, ALU.mult))
                dve.wait_ge(L["act"], 1)
                dve.wait_ge(L["lam"], 1)
                nc.vector.tensor_tensor(fold[:], ident[:, 0:B_VDIM], ident[:, B_VDIM:], ALU.add)
                ch.step(nc.vector.tensor_tensor(lam[:], lam2[:, 1:2], lam2[:, 0:1], ALU.subtract))
                ch.wait()
                ch.step(nc.vector.tensor_scalar(lam[:], lam[:], LAM_INIT, None, ALU.subtract))
                ch.wait()
                nc.vector.tensor_copy(lp[:, 1, 1:2], lam[:]).then_inc(L["ready"], 1)

                def sub_a(t, h):
                    n = U_A * t + h
                    k = 2 * h
                    for m in range(2):
                        if m == 0:
                            dve.wait_ge(A["s"], done(n + 1))
                            dve.wait_ge(A["dist"], done(t + 1))
                            dve.wait_ge(A["bias"], done(n))
                        dve.wait_ge(A[f"exp{m}"], done(n))
                        dve.sem_inc(L["gate"], 1)
                        nc.vector.tensor_tensor_reduce(scores[m][:], PS[m][:], dist[:], 1.0, NEG_BIG, ALU.subtract, ALU.max,
                                                       mx[:, k + m:k + m + 1]).then_inc(A["sub0"], 1)
                    dve.wait_ge(A["sub0"], done(2 * n + 2))
                    nc.vector.tensor_scalar(nb[:, k:k + 2], mx[:, k:k + 2], -A_SLOPES[h], None, ALU.mult).then_inc(A["bias"], 1)

                def comb_a(t, h):
                    n = U_A * t + h
                    k = 2 * h
                    dve.wait_ge(A["exp0"], done(n + 1))
                    dve.wait_ge(A["exp1"], done(n + 1))
                    dve.wait_ge(A["o"], done(n - 3))
                    dve.wait_ge(A["comb"], done(n))
                    ops.step(nc.vector.reciprocal(rc[:, k:k + 2], sm[:, k:k + 2]))
                    ops.wait()
                    ops.step(nc.vector.scalar_tensor_tensor(out=cc[:, k:k + 1], in0=sm[:, k:k + 1], scalar=rc[:, k + 1:k + 2], in1=lam[:],
                                                            op0=ALU.mult, op1=ALU.mult))
                    ops.wait()
                    e0, e1 = e[2 * (h % 2)], e[2 * (h % 2) + 1]
                    nc.vector.scalar_tensor_tensor(out=e0[:], in0=e1[:], scalar=cc[:, k:k + 1], in1=e0[:],
                                                   op0=ALU.mult, op1=ALU.add).then_inc(A["comb"], 1)

                def o_a(t, h):
                    n = U_A * t + h
                    k = 2 * h
                    dve.wait_ge(A["pv"], done(n + 1))
                    dve.wait_ge(A["out"], done(4 * t))
                    nc.vector.tensor_scalar(o4[:, h * P:(h + 1) * P], PO[h % 2][:, 0:P], rc[:, k:k + 1], None, ALU.mult)\
                      .then_inc(A["o"], 1)

                def norm_a(t, h):
                    if h < U_A - 1:
                        return
                    dve.wait_ge(A["sq"], done(U_A * t + U_A))
                    dve.wait_ge(A["out"], done(4 * t))
                    nc.vector.tensor_scalar(var, ssq, 1.0 / A_VDIM, EPS, ALU.mult, ALU.add).then_inc(A["var"], 1)

                def out_a(t, h):
                    if h < U_A - 1:
                        return
                    dve.wait_ge(A["rs"], done(t + 1))
                    dve.wait_ge(A["sent"], landed(t))
                    for i in range(A_HEADS):
                        v = slice(i * P, (i + 1) * P)
                        nc.vector.scalar_tensor_tensor(out=out[:, v], in0=o4[:, v], scalar=rs[:, i:i + 1], in1=go[:],
                                                       op0=ALU.mult, op1=ALU.mult).then_inc(A["out"], 1)

                own = Own(dve, L["dve"], ch.k, 2)
                ops = own

                def comb(t, h):
                    own.at(U_A * t + h)
                    comb_a(t, h)
                sweep(dve, [(0, sub_a), (1, comb), (4, out_a), (3, o_a), (3, norm_a)], U_A, T)
                base = own.end(U_A * T)

                def max_b(t, h):
                    n = U_B * t + h
                    dve.wait_ge(B["s"], done(n + 1))
                    dve.wait_ge(B["exp"], done(n - 3))
                    own.at(n)
                    own.step(nc.vector.tensor_reduce(mx[:, h:h + 1], PS[h % 2][:], AX.X, ALU.max))
                    own.wait()
                    nc.vector.tensor_scalar(nb[:, h:h + 1], mx[:, h:h + 1], -1.0, None, ALU.mult).then_inc(B["bias"], 1)

                def o_b(t, h):
                    n = U_B * t + h
                    dve.wait_ge(B["back"], done(n + 1))
                    dve.wait_ge(B["o"], done(n))
                    nc.vector.reciprocal(rc[:, h:h + 1], sm[:, h:h + 1]).then_inc(L["pads"], 1)
                    dve.wait_ge(L["pads"], n + 1)
                    if h % 4 == 0:
                        dve.wait_ge(B[f"sent{h // 4}"], landed(t))
                    nc.vector.tensor_scalar(out[:, h * B_VDIM:(h + 1) * B_VDIM], PO[h % 2][:, 2 * P:2 * P + B_VDIM], rc[:, h:h + 1],
                                            None, ALU.mult).then_inc(B["o"], 1)

                def sum_b(t, h):
                    n = U_B * t + h
                    dve.wait_ge(B["pv"], done(n + 1))
                    dve.wait_ge(B["back"], done(n - 1))
                    nc.vector.tensor_copy(o_sum[h % 2], PO[h % 2][:, 0:P]).then_inc(L["half"], 1)
                    dve.wait_ge(L["half"], n + 1)
                    nc.vector.tensor_tensor(o_sum[h % 2], PO[h % 2][:, P:2 * P], o_sum[h % 2], ALU.add).then_inc(B["sum"], 1)

                def lo_b(t, h):
                    n = U_B * t + h
                    dve.wait_ge(B["pt"], done(n + 1))
                    nc.vector.tensor_tensor(pT_s[h % 2][:, :, 1, :], PT[:].rearrange("p (b w) -> p b w", b=T),
                                            pT_s[h % 2][:, :, 0, :].bitcast(F32), ALU.subtract).then_inc(B["lo"], 1)
                own = Own(dve, L["dve"], base, 1)
                dve.wait_ge(A["sent"], landed(T))
                dve.wait_ge(A["bias"], done(U_A * T))
                dve.wait_ge(B["v_hi"], 1)
                nc.vector.tensor_tensor(vb_s[:, :, :, 1, :], vb[:].rearrange("p t (h w) -> p t h w", h=B_HEADS),
                                        vb_s[:, :, :, 0, :].bitcast(F32), ALU.subtract).then_inc(B["v_lo"], 1)
                sweep(dve, [(0, max_b), (5, o_b), (4, sum_b), (2, lo_b)], U_B, T)
                base = own.end(U_B * T)

                def sub_c(t, h):
                    n = U_C * t + h
                    g = h // 4
                    win = window[0 if isinstance(t, int) and t == 0 else 2 if isinstance(t, int) else 1]
                    dve.wait_ge(C["s"], done(n + 1))
                    if not isinstance(t, int) or t:
                        dve.wait_ge(C["exp"], done(n - 7))
                    if h % 4 == 0:
                        dve.wait_ge(C["esk"], done(2 * t + g - 1))
                    dve.sem_inc(L["gate"], 1)
                    nc.vector.tensor_tensor_reduce(c_scores[h], PS[h % 4 // 2][:, 512 * (h % 2):512 * (h % 2) + 3 * WIN], win[:], 1.0,
                                                   NEG_BIG, ALU.subtract, ALU.max, mx[:, h:h + 1]).then_inc(C["sub"], 1)
                    if h % 4 == 3:
                        v = slice(4 * g, 4 * g + 4)
                        own.at(2 * t + g)
                        dve.wait_ge(C["sub"], done(n + 1))
                        own.step(nc.vector.tensor_tensor(mx[:, v], mx[:, v], sk_s[:, v], ALU.max))
                        own.wait()
                        own.step(nc.vector.scalar_tensor_tensor(out=nb[:, v], in0=mx[:, v], scalar=-1.0, in1=slope[:, v],
                                                                op0=ALU.mult, op1=ALU.mult))
                        own.wait()
                        nc.vector.tensor_tensor(mx[:, v], nb[:, v], sk[:, v], ALU.add).then_inc(C["bias"], 1)

                def o_c(t, h):
                    if h % 4 < 3:
                        return
                    n = U_C * t + h
                    g = h // 4
                    v = slice(4 * g, 4 * g + 4)
                    dve.wait_ge(C["pv"], done(n + 1))
                    dve.wait_ge(C["esk"], done(2 * t + g + 1))
                    dve.wait_ge(C["o"], done(2 * t + g))
                    nc.vector.tensor_tensor(rc[:, v], sm[:, v], cc[:, v], ALU.add).then_inc(C["den"], 1)
                    dve.wait_ge(C["den"], done(4 * t + 2 * g + 1))
                    nc.vector.reciprocal(rc[:, v], rc[:, v]).then_inc(C["den"], 1)
                    dve.wait_ge(C["den"], done(4 * t + 2 * g + 2))
                    dve.wait_ge(C[f"sent{g}"], landed(t))
                    nc.vector.tensor_tensor(out[:, 256 * g:256 * g + 256].rearrange("p (h w) -> p h w", h=4),
                                            PO[g][:, 0:256].rearrange("p (h w) -> p h w", h=4),
                                            rc[:, v].rearrange("p (h a) -> p h a", a=1).to_broadcast([P, 4, C_DIM]), ALU.mult)\
                      .then_inc(C["o"], 1)
                own = Own(dve, L["dve"], base, 2)
                for i in range(2):
                    dve.wait_ge(B[f"sent{i}"], landed(T))
                dve.wait_ge(B["exp"], done(U_B * T))
                dve.wait_ge(B["o"], done(U_B * T))
                dve.wait_ge(L["consts"], 5 + C_HEADS + 5)
                sweep(dve, [(0, sub_c), (8, o_c)], U_C, T, peel_last=True)
        clear(nc, [s for group in (L, A, B, C) for s in group.values()])


def merge(nc, ident, x, w_branch, w_o, g_ffn, w_router, x2_out, aff, D):
    OK = OUT_W // P
    NB = len(w_branch)
    with ExitStack() as st:
        def sb(name, shape, dt=F32):
            return st.enter_context(nc.sbuf_tensor(name, shape, dt))

        NW = NB * OK + KT
        w_hi = sb("mw_hi", [P, NW, DM], F32R)
        w_lo = sb("mw_lo", [P, NW, DM], F32R)
        o_in = sb("o_in", [P, NB * OUT_W])
        sig = [sb(f"msig{i}", [P, 512]) for i in range(3)]
        oT_hi = [sb(f"oT_hi{b}", [P, OK * P], F32R) for b in range(NB)]
        oT_lo = [sb(f"oT_lo{b}", [P, OK * P], F32R) for b in range(NB)]
        merged = sb("merged", [P, DM])
        mT_hi = sb("mT_hi", [P, DM], F32R)
        mT_lo = sb("mT_lo", [P, DM], F32R)
        x2 = sb("x2", [P, DM])
        hT = sb("hT", [P, DM])
        wr = sb("wr", [P, KT, N_EXP])
        gT = sb("gT", [P, KT])
        few = sb("few", [P, 8])
        ex = sb("ex", [P, N_EXP])
        neg_half = sb("mneg_half", [P, 1])
        ssq, var, rs, top, neg, den, rden = (few[:, i:i + 1] for i in range(7))

        BR = [st.enter_context(nc.psum_tensor(f"BR{i}", [P, 512], F32)) for i in range(2)]
        WO = [st.enter_context(nc.psum_tensor(f"WO{i}", [P, 512], F32)) for i in range(2)]
        OT = st.enter_context(nc.psum_tensor("OT", [P, 512], F32))
        MT = [st.enter_context(nc.psum_tensor(f"MT{i}", [P, 512], F32)) for i in range(2)]
        RT = st.enter_context(nc.psum_tensor("RT", [P, 512], F32))

        S = {n: st.enter_context(nc.semaphore("m_" + n)) for n in
             "small consts w_in0 w_in1 w_in2 w_in3 w_in4 w_hi w_lo o_in sig0 sig1 sig2 x_in o_tr oT_hi oT_lo br mul mrg m_tr mT_hi mT_lo wo x2 "
             "out_sent sq var rs h2 h2_sent h_tr hT rt bias exp den aff".split()}
        NBR = NB * OK

        def stage_of(i):
            return ((merged, x2, hT)[i % 3], S[f"w_in{i % 3}"], i // 3 + 1) if i < NBR else \
                   ((x2, hT)[i % 2], S[f"w_in{3 + i % 2}"], (i - NBR) // 2 + 1)

        halves = [slice(512 * h, 512 * h + 512) for h in range(2)]
        OB = [OT, MT[1], OT]

        def w_rows(i):
            if i < NB * OK:
                return w_branch[i // OK][(i % OK) * P:(i % OK + 1) * P, :]
            i -= NB * OK
            return w_o[i * P:(i + 1) * P, :]

        with nc.Block() as block:
            def over_tiles(eng, turn):
                turn(0, None, True)
                with eng.Fori(1, T - 1) as t:
                    turn(t, t - 1, True)
                turn(T - 1, T - 2, False)
                turn(None, T - 1, False)

            @block.sync
            def _(sp):
                for n in ("o_in", "sig0", "sig1", "sig2", "x_in", "out_sent", "h2_sent"):
                    sp.sem_inc(S[n], 16 * CREDIT)
                sp.dma_start(wr[:], w_router.rearrange("(k p) n -> p k n", p=P)).then_inc(S["small"], 16)
                with nc.allow_non_contiguous_dma(reason="4 KB of gains, once"):
                    sp.dma_start(gT[:], g_ffn.rearrange("(k p) -> p k", p=P)).then_inc(S["small"], 16)

                def load_sig(t, i):
                    sp.wait_ge(S["mrg"], done(6 * t + i - 2))
                    sp.dma_start(sig[i % 3][:], tile_of(D["sig"][:, 512 * i:512 * i + 512], t)).then_inc(S[f"sig{i % 3}"], 16)

                def load_o(t):
                    sp.wait_ge(S["o_tr"], done(NB * t))
                    sp.dma_start(o_in[:], tile_of(D["o"], t)).then_inc(S["o_in"], 16)

                load_o(0)
                for i in range(NW):
                    if i >= 3:
                        sp.wait_ge(S["w_lo"], i - 2 if i < NBR else i - 1)
                    buffer, landed_in, _ = stage_of(i)
                    sp.dma_start(buffer[:], w_rows(i)).then_inc(landed_in, 16)
                    if i == OK:
                        for k in range(3):
                            load_sig(0, k)

                def turn(t, b, more=True):
                    if t is not None:
                        load_sig(t, 3)
                        load_sig(t, 4)
                    if more:
                        load_o(t + 1)
                    if b is not None:
                        sp.wait_ge(S["x2"], done(2 * b + 2))
                        sp.dma_start(tile_of(x2_out, b), x2[:]).then_inc(S["out_sent"], 16)
                    if t is not None:
                        load_sig(t, 5)
                    if more:
                        load_sig(t + 1, 0)
                    if b is not None:
                        sp.wait_ge(S["h2"], done(b + 1))
                        sp.dma_start(tile_of(D["h2"], b), x2[:]).then_inc(S["h2_sent"], 16)
                    if t is not None:
                        sp.wait_ge(S["h2_sent"], landed(t))
                        sp.wait_ge(S["h_tr"], done(2 * t))
                        if isinstance(t, int) and t == 0:
                            sp.wait_ge(S["w_lo"], NW)
                        sp.dma_start(x2[:], tile_of(x, t)).then_inc(S["x_in"], 16)
                    if more:
                        load_sig(t + 1, 1)
                        load_sig(t + 1, 2)
                turn(0, None)
                with sp.Fori(1, T - 1) as t:
                    turn(t, t - 1)
                turn(T - 1, T - 2, more=False)
                turn(None, T - 1, more=False)
                sp.wait_ge(S["out_sent"], landed(T))
                sp.wait_ge(S["h2_sent"], landed(T))

            @block.gpsimd
            def _(pool):
                pool.sem_inc(S["rs"], CREDIT)
                nc.gpsimd.memset(neg_half[:], -0.5).then_inc(S["consts"], 1)
                pool.wait_ge(S["consts"], 1)
                with pool.Fori(0, T) as t:
                    pool.wait_ge(S["var"], done(t + 1))
                    nc.gpsimd.tensor_tensor(rs, var, neg_half[:], ALU.pow).then_inc(S["rs"], 1)

            @block.tensor
            def _(pe):
                for n in ("o_tr", "br", "m_tr", "wo", "h_tr", "rt"):
                    pe.sem_inc(S[n], CREDIT)

                def flip(bank, src, at):
                    for k in range(4):
                        mm = nc.tensor.transpose(bank[:, k * P:(k + 1) * P], src[:, at + k * P:at + (k + 1) * P], ident[:])
                    return mm

                def turn_o(t, b):
                    if b == 0:
                        pe.wait_ge(S["o_in"], landed(t + 1))
                    if b == 1:
                        pe.wait_ge(S["hT"], done(2 * t - 2))
                    else:
                        pe.wait_ge(S["oT_lo"], done(NB * t + b - 1))
                    flip(OB[b], o_in, b * OUT_W).then_inc(S["o_tr"], 1)

                def branch(t, b, h):
                    if isinstance(t, int):
                        pe.wait_ge(S["w_lo"], OK * (b + 1))
                    pe.wait_ge(S["oT_lo"], done(NB * t + b + 1))
                    pe.wait_ge(S["mrg"], done(6 * t + 2 * b + h - 1))
                    n = 0
                    for k in range(OK):
                        at = slice(k * P, (k + 1) * P)
                        for l, r in ((oT_hi, w_hi), (oT_hi, w_lo), (oT_lo, w_hi)):
                            mm = nc.tensor.matmul(BR[h][:], l[b][:, at], r[:, b * OK + k, halves[h]],
                                                  start=(n == 0), stop=(n == 3 * OK - 1))
                            n += 1
                    mm.then_inc(S["br"], 1)

                def turn_m(t, now):
                    pe.wait_ge(S["oT_lo"], done(NB * t + NB + (2 if now else 0)))
                    pe.wait_ge(S["mrg"], done(6 * t + 6))
                    pe.wait_ge(S["hT"], done(2 * t))
                    for g in range(2):
                        flip(MT[g], merged, 512 * g).then_inc(S["m_tr"], 1)

                def w_out(t):
                    pe.wait_ge(S["w_lo"], NW)
                    pe.wait_ge(S["mT_lo"], done(2 * t + 2))
                    for h in range(2):
                        pe.wait_ge(S["x2"], done(2 * t + h - 1))
                        n = 0
                        for k in range(KT):
                            at = slice(k * P, (k + 1) * P)
                            for l, r in ((mT_hi, w_hi), (mT_hi, w_lo), (mT_lo, w_hi)):
                                mm = nc.tensor.matmul(WO[h][:], l[:, at], r[:, NB * OK + k, halves[h]],
                                                      start=(n == 0), stop=(n == 3 * KT - 1))
                                n += 1
                        mm.then_inc(S["wo"], 1)

                def turn_h(t):
                    pe.wait_ge(S["h2"], done(t + 1))
                    pe.wait_ge(S["mT_lo"], done(2 * t + 2))
                    for g in range(2):
                        flip(MT[g], x2, 512 * g).then_inc(S["h_tr"], 1)

                def router(t):
                    pe.wait_ge(S["hT"], done(2 * t + 2))
                    pe.wait_ge(S["exp"], done(t))
                    for k in range(KT):
                        mm = nc.tensor.matmul(RT[:, 0:N_EXP], hT[:, k * P:(k + 1) * P], wr[:, k, :], start=(k == 0), stop=(k == KT - 1))
                    mm.then_inc(S["rt"], 1)

                def turn(t, before, more):
                    now, last = t is not None, before is not None
                    if now and not last:
                        turn_o(t, 0)
                        turn_o(t, 1)
                    if now:
                        branch(t, 0, 0)
                    if last:
                        turn_m(before, now)
                    if now:
                        branch(t, 0, 1)
                        turn_o(t, 2)
                    if last:
                        w_out(before)
                    if now:
                        branch(t, 1, 0)
                        branch(t, 1, 1)
                        branch(t, 2, 0)
                    if last:
                        turn_h(before)
                    if now:
                        branch(t, 2, 1)
                    if more:
                        turn_o(t + 1, 0)
                        turn_o(t + 1, 1)
                    if last:
                        router(before)
                pe.wait_ge(S["small"], 32)
                over_tiles(pe, turn)

            @block.scalar
            def _(act):
                for n in ("oT_hi", "mT_hi", "sq", "exp"):
                    act.sem_inc(S[n], CREDIT)

                def w_hi_of(a, b):
                    for i in range(a, b):
                        buffer, landed_in, n = stage_of(i)
                        act.wait_ge(landed_in, 16 * n)
                        nc.scalar.activation(w_hi[:, i, :], buffer[:], ACT.Copy).then_inc(S["w_hi"], 1)

                def hi_o(t, b):
                    act.wait_ge(S["o_tr"], done(NB * t + b + 1))
                    act.wait_ge(S["br"], done(6 * t + 2 * b - 4) if not isinstance(t, int) or t else 1)
                    nc.scalar.activation(oT_hi[b][:], OB[b][:], ACT.Copy).then_inc(S["oT_hi"], 1)

                def hi_m(t):
                    for g in range(2):
                        act.wait_ge(S["m_tr"], done(2 * t + g + 1))
                        act.wait_ge(S["wo"], done(2 * t))
                        nc.scalar.activation(mT_hi[:, halves[g]], MT[g][:], ACT.Copy).then_inc(S["mT_hi"], 1)

                def turn(t, before, more):
                    now, last = t is not None, before is not None
                    first = not last
                    if first:
                        w_hi_of(0, OK)
                        hi_o(t, 0)
                        w_hi_of(OK, 2 * OK)
                        hi_o(t, 1)
                        w_hi_of(2 * OK, NBR + KT // 2)
                    if last:
                        hi_m(before)
                    if now:
                        hi_o(t, 2)
                    if first:
                        w_hi_of(NBR + KT // 2, NW)
                    if last:
                        act.wait_ge(S["w_lo"], NW)
                        act.wait_ge(S["x2"], done(2 * before + 2))
                        act.wait_ge(S["rt"], done(before))
                        act.wait_ge(S["var"], done(before))
                        nc.scalar.activation(hT[:], x2[:], ACT.Square, accum_out=ssq).then_inc(S["sq"], 1)
                    if more:
                        hi_o(t + 1, 0)
                        hi_o(t + 1, 1)
                    if last:
                        act.wait_ge(S["bias"], done(before + 1))
                        act.wait_ge(S["aff"], done(before))
                        nc.scalar.activation(ex[:], RT[:, 0:N_EXP], ACT.Exp, bias=neg, accum_out=den).then_inc(S["exp"], 1)
                over_tiles(act, turn)

            @block.vector
            def _(dve):
                for n in ("oT_lo", "mul", "mrg", "mT_lo", "x2", "var", "h2", "hT", "bias", "den", "aff"):
                    dve.sem_inc(S[n], CREDIT)
                dve.wait_ge(S["small"], 32)

                def w_lo_of(a, b):
                    for i in range(a, b):
                        dve.wait_ge(S["w_hi"], i + 1)
                        nc.vector.tensor_tensor(w_lo[:, i, :], stage_of(i)[0][:], w_hi[:, i, :].bitcast(F32), ALU.subtract)\
                          .then_inc(S["w_lo"], 1)

                def lo_o(t, b):
                    dve.wait_ge(S["oT_hi"], done(NB * t + b + 1))
                    nc.vector.tensor_tensor(oT_lo[b][:], OB[b][:], oT_hi[b][:].bitcast(F32), ALU.subtract).then_inc(S["oT_lo"], 1)

                def merge_half(t, b, h):
                    i = 2 * b + h
                    m = merged[:, halves[h]]
                    s = sig[i % 3]
                    dve.wait_ge(S["br"], done(6 * t + i + 1))
                    dve.wait_ge(S[f"sig{i % 3}"], landed(2 * t + i // 3 + 1))
                    if b == 0:
                        dve.wait_ge(S["m_tr"], done(2 * t))
                        nc.vector.tensor_tensor(m, BR[h][:], s[:], ALU.mult).then_inc(S["mrg"], 1)
                    else:
                        nc.vector.tensor_tensor(s[:], BR[h][:], s[:], ALU.mult).then_inc(S["mul"], 1)
                        dve.wait_ge(S["mul"], done(4 * t + i - 1))
                        dve.wait_ge(S["mrg"], done(6 * t + i - 1))
                        nc.vector.tensor_tensor(m, m, s[:], ALU.add).then_inc(S["mrg"], 1)

                def turn(t, before, more):
                    now, last = t is not None, before is not None
                    first = not last
                    if first:
                        w_lo_of(0, OK)
                        lo_o(t, 0)
                        w_lo_of(OK, 2 * OK)
                        lo_o(t, 1)
                        w_lo_of(2 * OK, NBR)
                        dve.wait_ge(S["w_lo"], NBR)
                    if now:
                        merge_half(t, 0, 0)
                    if first:
                        w_lo_of(NBR, NBR + 2)
                    if last:
                        for g in range(2):
                            dve.wait_ge(S["mT_hi"], done(2 * before + g + 1))
                            nc.vector.tensor_tensor(mT_lo[:, halves[g]], MT[g][:], mT_hi[:, halves[g]].bitcast(F32), ALU.subtract)\
                              .then_inc(S["mT_lo"], 1)
                    if now:
                        merge_half(t, 0, 1)
                    if first:
                        w_lo_of(NBR + 2, NBR + 4)
                    if now:
                        lo_o(t, 2)
                    if first:
                        w_lo_of(NBR + 4, NBR + 6)
                    if last:
                        dve.wait_ge(S["x_in"], landed(before + 1))
                        for h in range(2):
                            dve.wait_ge(S["wo"], done(2 * before + h + 1))
                            nc.vector.tensor_tensor(x2[:, halves[h]], WO[h][:], x2[:, halves[h]], ALU.add).then_inc(S["x2"], 1)
                        dve.wait_ge(S["sq"], done(before + 1))
                        dve.wait_ge(S["rs"], done(before))
                        nc.vector.tensor_scalar(var, ssq, 1.0 / DM, EPS, ALU.mult, ALU.add).then_inc(S["var"], 1)
                    if now:
                        merge_half(t, 1, 0)
                    if first:
                        w_lo_of(NBR + 6, NW)
                    if now:
                        merge_half(t, 1, 1)
                    if last:
                        dve.wait_ge(S["rs"], done(before + 1))
                        dve.wait_ge(S["out_sent"], landed(before + 1))
                        dve.wait_ge(S["x2"], done(2 * before + 2))
                        nc.vector.tensor_scalar(x2[:], x2[:], rs, None, ALU.mult).then_inc(S["h2"], 1)
                        for g in range(2):
                            dve.wait_ge(S["h_tr"], done(2 * before + g + 1))
                            nc.vector.tensor_tensor(hT[:, halves[g]].rearrange("p (k w) -> p k w", k=4),
                                                    MT[g][:].rearrange("p (k w) -> p k w", k=4),
                                                    gT[:, 4 * g:4 * g + 4].rearrange("p (k a) -> p k a", a=1).to_broadcast([P, 4, P]),
                                                    ALU.mult).then_inc(S["hT"], 1)
                    if now:
                        merge_half(t, 2, 0)
                        merge_half(t, 2, 1)
                    if more:
                        lo_o(t + 1, 0)
                        lo_o(t + 1, 1)
                    if last:
                        dve.wait_ge(S["rt"], done(before + 1))
                        dve.wait_ge(S["bias"], done(before))
                        nc.vector.tensor_reduce(top, RT[:, 0:N_EXP], AX.X, ALU.max).then_inc(S["den"], 1)
                        dve.wait_ge(S["den"], done(2 * before + 1))
                        dve.wait_ge(S["exp"], done(before))
                        nc.vector.tensor_scalar(neg, top, -1.0, None, ALU.mult).then_inc(S["bias"], 1)
                        dve.wait_ge(S["exp"], done(before + 1))
                        dve.wait_ge(S["aff"], done(before))
                        nc.vector.reciprocal(rden, den).then_inc(S["den"], 1)
                        dve.wait_ge(S["den"], done(2 * before + 2))
                        nc.vector.tensor_scalar(aff[:, bass.ds(before, 1), :].rearrange("p a n -> p (a n)"), ex[:], rden, None, ALU.mult)\
                          .then_inc(S["aff"], 1)
                over_tiles(dve, turn)


def experts(nc, ident, g_ffn, w_gate, w_up, w_down, out, aff, D):
    with ExitStack() as st:
        def sb(name, shape, dt=F32):
            return st.enter_context(nc.sbuf_tensor(name, shape, dt))

        SLOTS = 3 * KT
        RAW, SPLIT = 16, 8
        LEAD = 6
        TH = KT + 5
        raw = [sb(f"raw{i}", [P, DM]) for i in range(RAW)]
        e_hi = [sb(f"e_hi{i}", [P, DM], F32R) for i in range(SPLIT)]
        e_lo = [sb(f"e_lo{i}", [P, DM], F32R) for i in range(SPLIT)]
        xg = [sb(f"xg{i}", [P, DM]) for i in range(2)]
        xT_hi = [sb(f"xT_hi{i}", [P, DM], F32R) for i in range(2)]
        xT_lo = [sb(f"xT_lo{i}", [P, DM], F32R) for i in range(2)]
        hid = sb("hid", [P, DFF])
        dT_hi = sb("dT_hi", [P, DFF], F32R)
        dT_lo = sb("dT_lo", [P, DFF], F32R)
        y = [sb(f"y{i}", [P, DM]) for i in range(2)]
        gain = sb("egain", [P, DM])
        pool_of = [sb(f"affT{i}", [N_EXP, SEQ]) for i in range(2)]
        vals = sb("vals", [N_EXP, CAP])
        idx = sb("idx", [N_EXP, CAP], U32)
        idx_f = sb("idx_f", [N_EXP, CAP])
        idx_t = sb("idx_t", [P, N_EXP])
        val_t = sb("val_t", [P, N_EXP])
        take = [sb(f"take{i}", [P, 1], U32) for i in range(2)]
        give = [sb(f"give{i}", [P, 1], U32) for i in range(2)]
        weight = [sb(f"weight{i}", [P, 1]) for i in range(2)]

        G, U, Y, XT = ([st.enter_context(nc.psum_tensor(f"{n}ps{i}", [P, 512], F32)) for i in range(2)] for n in "GUYX")
        S = {n: st.enter_context(nc.semaphore("e_" + n)) for n in
             ("w_hi w_lo used silu hid x_tr xT_hi xT_lo d_tr dT_hi dT_lo y added sent take give gained gate "
              "gain aff_tr top idx_tr idx xg0 xg1").split() + [f"raw{i}" for i in range(RAW)]}
        halves = [slice(512 * h, 512 * h + 512) for h in range(2)]

        def number(e, s):
            return KT + SLOTS * e + s

        def uses(i, j, s):
            return (SLOTS * 2 // RAW) * i + (KT + SLOTS * j + s) // RAW

        def over_experts(eng, turn, first=0):
            for e in range(2 * first):
                turn(e, e // 2, e % 2)
            with eng.Fori(first, N_EXP // 2 - 1) as i:
                for j in range(2):
                    turn(2 * i + j, i, j)
            for j in range(2):
                turn(N_EXP - 2 + j, N_EXP // 2 - 1, j)

        def last(e):
            return isinstance(e, int) and e == N_EXP - 1

        def length(e):
            return 2 * KT if last(e) else SLOTS

        def after_gate(e):
            return KT if isinstance(e, int) and e == 0 else number(e, 0) - KT

        def after_up(e):
            return number(e, KT)

        def after_down(e):
            return number(e, length(e))

        with nc.Block() as block:
            @block.sync
            def _(sp):
                for i in range(RAW):
                    sp.sem_inc(S[f"raw{i}"], 16 * CREDIT)

                def load(w, e, k, n, pos):
                    if not isinstance(n, int) or n >= RAW:
                        sp.wait_ge(S["w_lo"], done(n - RAW + 1))
                    sp.dma_start(raw[pos % RAW][:], w[bass.ds(e, 1), k * P:(k + 1) * P, :].rearrange("a p n -> (a p) n"))\
                      .then_inc(S[f"raw{pos % RAW}"], 16)

                for k in range(KT):
                    load(w_gate, 0, k, k, k)

                def turn(e, i, j):
                    for s in range(length(e)):
                        w = w_up if s < KT else w_down if s >= length(e) - KT else w_gate
                        load(w, e + 1 if w is w_gate else e, s % KT, number(e, s), KT + SLOTS * j + s)
                over_experts(sp, turn, first=1)

            @block.gpsimd
            def _(pool):
                for n in ("gained", "sent"):
                    pool.sem_inc(S[n], CREDIT)
                pool.dma_start(gain[:], bcast_rows(g_ffn, DM)).then_inc(S["gain"], 16)
                pool.wait_ge(S["gain"], 16)

                def gather(e, i, j):
                    pool.wait_ge(S["take"], done(e + 1))
                    pool.wait_ge(S["x_tr"], done(2 * e - 2))
                    pool.sem_inc(S["gate"], 1)
                    nc.gpsimd.indirect_dma_start(xg[j][:], None, D["h2"], bass.IndirectOffsetOnAxis(ap=take[j][:, 0:1], axis=0))\
                      .then_inc(S[f"xg{j}"], 16)
                    pool.wait_ge(S[f"xg{j}"], 16 * (i + 1))
                    nc.gpsimd.tensor_tensor(xg[j][:], xg[j][:], gain[:], ALU.mult).then_inc(S["gained"], 1)

                def scatter(e, i, j):
                    pool.wait_ge(S["give"], done(e + 1))
                    pool.wait_ge(S["y"], done(2 * e + 2))
                    pool.sem_inc(S["gate"], 1)
                    nc.gpsimd.indirect_dma_start(out, bass.IndirectOffsetOnAxis(ap=give[j][:, 0:1], axis=0), y[j][:], None,
                                                 compute_op=ALU.add).then_inc(S["added"], 16)
                    pool.wait_ge(S["added"], 16 * (e + 1))
                    pool.sem_inc(S["sent"], 1)
                gather(0, 0, 0)
                gather(1, 0, 1)
                with pool.Fori(0, N_EXP // 2 - 1) as i:
                    for j in range(2):
                        gather(2 * i + j + 2, i + 1, j)
                        scatter(2 * i + j, i, j)
                for j in range(2):
                    scatter(N_EXP - 2 + j, N_EXP // 2 - 1, j)
                pool.wait_ge(S["added"], 16 * N_EXP)

            @block.tensor
            def _(pe):
                for n in ("used", "x_tr", "d_tr"):
                    pe.sem_inc(S[n], CREDIT)
                for t in range(T):
                    mm = nc.tensor.transpose(XT[t // 4][0:N_EXP, (t % 4) * P:(t % 4 + 1) * P], aff[:, t, :], ident[:])
                mm.then_inc(S["aff_tr"], 1)
                pe.wait_ge(S["top"], 1 + 3 * CAP // 8 + 1)
                nc.tensor.transpose(XT[0][:, 0:N_EXP], idx_f[:], ident[0:N_EXP, 0:N_EXP])
                nc.tensor.transpose(XT[1][:, 0:N_EXP], vals[:], ident[0:N_EXP, 0:N_EXP]).then_inc(S["idx_tr"], 1)
                pe.wait_ge(S["idx"], 2)

                def turn_x(e, j):
                    pe.wait_ge(S["gained"], done(e + 1))
                    pe.wait_ge(S["dT_lo"], done(2 * e - 2))
                    for g in range(2):
                        for k in range(4):
                            at = slice((4 * g + k) * P, (4 * g + k + 1) * P)
                            mm = nc.tensor.transpose(XT[g][:, k * P:(k + 1) * P], xg[j][:, at], ident[:])
                        mm.then_inc(S["x_tr"], 1)

                def chunk(bank, hi, lo, k, n):
                    pe.wait_ge(S["w_lo"], done(n + 1))
                    at = slice(k * P, (k + 1) * P)
                    for i, (l, r) in enumerate(((hi, e_hi), (hi, e_lo), (lo, e_hi))):
                        for h in range(2):
                            mm = nc.tensor.matmul(bank[h][:], l[:, at], r[k][:, halves[h]],
                                                  start=(k == 0 and i == 0), stop=(k == KT - 1 and i == 2))
                    mm.then_inc(S["used"], 1)

                def gate(e, j, k, n):
                    if k == 0:
                        pe.wait_ge(S["xT_lo"], done(2 * e + 2))
                        pe.wait_ge(S["silu"], done(2 * e))
                    chunk(G, xT_hi[j], xT_lo[j], k, n)

                turn_x(0, 0)
                for k in range(KT):
                    gate(0, 0, k, k)

                def turn(e, i, j):
                    if not last(e):
                        turn_x(e + 1, 1 - j)
                    pe.wait_ge(S["hid"], done(2 * e))
                    for k in range(KT):
                        chunk(U, xT_hi[j], xT_lo[j], k, number(e, k))
                    for s in range(KT, TH):
                        if not last(e):
                            gate(e + 1, 1 - j, s - KT, number(e, s))
                    pe.wait_ge(S["hid"], done(2 * e + 2))
                    for g in range(2):
                        pe.wait_ge(S["xT_lo"], done(2 * e + 3 + g) if not last(e) else done(2 * e + 2))
                        for k in range(4):
                            at = slice((4 * g + k) * P, (4 * g + k + 1) * P)
                            mm = nc.tensor.transpose(XT[g][:, k * P:(k + 1) * P], hid[:, at], ident[:])
                        mm.then_inc(S["d_tr"], 1)
                    for s in range(TH, 2 * KT):
                        if not last(e):
                            gate(e + 1, 1 - j, s - KT, number(e, s))
                    pe.wait_ge(S["dT_lo"], done(2 * e + 2))
                    pe.wait_ge(S["y"], done(2 * e))
                    for k in range(KT):
                        chunk(Y, dT_hi, dT_lo, k, number(e, length(e) - KT + k))
                over_experts(pe, turn)

            def around(split, ops):
                def turn(e, i, j):
                    n = length(e)
                    for s in range(n):
                        if s + LEAD < n or not last(e):
                            split(i, j, s + LEAD, number(e, s + LEAD))
                        ops(e, i, j, s if not last(e) or s < KT else s + KT)
                        if last(e) and s == KT - 1:
                            ops(e, i, j, TH - 1)
                return turn

            @block.scalar
            def _(act):
                for n in ("w_hi", "silu", "xT_hi", "dT_hi", "y"):
                    act.sem_inc(S[n], CREDIT)

                def split(i, j, s, n):
                    act.wait_ge(S[f"raw{(KT + SLOTS * j + s) % RAW}"], landed(uses(i, j, s) + 1))
                    if not isinstance(n, int) or n >= SPLIT:
                        act.wait_ge(S["used"], done(n - SPLIT + 1))
                    nc.scalar.activation(e_hi[s % SPLIT][:], raw[(KT + SLOTS * j + s) % RAW][:], ACT.Copy).then_inc(S["w_hi"], 1)

                def x_hi(e, j):
                    for g in range(2):
                        act.wait_ge(S["x_tr"], done(2 * e + g + 1))
                        nc.scalar.activation(xT_hi[j][:, halves[g]], XT[g][:], ACT.Copy).then_inc(S["xT_hi"], 1)

                def silu(e):
                    for h in range(2):
                        act.wait_ge(S["used"], done(after_gate(e)))
                        act.wait_ge(S["d_tr"], done(2 * e))
                        nc.scalar.activation(hid[:, halves[h]], G[h][:], ACT.Silu).then_inc(S["silu"], 1)

                def ops(e, i, j, s):
                    if s == 0 and not last(e):
                        x_hi(e + 1, 1 - j)
                    if s == TH - 1:
                        for g in range(2):
                            act.wait_ge(S["d_tr"], done(2 * e + g + 1))
                            act.wait_ge(S["used"], done(number(e, 0)))
                            nc.scalar.activation(dT_hi[:, halves[g]], XT[g][:], ACT.Copy).then_inc(S["dT_hi"], 1)
                    if s == 2 * KT and not last(e):
                        silu(e + 1)
                    if s == SLOTS - 1:
                        for h in range(2):
                            act.wait_ge(S["used"], done(after_down(e)))
                            act.wait_ge(S["sent"], done(e - 1))
                            act.wait_ge(S["give"], done(e + 1))
                            nc.scalar.activation(y[j][:, halves[h]], Y[h][:], ACT.Copy, scale=weight[j][:]).then_inc(S["y"], 1)

                for s in range(-KT, LEAD - KT):
                    split(0, 0, s, KT + s)
                x_hi(0, 0)
                for s in range(LEAD - KT, LEAD):
                    split(0, 0, s, KT + s)
                silu(0)
                over_experts(act, around(split, ops))

            @block.vector
            def _(dve):
                for n in ("w_lo", "hid", "xT_lo", "dT_lo", "take", "give"):
                    dve.sem_inc(S[n], CREDIT)

                def split(i, j, s, n):
                    dve.wait_ge(S["w_hi"], done(n + 1))
                    at = (KT + SLOTS * j + s) % RAW
                    nc.vector.tensor_tensor(e_lo[s % SPLIT][:], raw[at][:], e_hi[s % SPLIT][:].bitcast(F32), ALU.subtract)\
                      .then_inc(S["w_lo"], 1)

                dve.wait_ge(S["aff_tr"], 1)
                for h in range(2):
                    op = nc.vector.tensor_copy(pool_of[0][:, halves[h]], XT[h][0:N_EXP, :])
                op.then_inc(S["top"], 1)
                n = 1
                for r in range(CAP // 8):
                    at = slice(8 * r, 8 * r + 8)
                    left, rest = pool_of[r % 2], pool_of[1 - r % 2]
                    dve.wait_ge(S["top"], n - 1 if r else n)
                    nc.vector.max(vals[:, at], left[:]).then_inc(S["top"], 1)
                    dve.wait_ge(S["top"], n + 1)
                    nc.vector.match_replace(rest[:], vals[:, at], left[:], -1.0).then_inc(S["top"], 1)
                    nc.vector.max_index(idx[:, at], vals[:, at], left[:]).then_inc(S["top"], 1)
                    n += 3
                dve.wait_ge(S["top"], n)
                nc.vector.tensor_copy(idx_f[:], idx[:]).then_inc(S["top"], 1)
                dve.wait_ge(S["idx_tr"], 1)
                nc.vector.tensor_copy(idx_t[:], XT[0][:, 0:N_EXP]).then_inc(S["idx"], 1)
                nc.vector.tensor_copy(val_t[:], XT[1][:, 0:N_EXP]).then_inc(S["idx"], 1)
                dve.wait_ge(S["idx"], 2)
                nc.vector.tensor_copy(take[0][:], idx_t[:, 0:1]).then_inc(S["take"], 1)
                nc.vector.tensor_copy(take[1][:], idx_t[:, 1:2]).then_inc(S["take"], 1)

                def x_lo(e, j):
                    for g in range(2):
                        dve.wait_ge(S["xT_hi"], done(2 * e + g + 1))
                        nc.vector.tensor_tensor(xT_lo[j][:, halves[g]], XT[g][:], xT_hi[j][:, halves[g]].bitcast(F32), ALU.subtract)\
                          .then_inc(S["xT_lo"], 1)

                def ops(e, i, j, s):
                    if s == 0 and not last(e):
                        x_lo(e + 1, 1 - j)
                    if s == 3 and not (isinstance(e, int) and e >= N_EXP - 2):
                        dve.wait_ge(S[f"xg{j}"], 16 * (i + 1))
                        nc.vector.tensor_scalar(take[j][:], idx_t[:, bass.ds(e + 2, 1)], 1.0, None, ALU.mult).then_inc(S["take"], 1)
                    if s == 5:
                        dve.wait_ge(S["sent"], done(e - 1))
                        dve.wait_ge(S["y"], done(2 * e - 2))
                        nc.vector.tensor_scalar(weight[j][:], val_t[:, bass.ds(e, 1)], 1.0, None, ALU.mult)
                        nc.vector.tensor_scalar(give[j][:], idx_t[:, bass.ds(e, 1)], 1.0, None, ALU.mult).then_inc(S["give"], 1)
                    if s == KT - 1:
                        for h in range(2):
                            dve.wait_ge(S["used"], done(after_up(e)))
                            dve.wait_ge(S["silu"], done(2 * e + 2))
                            nc.vector.tensor_tensor(hid[:, halves[h]], U[h][:], hid[:, halves[h]], ALU.mult).then_inc(S["hid"], 1)
                    if s == TH - 1:
                        for g in range(2):
                            dve.wait_ge(S["dT_hi"], done(2 * e + g + 1))
                            nc.vector.tensor_tensor(dT_lo[:, halves[g]], XT[g][:], dT_hi[:, halves[g]].bitcast(F32), ALU.subtract)\
                              .then_inc(S["dT_lo"], 1)

                for s in range(-KT, LEAD - KT):
                    split(0, 0, s, KT + s)
                x_lo(0, 0)
                for s in range(LEAD - KT, LEAD):
                    split(0, 0, s, KT + s)
                over_experts(dve, around(split, ops))


def build(nc, A, out, D):
    with nc.sbuf_tensor("ident", [P, P], F32) as ident, nc.sbuf_tensor("aff", [P, T, N_EXP], F32) as aff:
        project(nc, ident, A["x"], A["positions"], A["norm_mix_g"], A["w_in"], A["diff_qk_g"], A["mla_cq_g"], A["w_uq"],
                A["mla_ckv_g"], A["w_ukv"], A["mla_qk_g"], A["swa_qk_g"], A["inv_freq"], D)
        attention(nc, ident, A["positions"], A["diff_lambda"], A["diff_out_g"], A["swa_sink"], D)
        merge(nc, ident, A["x"], [A["w_branch_a"], A["w_branch_b"], A["w_branch_c"]], A["w_o"], A["norm_ffn_g"], A["w_router"],
              out, aff, D)
        experts(nc, ident, A["norm_ffn_g"], A["w_exp_gate"], A["w_exp_up"], A["w_exp_down"], out, aff, D)


def kernel(**inputs):
    import numpy as np
    import concourse.bacc as bacc
    from concourse.bass_utils import run_bass_kernel_spmd

    nc = bacc.Bacc("TRN2", target_bir_lowering=False, num_devices=1)
    given = {name: np.ascontiguousarray(a)[0] for name, a in inputs.items()}
    given["inv_freq"] = (1.0 / (ROPE_THETA ** (np.arange(0, B_ROPE, 2, dtype=np.float32) / np.float32(B_ROPE)))).astype(np.float32)
    A = {name: nc.dram_tensor("in_" + name, a.shape, mybir.dt.from_np(a.dtype), kind="ExternalInput").ap() for name, a in given.items()}
    shapes = dict(mix=(SEQ, N_MIX), sig=(SEQ, 3 * DM), qa=(T, P, 2048), ka=(P, 2 * A_HEADS, SEQ), qc=(T, P, 2048),
                  kc=(P, C_KV, SEQ), qb=(T, B_QK, 2048), kb=(B_QK, 2 * B_HEADS, SEQ), vb=(SEQ, OUT_W), o=(SEQ, 3 * OUT_W),
                  h2=(SEQ, DM))
    D = {name: nc.dram_tensor("s_" + name, shape, F32, kind="Internal").ap() for name, shape in shapes.items()}
    out = nc.dram_tensor("layer_out", (SEQ, DM), F32, kind="ExternalOutput").ap()
    build(nc, A, out, D)
    result = run_bass_kernel_spmd(nc, [{"in_" + name: a for name, a in given.items()}], core_ids=[0])
    return result.results[0]["layer_out"].reshape(1, SEQ, DM)
```
